# Optimizing a Trainium2 kernel written in Bass

```python
import jax, jax.numpy as jnp
from jax import lax
import numpy as np

D_MODEL = 1024
BATCH = 1
SEQ = 512
DEPTH = 2

CHUNK = 64
N_MIXERS = 2
N_LAYERS_A = (DEPTH + 1) // 2
N_LAYERS_B = DEPTH // 2
EPS = 1e-6

DN_HEADS = 8
DN_DK = 128
DN_DV = 128
DN_CONV = 4
DN_QK = DN_HEADS * DN_DK
DN_V = DN_HEADS * DN_DV
DN_CONV_DIM = 2 * DN_QK + DN_V
DN_IN = DN_CONV_DIM + DN_V + 2 * DN_HEADS

SW_HEADS = 16
SW_KV_HEADS = 4
SW_HEAD_DIM = 64
SW_GROUPS = SW_HEADS // SW_KV_HEADS
SW_WINDOW = 128
SW_WINDOW_CHUNKS = SW_WINDOW // CHUNK
SW_IN = (SW_HEADS + 2 * SW_KV_HEADS) * SW_HEAD_DIM
ROPE_THETA = 10000.0

D_FF = 4 * D_MODEL
PLE_DIM = 256

kernel_name = "hybrid_deltanet_swa_sink_encoder"

def rmsnorm(x, gain):
    x32 = x.astype(jnp.float32)
    y = x32 * lax.rsqrt(jnp.mean(x32 * x32, axis=-1, keepdims=True) + EPS)
    return (y * gain.astype(jnp.float32)).astype(x.dtype)

def l2norm(x):
    return x * lax.rsqrt(jnp.sum(x * x, axis=-1, keepdims=True) + EPS)

def causal_depthwise_conv(x, w):
    k_w, c = w.shape
    return lax.conv_general_dilated(
        x, w[:, None, :], window_strides=(1,), padding=[(k_w - 1, 0)],
        dimension_numbers=("NWC", "WIO", "NWC"), feature_group_count=c)

def rope_tables(positions):
    inv_freq = ROPE_THETA ** (-jnp.arange(0, SW_HEAD_DIM, 2, dtype=jnp.float32) / SW_HEAD_DIM)
    ang = positions.astype(jnp.float32)[..., None] * inv_freq
    return jnp.cos(ang), jnp.sin(ang)

def apply_rope(x, cos, sin):
    x32 = x.astype(jnp.float32)
    half = x.shape[-1] // 2
    x1, x2 = x32[..., :half], x32[..., half:]
    c, s = cos[:, :, None, :], sin[:, :, None, :]
    return jnp.concatenate([x1 * c - x2 * s, x2 * c + x1 * s], axis=-1).astype(x.dtype)

def gated_deltanet(h, w_in, conv_w, a_log, dt_bias, norm_w, w_out):
    b, s, _ = h.shape
    n = s // CHUNK
    proj = h @ w_in
    qkv = jax.nn.silu(causal_depthwise_conv(proj[..., :DN_CONV_DIM], conv_w))
    z = proj[..., DN_CONV_DIM:DN_CONV_DIM + DN_V]
    b_logit = proj[..., DN_CONV_DIM + DN_V:DN_CONV_DIM + DN_V + DN_HEADS]
    a_logit = proj[..., DN_CONV_DIM + DN_V + DN_HEADS:]
    qkv = qkv.astype(jnp.float32)
    q = l2norm(qkv[..., :DN_QK].reshape(b, s, DN_HEADS, DN_DK)) * (DN_DK ** -0.5)
    k = l2norm(qkv[..., DN_QK:2 * DN_QK].reshape(b, s, DN_HEADS, DN_DK))
    v = qkv[..., 2 * DN_QK:].reshape(b, s, DN_HEADS, DN_DV)
    beta = jax.nn.sigmoid(b_logit.astype(jnp.float32))
    g = -jnp.exp(a_log.astype(jnp.float32)) * jax.nn.softplus(
        a_logit.astype(jnp.float32) + dt_bias.astype(jnp.float32))

    def to_chunks(t):
        return t.reshape(b, n, CHUNK, DN_HEADS, -1).transpose(0, 3, 1, 2, 4)

    q, k, v = to_chunks(q), to_chunks(k), to_chunks(v)
    beta = beta.reshape(b, n, CHUNK, DN_HEADS).transpose(0, 3, 1, 2)
    g = jnp.cumsum(g.reshape(b, n, CHUNK, DN_HEADS).transpose(0, 3, 1, 2), axis=-1)

    tri = jnp.tril(jnp.ones((CHUNK, CHUNK), dtype=bool))
    strict = jnp.tril(jnp.ones((CHUNK, CHUNK), dtype=bool), -1)
    decay = jnp.exp(jnp.where(tri, g[..., :, None] - g[..., None, :], -jnp.inf))
    k_beta = k * beta[..., None]
    lower = jnp.where(strict, jnp.einsum("bhncd,bhnkd->bhnck", k_beta, k) * decay, 0.0)
    a_mat = lower + jnp.eye(CHUNK, dtype=jnp.float32)
    rhs = jnp.concatenate([v * beta[..., None], k_beta * jnp.exp(g)[..., None]], axis=-1)
    sol = lax.linalg.triangular_solve(a_mat, rhs, left_side=True, lower=True, unit_diagonal=True)
    u, w = sol[..., :DN_DV], sol[..., DN_DV:]
    attn_intra = jnp.einsum("bhncd,bhnkd->bhnck", q, k) * decay
    q_dec = q * jnp.exp(g)[..., None]
    g_last = g[..., -1]
    k_dec = k * jnp.exp(g_last[..., None] - g)[..., None]

    def step(state, xs):
        q_n, k_n, u_n, w_n, a_n, gl_n = xs
        v_new = u_n - jnp.einsum("bhcd,bhde->bhce", w_n, state)
        o = jnp.einsum("bhcd,bhde->bhce", q_n, state) + jnp.einsum("bhck,bhke->bhce", a_n, v_new)
        state = state * jnp.exp(gl_n)[..., None, None] + jnp.einsum("bhcd,bhce->bhde", k_n, v_new)
        return state, o

    xs = tuple(jnp.moveaxis(t, 2, 0) for t in (q_dec, k_dec, u, w, attn_intra, g_last))
    state0 = jnp.zeros((b, DN_HEADS, DN_DK, DN_DV), jnp.float32)
    _, o = lax.scan(step, state0, xs)
    o = o.transpose(1, 0, 3, 2, 4).reshape(b, s, DN_HEADS, DN_DV)
    o = rmsnorm(o, norm_w) * jax.nn.silu(z.reshape(b, s, DN_HEADS, DN_DV).astype(jnp.float32))
    return o.reshape(b, s, DN_V).astype(h.dtype) @ w_out

def band_chunks(t, n_back):
    parts = []
    for sft in range(n_back, 0, -1):
        pad = [(0, 0), (sft, 0)] + [(0, 0)] * (t.ndim - 2)
        parts.append(jnp.pad(t, pad)[:, :t.shape[1]])
    parts.append(t)
    return jnp.concatenate(parts, axis=2)

def swa_sinks(h, cos, sin, w_in, b_in, sinks, w_out, b_out):
    b, s, _ = h.shape
    n = s // CHUNK
    qd, kd = SW_HEADS * SW_HEAD_DIM, SW_KV_HEADS * SW_HEAD_DIM
    proj = h @ w_in + b_in
    q = apply_rope(proj[..., :qd].reshape(b, s, SW_HEADS, SW_HEAD_DIM), cos, sin)
    k = apply_rope(proj[..., qd:qd + kd].reshape(b, s, SW_KV_HEADS, SW_HEAD_DIM), cos, sin)
    v = proj[..., qd + kd:].reshape(b, s, SW_KV_HEADS, SW_HEAD_DIM)
    q = q.reshape(b, n, CHUNK, SW_KV_HEADS, SW_GROUPS, SW_HEAD_DIM)
    kb = band_chunks(k.reshape(b, n, CHUNK, SW_KV_HEADS, SW_HEAD_DIM), SW_WINDOW_CHUNKS - 1)
    vb = band_chunks(v.reshape(b, n, CHUNK, SW_KV_HEADS, SW_HEAD_DIM), SW_WINDOW_CHUNKS - 1)
    scores = jnp.einsum("bnqhgd,bnkhd->bnhgqk", q, kb).astype(jnp.float32) * (SW_HEAD_DIM ** -0.5)
    key_chunk_back = (SW_WINDOW_CHUNKS - 1) - jnp.arange(SW_WINDOW_CHUNKS * CHUNK) // CHUNK
    valid = (jnp.arange(n)[:, None] - key_chunk_back[None, :]) >= 0
    scores = jnp.where(valid[None, :, None, None, None, :], scores, -jnp.inf)
    sink = sinks.astype(jnp.float32).reshape(SW_KV_HEADS, SW_GROUPS)[None, None, :, :, None, None]
    m = jnp.maximum(jnp.max(scores, axis=-1, keepdims=True), sink)
    pexp = jnp.exp(scores - m)
    probs = pexp / (jnp.sum(pexp, axis=-1, keepdims=True) + jnp.exp(sink - m))
    o = jnp.einsum("bnhgqk,bnkhd->bnqhgd", probs.astype(vb.dtype), vb)
    return o.reshape(b, s, qd) @ w_out + b_out

def setup_inputs(seed: int = 0) -> dict:
    key = jax.random.key(seed)
    ks = jax.random.split(key, 24)
    f32 = jnp.float32
    nrm = lambda k, shape, scale: jax.random.normal(k, shape, f32) * scale
    return {
        "x": nrm(ks[0], (BATCH, SEQ, D_MODEL), 1.0),
        "p": nrm(ks[1], (DEPTH, BATCH, SEQ, PLE_DIM), 1.0),
        "positions": jax.random.randint(ks[2], (BATCH, 1), 0, 4096, jnp.int32)
                     + jnp.arange(SEQ, dtype=jnp.int32)[None, :],
        "norm_mix": 1.0 + nrm(ks[3], (DEPTH, D_MODEL), 0.02),
        "norm_mlp": 1.0 + nrm(ks[4], (DEPTH, D_MODEL), 0.02),
        "norm_ple": 1.0 + nrm(ks[5], (DEPTH, D_MODEL), 0.02),
        "norm_final": 1.0 + nrm(ks[6], (D_MODEL,), 0.02),
        "dn_w_in": nrm(ks[7], (N_LAYERS_A, D_MODEL, DN_IN), D_MODEL ** -0.5),
        "dn_conv_w": nrm(ks[8], (N_LAYERS_A, DN_CONV, DN_CONV_DIM), DN_CONV ** -0.5),
        "dn_a_log": jnp.log(jax.random.uniform(ks[9], (N_LAYERS_A, DN_HEADS), f32, 1.0, 16.0)),
        "dn_dt_bias": 1.0 + nrm(ks[10], (N_LAYERS_A, DN_HEADS), 0.1),
        "dn_norm_w": 1.0 + nrm(ks[11], (N_LAYERS_A, DN_DV), 0.02),
        "dn_w_out": nrm(ks[12], (N_LAYERS_A, DN_V, D_MODEL), DN_V ** -0.5),
        "sw_w_in": nrm(ks[13], (N_LAYERS_B, D_MODEL, SW_IN), D_MODEL ** -0.5),
        "sw_b_in": nrm(ks[14], (N_LAYERS_B, SW_IN), 0.02),
        "sw_sinks": nrm(ks[15], (N_LAYERS_B, SW_HEADS), 0.5),
        "sw_w_out": nrm(ks[16], (N_LAYERS_B, SW_HEADS * SW_HEAD_DIM, D_MODEL), (SW_HEADS * SW_HEAD_DIM) ** -0.5),
        "sw_b_out": nrm(ks[17], (N_LAYERS_B, D_MODEL), 0.02),
        "mlp_w_up": nrm(ks[18], (DEPTH, D_MODEL, D_FF), D_MODEL ** -0.5),
        "mlp_w_down": nrm(ks[19], (DEPTH, D_FF, D_MODEL), D_FF ** -0.5),
        "ple_w_proj": nrm(ks[20], (DEPTH, PLE_DIM, D_MODEL), PLE_DIM ** -0.5),
        "ple_w_gate": nrm(ks[21], (DEPTH, D_MODEL, D_MODEL), D_MODEL ** -0.5),
    }

def reference(x, p, positions, norm_mix, norm_mlp, norm_ple, norm_final,
              dn_w_in, dn_conv_w, dn_a_log, dn_dt_bias, dn_norm_w, dn_w_out,
              sw_w_in, sw_b_in, sw_sinks, sw_w_out, sw_b_out,
              mlp_w_up, mlp_w_down, ple_w_proj, ple_w_gate):
    cos, sin = rope_tables(positions)
    h = x
    for i in range(DEPTH):
        j = i // N_MIXERS
        hn = rmsnorm(h, norm_mix[i])
        if i % N_MIXERS == 0:
            mix = gated_deltanet(hn, dn_w_in[j], dn_conv_w[j], dn_a_log[j], dn_dt_bias[j],
                                 dn_norm_w[j], dn_w_out[j])
        else:
            mix = swa_sinks(hn, cos, sin, sw_w_in[j], sw_b_in[j], sw_sinks[j],
                            sw_w_out[j], sw_b_out[j])
        h = h + mix
        hn = rmsnorm(h, norm_mlp[i])
        h = h + jnp.square(jax.nn.relu(hn @ mlp_w_up[i])) @ mlp_w_down[i]
        gate = jax.nn.sigmoid(rmsnorm(h, norm_ple[i]) @ ple_w_gate[i])
        h = h + (p[i] @ ple_w_proj[i]) * gate
    return rmsnorm(h, norm_final)


_drawn_inputs = setup_inputs


def setup_inputs(seed=0):
    import zlib

    import numpy as np

    out = dict(_drawn_inputs(seed))
    spreads = {}
    factors = {'norm_mix': 3.163,
     'norm_mlp': 2.704,
     'norm_ple': 64.0,
     'norm_final': 7.349,
     'dn_dt_bias': 43.844,
     'dn_norm_w': 5.718,
     'sw_b_in': 13.629,
     'sw_sinks': 64.0,
     'sw_b_out': 39.712,
     'dn_a_log': 5.94}
    for name, (base, spread) in spreads.items():
        noise = np.random.default_rng([zlib.crc32(name.encode()), seed]).standard_normal(out[name].shape)
        drawn = base * np.exp(spread * noise) if base else spread * noise
        out[name] = __import__('jax').numpy.asarray(drawn.astype(out[name].dtype))
    for name, factor in factors.items():
        out[name] = (out[name] * factor).astype(out[name].dtype)
    return out
```

```python
import math
from contextlib import ExitStack

import numpy as np
import concourse.bass as bass
from concourse import mybir

F32 = mybir.dt.float32
F32R = mybir.dt.float32r
I32 = mybir.dt.int32
ALU = mybir.AluOpType
ACT = mybir.ActivationFunctionType
AX = mybir.AxisListType.X

P = 128
D = 1024
S = 512
KT = D // P
NT = S // P
CH = 64
EPS = 1e-6
HEADS_A = 8
CONV = 4
GATE_COLS = 2 * HEADS_A
HD = 64
KVH = 4
GRP = 4
HALF = HD // 2
FF = 4 * D
GROUPS = 4
PLE = 256
PW = 2 * D
THETA = 10000.0
PANEL_INC = 128
SCALE = HD ** -0.5
TWO_PI = (6.28125, 0.0019350051879882812, 3.019916050561733e-07)


def hybrid_trunk(nc, x, p, positions, norm_mix, norm_mlp, norm_ple, norm_final,
                 dn_w_in, dn_conv_w, dn_a_log, dn_dt_bias, dn_norm_w, dn_w_out,
                 sw_w_in, sw_b_in, sw_sinks, sw_w_out, sw_b_out,
                 mlp_w_up, mlp_w_down, ple_w_proj, ple_w_gate, out, upto=99, dbg=None):
    ctx = ExitStack()
    with ctx:
        def sb(name, shape, dt=F32):
            return ctx.enter_context(nc.sbuf_tensor(name, shape, dt))

        def sem(name):
            return ctx.enter_context(nc.semaphore(name))

        hT = sb("hT", [P, KT, S])
        aH, aL = sb("aH", [P, KT, S], F32R), sb("aL", [P, KT, S], F32R)
        bH, bL = sb("bH", [P, KT, S], F32R), sb("bL", [P, KT, S], F32R)
        wRaw = sb("wRaw", [P, 2, PW])
        wH, wL = sb("wH", [P, 2, PW], F32R), sb("wL", [P, 2, PW], F32R)
        psum = ctx.enter_context(nc.psum_tensor("psum", [P, 8, S], F32))
        bank = [psum[:, i, :] for i in range(8)]

        ropeC, ropeS = sb("ropeC", [P, S]), sb("ropeS", [P, S])
        ident = sb("ident", [P, P])
        ones = sb("ones", [P, P])
        rBC = sb("rBC", [P, S])
        rCol = sb("rCol", [P, NT])
        sqT = sb("sqT", [P, 2, S])
        sqSum = sb("sqSum", [P, S])
        minusHalf = sb("minusHalf", [P, 8])

        def rng(i):
            return slice(i * P, (i + 1) * P)

        panel_in = [sem("panel_in0"), sem("panel_in1")]
        panel_hi = sem("panel_hi")
        panel_lo = sem("panel_lo")
        tile_done = sem("tile_done")
        const_in = sem("const_in")
        const_ok = sem("const_ok")

        dn_in_v = dn_w_in[0].rearrange("(k p) n -> p k n", p=P)

        def square_panel(w, rows0, cols0):
            v = w[rows0:rows0 + D, cols0:cols0 + 256].rearrange("(k p) n -> p k n", p=P)
            return v

        def load_square(sp, n, view):
            s = n % 2
            dst = wRaw[:, s, :].rearrange("p (k n) -> p k n", k=KT)
            for q in range(2):
                sp.dma_start(dst[:, 4 * q:4 * q + 4, :], view[:, 4 * q:4 * q + 4, :]).then_inc(panel_in[s], PANEL_INC // 2)

        N_DN = 0
        N_DNOUT = N_DN + 2 * HEADS_A
        N_MLP0 = N_DNOUT + 4
        N_PLE0 = N_MLP0 + 8 * GROUPS
        N_SW = N_PLE0 + 5
        N_SWOUT = N_SW + 6
        N_MLP1 = N_SWOUT + 4
        N_PLE1 = N_MLP1 + 8 * GROUPS
        N_END = N_PLE1 + 5
        LAST = N_SW if upto <= 4 else N_END

        def tiles_before(n):
            return 2 * n + 6 * (n > N_PLE0) + 6 * (n > N_PLE1)

        def panel_parts(w, slot, n, split):
            v = w[:, slot, :]
            if not (isinstance(n, int) and N_SW <= n <= N_SW + GRP):
                return [v]
            order = "p (k f g c) -> p k f g c" if split else "p (k g f c) -> p k f g c"
            v = v.rearrange(order, k=KT, f=2, g=KVH)
            return [v[:, :, f] for f in range(2)]

        def prep_hi(act, n, slot, extra=0):
            if isinstance(n, int) and n >= LAST:
                return
            act.wait_ge(panel_in[slot], (n - slot) * (PANEL_INC // 2) + PANEL_INC)
            if not (isinstance(n, int) and n < 2):
                act.wait_ge(tile_done, tiles_before(n - 1) if isinstance(n, int) else 2 * n - 2 + extra)
            last = [nc.scalar.copy(o, r) for o, r in zip(panel_parts(wH, slot, n, True), panel_parts(wRaw, slot, n, False))][-1]
            last.then_inc(panel_hi, 1)

        def prep_lo(dve, n, slot):
            if isinstance(n, int) and n >= LAST:
                return
            dve.wait_ge(panel_hi, n + 1)
            last = [nc.vector.tensor_tensor(o, r, h_.bitcast(F32), ALU.subtract)
                    for o, r, h_ in zip(*(panel_parts(w, slot, n, w is not wRaw) for w in (wL, wRaw, wH)))][-1]
            last.then_inc(panel_lo, 1)

        def product(o, wh, wl, xh, xl, first, last):
            nc.tensor.matmul(o, wh, xh, start=first, stop=False)
            nc.tensor.matmul(o, wl, xh, start=False, stop=False)
            return nc.tensor.matmul(o, wh, xl, start=False, stop=last)

        msq = sb("msq", [P, 8])
        colsA = sb("colsA", [P, P])
        sinks = sb("sinks", [P, KVH, GRP])
        vBias = sb("vBias", [P, KVH * HD])
        dn_mem = ExitStack()
        dn_mem.__enter__()

        def sbd(name, shape, dt=F32):
            return dn_mem.enter_context(nc.sbuf_tensor(name, shape, dt))
        work = sbd("work", [P, 10, S])
        xTok = [work[:, 2 * t:2 * t + 2, :].rearrange("p a b -> p (a b)") for t in range(NT)]
        x_in = sem("x_in")
        x_ss = sem("x_ss")
        x_ms = sem("x_ms")
        x_r = sem("x_r")
        x_scaled = sem("x_scaled")
        x_tr = sem("x_tr")
        x_raw = sem("x_raw")
        x_hi = sem("x_hi")
        x_lo = sem("x_lo")

        maskIncl = sbd("maskIncl", [P, P])
        maskLow = sbd("maskLow", [P, P])
        maskUp = sbd("maskUp", [P, P])
        maskPair = sbd("maskPair", [P, P])
        LEVELS = [2, 4, 8, 16, 32]
        maskLev = sbd("maskLev", [P, len(LEVELS), P])
        chunkSel = sbd("chunkSel", [P, 2, P])
        inclSw = sbd("inclSw", [P, P])

        gw = sbd("gw", [P, KT, GATE_COLS])
        gwH, gwL = sbd("gwH", [P, KT, GATE_COLS], F32R), sbd("gwL", [P, KT, GATE_COLS], F32R)
        convW = sbd("convW", [P, CONV, 3 * HEADS_A])
        aLog = sbd("aLog", [P, HEADS_A])
        dtB = sbd("dtB", [P, HEADS_A])
        rowsA, rowsB = sbd("rowsA", [P, P]), sbd("rowsB", [P, P])
        R_NORMW, R_BOUT, R_BQ, R_BK = 7 * KT, 7 * KT + 1, 8 * KT + 1, 9 * KT + 1
        normW = colsA[:, R_NORMW:R_NORMW + 1]
        gains = colsA[:, 0:7 * KT].rearrange("p (i k) -> p i k", k=KT)
        rows_zero = sem("rows_zero")
        cols_done = sem("cols_done")
        cols_ok = sem("cols_ok")

        def consts_sp(sp):
            for t in range(NT):
                sp.dma_start(xTok[t], x[0, t * P:(t + 1) * P, :]).then_inc(x_in, 16)
            sp.wait_ge(rows_zero, 1)
            for i, g in enumerate((norm_mix[0], norm_mlp[0], norm_ple[0], norm_mix[1], norm_mlp[1], norm_ple[1], norm_final)):
                sp.dma_start(rowsA[i * KT:(i + 1) * KT, :], g.rearrange("(k p) -> k p", p=P)).then_inc(const_in, 16)
            sp.dma_start(rowsA[R_NORMW:R_NORMW + 1, :], dn_norm_w[0:1, :]).then_inc(const_in, 16)
            sp.dma_start(rowsA[R_BOUT:R_BOUT + KT, :], sw_b_out[0].rearrange("(k p) -> k p", p=P)).then_inc(const_in, 16)
            for j in range(GRP):
                for f in range(2):
                    src = sw_b_in[0, 0:D].rearrange("(g j f i) -> j f g i", g=KVH, j=GRP, f=2)[j:j + 1, f]
                    sp.dma_start(rowsA[R_BQ + 2 * j + f:R_BQ + 2 * j + f + 1, :].rearrange("o (g i) -> o g i", g=KVH), src).then_inc(const_in, 16)
            for f in range(2):
                src = sw_b_in[0, D:D + KVH * HD].rearrange("(o g f i) -> o f g i", o=1, g=KVH, f=2)[:, f]
                sp.dma_start(rowsA[R_BK + f:R_BK + f + 1, :].rearrange("o (g i) -> o g i", g=KVH), src).then_inc(const_in, 16)
            sp.dma_start(rowsB[0:CONV * 3 * HEADS_A, :], dn_conv_w[0].rearrange("c (k p) -> (c k) p", p=P)).then_inc(const_in, 16)
            sp.dma_start(gw[:], dn_in_v[:, :, 4 * D:4 * D + GATE_COLS]).then_inc(const_in, 16)
            sp.dma_start(aLog[:], dn_a_log[0:1, :].to_broadcast([P, HEADS_A])).then_inc(const_in, 16)
            sp.dma_start(posI[:], positions[0].rearrange("(t p) -> p t", p=P), allow_slow_non_contiguous=True).then_inc(const_in, 16)
            sp.dma_start(sinks[:].rearrange("p g j -> p (g j)"), sw_sinks[0:1, :].to_broadcast([P, KVH * GRP])).then_inc(const_in, 16)
            sp.dma_start(vBias[:], sw_b_in[0:1, D + KVH * HD:].to_broadcast([P, KVH * HD])).then_inc(const_in, 16)
            sp.dma_start(dtB[:], dn_dt_bias[0:1, :].to_broadcast([P, HEADS_A])).then_inc(const_in, 16)
        N_CONST = 16 * (7 + 2 + 2 * GRP + 2 + 1 + 6)

        posI = sbd("posI", [P, NT], I32)
        posF = sbd("posF", [P, NT])
        freq = sbd("freq", [P, HALF])
        ang = sbd("ang", [P, 2, NT, HALF])
        turn = sbd("turn", [P, 2, NT, HALF])
        trig = sbd("trig", [P, 2, NT, P])
        freq_ok = sem("freq_ok")
        ang_ok = sem("ang_ok")
        trig_ok = sem("trig_ok")
        trig_done = sem("trig_done")
        rope_ok = sem("rope_ok")

        def rope_dve(dve):
            v = nc.vector
            dve.wait_ge(freq_ok, 1)
            dve.wait_ge(const_in, N_CONST)
            v.tensor_copy(posF[:], posI[:])
            dve.drain()
            for s_ in range(2):
                v.tensor_tensor(ang[:, s_], posF[:].unsqueeze(2).to_broadcast([P, NT, HALF]),
                                freq[:].unsqueeze(1).to_broadcast([P, NT, HALF]), ALU.mult)
            dve.drain()
            big = 1.5 * 2 ** 23
            for s_ in range(2):
                v.tensor_scalar(turn[:, s_], ang[:, s_], 1.0 / (2 * math.pi), 0.25 * (1 - s_), ALU.mult, ALU.add)
            dve.drain()
            v.tensor_scalar(turn[:], turn[:], big, None, ALU.add)
            dve.drain()
            v.tensor_scalar(turn[:], turn[:], big, None, ALU.subtract)
            dve.drain()
            for part in TWO_PI:
                v.scalar_tensor_tensor(out=ang[:], in0=turn[:], scalar=-part, in1=ang[:], op0=ALU.mult, op1=ALU.add)
                dve.drain()
            v.tensor_scalar(ang[:, 0], ang[:, 0], math.pi / 2, None, ALU.add)
            dve.drain()
            v.tensor_scalar(ang[:], ang[:], 3.1415925, -3.1415925, ALU.min, ALU.max).then_inc(ang_ok, 1)

        def rope_act(act):
            act.wait_ge(ang_ok, 1)
            for g in range(KVH):
                last = nc.scalar.activation(trig[:, :, :, g * HALF:(g + 1) * HALF], ang[:], ACT.Sin)
            last.then_inc(trig_ok, 1)
            act.wait_ge(trig_done, 1)
            nc.scalar.copy(ropeC[:], bank[6])
            nc.scalar.copy(ropeS[:], bank[7]).then_inc(rope_ok, 1)

        def rope_pe(pe):
            pe.wait_ge(trig_ok, 1)
            for s_ in range(2):
                for t in range(NT):
                    last = nc.tensor.transpose(bank[6 + s_][:, rng(t)], trig[:, s_, t, :], ident[:])
            last.then_inc(trig_done, 1)


        def consts_pool(pool):
            g = nc.gpsimd
            for i in range(HALF):
                g.memset(freq[:, i:i + 1], float(np.float32(THETA) ** (-np.float32(2 * i) / np.float32(HD))))
            g.memset(ones[:], 1.0).then_inc(freq_ok, 1)
            pool.drain()

            def keep(view, base, pattern, cm):
                g.affine_select(out=view, in_=view, compare_op=ALU.is_ge, fill=0.0, base=base,
                                pattern=pattern, channel_multiplier=cm)
                pool.drain()
            g.memset(rowsB[:], 0.0)
            g.memset(rowsA[:], 0.0)
            pool.drain()
            pool.sem_inc(rows_zero, 1)
            for m in (ident, maskIncl, maskLow, maskUp, maskPair, maskLev, chunkSel, inclSw):
                g.memset(m[:], 1.0)
            g.memset(minusHalf[:], -0.5)
            pool.drain()
            keep(ident[:], 0, [[-1, P]], 1)
            keep(ident[:], 0, [[1, P]], -1)
            for m, base, st, cm in ((maskIncl, 0, 1, -1), (maskLow, -1, -1, 1), (maskUp, -1, 1, -1)):
                v = m[:].rearrange("p (a b) -> p a b", a=2)
                keep(v, base, [[CH * st, 2], [st, CH]], cm)
                keep(v, 0, [[-CH, 2], [0, CH]], 1)
                keep(v, CH - 1, [[CH, 2], [0, CH]], -1)
            v = inclSw[:].rearrange("p (a b) -> p a b", a=2)
            keep(v, CH, [[-CH, 2], [1, CH]], -1)
            keep(v, -CH, [[CH, 2], [0, CH]], 1)
            keep(v, 2 * CH - 1, [[-CH, 2], [0, CH]], -1)
            v = maskPair[:].rearrange("p (a b) -> p a b", b=2)
            keep(v, 0, [[-2, CH], [0, 2]], 1)
            keep(v, 0, [[2, CH], [0, 2]], -1)
            keep(v, -1, [[0, CH], [1, 2]], 0)
            for i, b in enumerate(LEVELS):
                n = P // (2 * b)
                v = maskLev[:, i, :].rearrange("p (a b) -> p a b", b=2 * b)
                keep(v, -b, [[-2 * b, n], [0, 2 * b]], 1)
                keep(v, 2 * b - 1, [[2 * b, n], [0, 2 * b]], -1)
                keep(v, b - 1, [[0, n], [-1, 2 * b]], 0)
            keep(chunkSel[:, 0, :], CH - 1, [[0, P]], -1)
            g.affine_select(out=chunkSel[:, 1, :], in_=chunkSel[:, 1, :], compare_op=ALU.is_ge, fill=0.0, base=-CH,
                            pattern=[[0, P]], channel_multiplier=1).then_inc(const_ok, 1)

        ssq = sbd("ssq", [P, NT])
        xScaled = sbd("xScaled", [P, NT, D])

        def first_norm_act(act):
            act.wait_ge(x_in, 16 * NT)
            for t in range(NT):
                nc.scalar.activation(xScaled[:, t, :], xTok[t], ACT.Square, accum_out=ssq[:, t:t + 1]).then_inc(x_ss, 1)

        def first_norm_dve(dve):
            dve.wait_ge(x_ss, NT)
            nc.vector.tensor_scalar(msq[:, 0:NT], ssq[:], 1.0 / D, EPS, ALU.mult, ALU.add).then_inc(x_ms, 1)
            dve.wait_ge(x_r, 1)
            for t in range(NT):
                nc.vector.tensor_scalar(xScaled[:, t, :], xTok[t], rCol[:, t:t + 1], None, ALU.mult).then_inc(x_scaled, 1)

        def first_norm_pool(pool):
            pool.wait_ge(x_ms, 1)
            nc.gpsimd.tensor_tensor(rCol[:], msq[:, 0:NT], minusHalf[:, 0:NT], ALU.pow).then_inc(x_r, 1)

        def first_tr_pe(pe):
            pe.wait_ge(x_in, 16 * NT)
            pe.wait_ge(const_ok, 1)
            for k in range(KT):
                b = k % 2
                if k >= 2:
                    pe.wait_ge(x_raw, k - 1)
                for t in range(NT):
                    last = nc.tensor.transpose(bank[b][:, rng(t)], xTok[t][:, rng(k)], ident[:])
                last.then_inc(x_tr, 1)
            pe.wait_ge(const_in, N_CONST)
            nc.tensor.transpose(bank[4][:, 0:P], rowsA[:], ident[:])
            nc.tensor.transpose(bank[4][:, P:2 * P], rowsB[:], ident[:]).then_inc(cols_done, 1)
            pe.wait_ge(x_scaled, NT)
            for k in range(KT):
                b = 2 + k % 2
                if k >= 2:
                    pe.wait_ge(x_lo, k - 1)
                for t in range(NT):
                    last = nc.tensor.transpose(bank[b][:, rng(t)], xScaled[:, t, rng(k)], ident[:])
                last.then_inc(x_tr, 1)

        def first_tr_act(act):
            for k in range(KT):
                act.wait_ge(x_tr, k + 1)
                nc.scalar.copy(hT[:, k, :], bank[k % 2]).then_inc(x_raw, 1)
            act.wait_ge(cols_done, 1)
            nc.scalar.copy(colsA[:], bank[4][:, 0:P])
            nc.scalar.copy(convW[:].rearrange("p c k -> p (c k)"), bank[4][:, P:P + CONV * 3 * HEADS_A]).then_inc(cols_ok, 1)
            act.drain()
            for k in range(KT):
                act.wait_ge(x_tr, KT + k + 1)
                nc.scalar.activation(aH[:, k, :], bank[2 + k % 2], ACT.Copy, scale=gains[:, 0, k:k + 1]).then_inc(x_hi, 1)

        def first_tr_dve(dve):
            dve.wait_ge(cols_ok, 1)
            for k in range(KT):
                dve.wait_ge(x_hi, k + 1)
                nc.vector.scalar_tensor_tensor(out=aL[:, k, :], in0=bank[2 + k % 2], scalar=gains[:, 0, k:k + 1],
                                               in1=aH[:, k, :].bitcast(F32), op0=ALU.mult, op1=ALU.subtract).then_inc(x_lo, 1)

        G_, B_, NB_, EG_, EGS_, ED_, EL0_, EL1_ = range(8)
        gate = sbd("gate", [P, HEADS_A, 8, NT])
        hc = sbd("hc", [P, 8, NT])
        gt = sbd("gt", [P, 8, HEADS_A, NT])
        gw_hi = sem("gw_hi"); gw_lo = sem("gw_lo")
        gate_raw = sem("gate_raw")
        gate_e = sem("gate_e")
        gate_v = sem("gate_v")
        gate_cum = sem("gate_cum")
        gate_ok = sem("gate_ok")
        logits = bank[4][:, 0:NT * GATE_COLS].rearrange("p (t c) -> p t c", t=NT)
        cums = bank[5][:, 0:5 * HEADS_A * NT].rearrange("p (q h t) -> p q h t", q=5, h=HEADS_A)

        def gates_act(act):
            act.wait_ge(const_in, N_CONST)
            nc.scalar.copy(gwH[:], gw[:]).then_inc(gw_hi, 1)

        def gates_act2(act):
            act.wait_ge(gate_v, 1)
            nc.scalar.activation(gt[:, 1], gt[:, 0], ACT.Abs).then_inc(gate_e, 1)
            nc.scalar.activation(gt[:, 7, :, 0], aLog[:], ACT.Exp)
            act.drain()
            nc.scalar.activation(gt[:, 2], gt[:, 1], ACT.Exp, scale=-1.0)
            act.wait_ge(gate_v, 2)
            nc.scalar.activation(gt[:, 3], gt[:, 3], ACT.Tanh, scale=0.5).then_inc(gate_e, 1)
            act.wait_ge(gate_cum, 1)
            nc.scalar.activation(gate[:, :, EG_:EL1_ + 1, :].rearrange("p h q t -> p q h t"), cums, ACT.Exp).then_inc(gate_e, 1)

        def gates_dve(dve):
            v = nc.vector
            dve.wait_ge(gw_hi, 1)
            v.tensor_tensor(gwL[:], gw[:], gwH[:].bitcast(F32), ALU.subtract).then_inc(gw_lo, 1)
            dve.wait_ge(gate_raw, 1)
            dve.wait_ge(const_in, N_CONST)
            v.tensor_tensor(gt[:, 0], logits[:, :, HEADS_A:].rearrange("p t h -> p h t"),
                            dtB[:].unsqueeze(2).to_broadcast([P, HEADS_A, NT]), ALU.add).then_inc(gate_v, 1)
            v.tensor_copy(gt[:, 3], logits[:, :, 0:HEADS_A].rearrange("p t h -> p h t")).then_inc(gate_v, 1)
            dve.wait_ge(gate_e, 2)
            v.tensor_scalar(gt[:, 4], gt[:, 2], 2.0, None, ALU.add)
            dve.drain()
            v.reciprocal(gt[:, 4], gt[:, 4])
            dve.drain()
            v.tensor_tensor(gt[:, 5], gt[:, 4], gt[:, 2], ALU.mult)
            dve.drain()
            v.tensor_tensor(gt[:, 6], gt[:, 5], gt[:, 5], ALU.mult)
            dve.drain()
            v.tensor_scalar(gt[:, 4], gt[:, 6], 1.0 / 19, None, ALU.mult)
            for n in (17, 15, 13, 11, 9, 7, 5, 3):
                dve.drain()
                v.scalar_tensor_tensor(out=gt[:, 4], in0=gt[:, 4], scalar=1.0 / n, in1=gt[:, 6], op0=ALU.add, op1=ALU.mult)
            dve.drain()
            v.scalar_tensor_tensor(out=gt[:, 4], in0=gt[:, 4], scalar=1.0, in1=gt[:, 5], op0=ALU.add, op1=ALU.mult)
            v.tensor_scalar(gt[:, 0], gt[:, 0], 0.0, None, ALU.max)
            dve.drain()
            v.scalar_tensor_tensor(out=gt[:, 4], in0=gt[:, 4], scalar=2.0, in1=gt[:, 0], op0=ALU.mult, op1=ALU.add)
            dve.drain()
            v.scalar_tensor_tensor(out=gate[:, :, G_, :], in0=gt[:, 4], scalar=-1.0,
                                   in1=gt[:, 7, :, 0:1].to_broadcast([P, HEADS_A, NT]), op0=ALU.mult, op1=ALU.mult)
            v.tensor_scalar(gate[:, :, B_, :], gt[:, 3], 1.0, 0.5, ALU.add, ALU.mult)
            dve.drain()
            v.tensor_scalar(gate[:, :, NB_, :], gate[:, :, B_, :], -1.0, None, ALU.mult)
            v.tensor_copy(gt[:, 5], gate[:, :, G_, :]).then_inc(gate_v, 1)

        def gates_pe(pe):
            pe.wait_ge(gw_lo, 1)
            pe.wait_ge(cols_ok, 1)
            pe.wait_ge(x_lo, KT)
            for t in range(NT):
                for k in range(KT):
                    for i, (a, w) in enumerate(((aH, gwH), (aL, gwH), (aH, gwL))):
                        last = nc.tensor.matmul(logits[:, t, :], a[:, k, rng(t)], w[:, k, :],
                                                start=(k == 0 and i == 0), stop=(k == KT - 1 and i == 2))
            last.then_inc(gate_raw, 1)
            pe.wait_ge(gate_v, 3)
            g = gt[:, 5].rearrange("p h t -> p (h t)")
            for i, m in enumerate((maskIncl[:], inclSw[:], maskLow[:], chunkSel[:, 0, :], chunkSel[:, 1, :])):
                last = nc.tensor.matmul(cums[:, i].rearrange("p h t -> p (h t)"), m, g, start=True, stop=True)
            last.then_inc(gate_cum, 1)

        qF, kF, vF, zF = (work[:, i, :] for i in range(4))
        tanhT = work[:, 4, :]
        taps = sbd("taps", [P, CONV, S])
        sq2 = xScaled[:, 0, :].rearrange("p (a b) -> p a b", a=2)
        kTok, vTok = sbd("kTok", [P, NT, P]), sbd("vTok", [P, NT, P])
        kEg, kDec = trig[:, 0], trig[:, 1]
        kHatT = sbd("kHatT", [P, S])
        gA = work[:, 6, :].rearrange("p (t c) -> p t c", t=NT)
        decT = work[:, 7, :].rearrange("p (t c) -> p t c", t=NT)
        attT = work[:, 8, :].rearrange("p (t c) -> p t c", t=NT)
        lowT = work[:, 9, :].rearrange("p (t c) -> p t c", t=NT)
        betaUp = xScaled[:, 1, 0:S].rearrange("p (t c) -> p t c", t=NT)
        inv = xScaled[:, 1, S:].rearrange("p (t c) -> p t c", t=NT)
        invT = xScaled[:, 2, 0:S].rearrange("p (t c) -> p t c", t=NT)
        tMask = xScaled[:, 2, S:].rearrange("p (t c) -> p t c", t=NT)
        qw = xScaled[:, 3, :].rearrange("p (t r c) -> p t r c", t=NT, r=2)
        uB = kHatT[:].rearrange("p (t c) -> p t c", t=NT)
        vNew = sbd("vNew", [P, P])
        state = sbd("state", [P, P])
        oTok = sbd("oTok", [P, NT, P])
        oSq = tMask
        yF = sbd("yF", [P, S])
        st8 = sbd("st8", [P, 8])
        rs8 = sbd("rs8", [P, 8])
        os4 = sbd("os4", [P, 4, NT])

        oq_ok = sem("oq_ok")
        taps_ok = sem("taps_ok")
        conv_ok = sem("conv_ok")
        tanh_ok = sem("tanh_ok")
        feat_ok = sem("feat_ok")
        sq_ok = sem("sq_ok")
        hc_ok = sem("hc_ok")
        nrm_done = sem("nrm_done"); ktr_done = sem("ktr_done"); vtr_done = sem("vtr_done")
        st_ok = sem("st_ok")
        rs_ok = sem("rs_ok")
        khat_ok = sem("khat_ok")
        kscaled = sem("kscaled")
        bup_ok = sem("bup_ok")
        vtok_ok = sem("vtok_ok")
        khtr_done = sem("khtr_done")
        khT_ok = sem("khT_ok")
        gA_ok = sem("gA_ok")
        dec_done = sem("dec_done")
        dec_ok = sem("dec_ok")
        gram_done = sem("gram_done")
        att_ok = sem("att_ok")
        x1_ok = sem("x1_ok")
        xtr_done = sem("xtr_done")
        xtr_ok = sem("xtr_ok")
        t_done = sem("t_done"); t_ok = sem("t_ok")
        p_done = sem("p_done"); x_ok = sem("x_ok")
        wT_done = sem("wT_done"); u_done = sem("u_done")
        qw_ok = sem("qw_ok")
        qq_ok = sem("qq_ok")
        s_ok = sem("s_ok")
        ws_done = sem("ws_done"); vn_ok = sem("vn_ok")
        su_done = sem("su_done"); av_done = sem("av_done"); o_ok = sem("o_ok")
        osq_ok = sem("osq_ok"); os_ok = sem("os_ok"); or_ok = sem("or_ok"); on_ok = sem("on_ok")
        otr_done = sem("otr_done"); y_ok = sem("y_ok"); yh_ok = sem("yh_ok"); yl_ok = sem("yl_ok")

        def bc(col):
            return col.unsqueeze(2).to_broadcast([P, NT, P])

        def bm(mask):
            return mask.unsqueeze(1).to_broadcast([P, NT, P])

        def tiles(b):
            return bank[b].rearrange("p (t c) -> p t c", t=NT)

        def load_dn(sp, h, j):
            for i in range(2):
                dst = wRaw[:, j, i * D:(i + 1) * D].rearrange("p (k n) -> p k n", k=KT)
                sp.dma_start(dst, dn_in_v[:, :, bass.ds(h * P + (2 * j + i) * D, P)]).then_inc(panel_in[j], PANEL_INC // 2)

        def dn_sp(sp):
            for j in range(2):
                load_dn(sp, 0, j)
            with sp.Fori(1, HEADS_A) as h:
                for j in range(2):
                    sp.wait_ge(panel_lo, 2 * h + j - 1)
                    load_dn(sp, h, j)

        UNITS = 4 * KT

        def project_pe(pe, h, u0, u1, first=False):
            for u in range(u0, u1):
                b, k = u // KT, u % KT
                if u % (2 * KT) == 0:
                    pe.wait_ge(panel_lo, 2 * h + b // 2 + 1)
                if k == 0 and not first:
                    if b < 3:
                        pe.wait_ge(taps_ok, 3 * h + b - 2)
                    else:
                        pe.wait_ge(feat_ok, 4 * h)
                c = (b % 2) * D + k * P
                last = product(bank[b], wH[:, b // 2, c:c + P], wL[:, b // 2, c:c + P],
                               aH[:, k, :], aL[:, k, :], k == 0, k == KT - 1)
                if k == KT - 1:
                    last.then_inc(tile_done, 1)

        def taps_act(act, h, b, first=False):
            act.wait_ge(tile_done, 4 * h + b + 1)
            if b or not first:
                act.wait_ge(feat_ok, 4 * h + b - (b == 0))
            for c in range(CONV):
                last = nc.scalar.activation(taps[:, c, c:S], bank[b][:, 0:S - c], ACT.Copy,
                                            scale=convW[:, CONV - 1 - c, bass.ds(b * HEADS_A + h, 1)])
            last.then_inc(taps_ok, 1)

        def taps_pool(pool, h, b):
            g = nc.gpsimd
            pool.wait_ge(taps_ok, 3 * h + b + 1)
            g.tensor_tensor(taps[:, 0, 1:], taps[:, 0, 1:], taps[:, 1, 1:], ALU.add)
            g.tensor_tensor(taps[:, 2, 3:], taps[:, 2, 3:], taps[:, 3, 3:], ALU.add)
            pool.drain()
            g.tensor_tensor(taps[:, 0, 2:], taps[:, 0, 2:], taps[:, 2, 2:], ALU.add).then_inc(conv_ok, 1)

        def tanh_act(act, h, b, first=False):
            act.wait_ge(conv_ok, 3 * h + b + 1)
            if b == 0 and not first:
                act.wait_ge(feat_ok, 4 * h)
            nc.scalar.activation(tanhT, taps[:, 0, :], ACT.Tanh, scale=0.5).then_inc(tanh_ok, 1)

        def silu_dve(dve, h, b, first=False):
            dve.wait_ge(tanh_ok, 4 * h + b + 1)
            if b == 0 and not first:
                dve.wait_ge(qq_ok, h)
            nc.vector.scalar_tensor_tensor(out=(qF, kF, vF)[b], in0=tanhT, scalar=1.0, in1=taps[:, 0, :],
                                           op0=ALU.add, op1=ALU.mult).then_inc(feat_ok, 1)

        def squares_pool(pool, h):
            pool.wait_ge(feat_ok, 4 * h + 2)
            nc.gpsimd.tensor_tensor(sq2[:, 0], qF, qF, ALU.mult)
            nc.gpsimd.tensor_tensor(sq2[:, 1], kF, kF, ALU.mult).then_inc(sq_ok, 1)

        def z_act(act, h):
            act.wait_ge(tile_done, 4 * h + 4)
            act.wait_ge(feat_ok, 4 * h + 3)
            nc.scalar.activation(tanhT, bank[3], ACT.Tanh, scale=0.5).then_inc(tanh_ok, 1)

        def z_dve(dve, h):
            dve.wait_ge(tanh_ok, 4 * h + 4)
            nc.vector.scalar_tensor_tensor(out=zF, in0=tanhT, scalar=1.0, in1=bank[3], op0=ALU.add, op1=ALU.mult).then_inc(feat_ok, 1)

        def delta_pe(pe, h, nxt):
            done = [0]

            def fill(n):
                if nxt:
                    project_pe(pe, h + 1, done[0], done[0] + n)
                    done[0] += n
            pe.wait_ge(sq_ok, h + 1)
            for t in range(NT):
                for a in range(2):
                    src = sq2[:, 0, t * P + (1 - a) * CH:t * P + (1 - a) * CH + CH]
                    nc.tensor.matmul(bank[6][a * CH:(a + 1) * CH, t:t + 1], src, ones[:, 0:1], start=True, stop=True)
            for t in range(NT):
                last = nc.tensor.matmul(bank[7][:, t:t + 1], sq2[:, 1, rng(t)], ones[:, 0:1], start=True, stop=True)
            last.then_inc(nrm_done, 1)
            for t in range(NT):
                last = nc.tensor.transpose(bank[4][:, rng(t)], kF[:, rng(t)], ident[:])
            last.then_inc(ktr_done, 1)
            fill(1)
            pe.wait_ge(feat_ok, 4 * h + 4)
            for t in range(NT):
                last = nc.tensor.transpose(bank[5][:, rng(t)], vF[:, rng(t)], ident[:])
            last.then_inc(vtr_done, 1)
            fill(3)
            pe.wait_ge(khat_ok, h + 1)
            for t in range(NT):
                last = nc.tensor.transpose(bank[4][:, rng(t)], kTok[:, t, :], ident[:])
            last.then_inc(khtr_done, 1)
            pe.wait_ge(gA_ok, h + 1)
            pe.wait_ge(vtok_ok, h + 1)
            for t in range(NT):
                last = nc.tensor.matmul(bank[5][:, rng(t)], gA[:, t, :], maskIncl[:], start=True, stop=True)
            last.then_inc(dec_done, 1)
            fill(1)
            pe.wait_ge(khT_ok, h + 1)
            pe.wait_ge(st_ok, h + 1)
            for t in range(NT):
                last = nc.tensor.matmul(bank[6][:, rng(t)], kHatT[:, rng(t)], kHatT[:, rng(t)], start=True, stop=True)
            last.then_inc(gram_done, 1)
            for t in range(NT):
                last = nc.tensor.matmul(bank[7][:, rng(t)], kHatT[:, rng(t)], qF[:, rng(t)], start=True, stop=True)
            last.then_inc(gram_done, 1)
            fill(5)
            pe.wait_ge(x1_ok, h + 1)
            for t in range(NT):
                last = nc.tensor.transpose(bank[6][:, rng(t)], invT[:, t, :], ident[:])
            last.then_inc(xtr_done, 1)
            for i in range(len(LEVELS)):
                fill(1)
                pe.wait_ge(xtr_ok, 6 * h + i + 1)
                for t in range(NT):
                    last = nc.tensor.matmul(bank[4][:, rng(t)], lowT[:, t, :], inv[:, t, :], start=True, stop=True)
                last.then_inc(t_done, 1)
                fill(1)
                pe.wait_ge(t_ok, 5 * h + i + 1)
                if i == 0:
                    pe.wait_ge(dec_ok, h + 1)
                for t in range(NT):
                    last = nc.tensor.matmul(bank[5][:, rng(t)], invT[:, t, :], tMask[:, t, :], start=True, stop=True)
                last.then_inc(p_done, 1)
                if i < 3:
                    fill(1)
                pe.wait_ge(x_ok, 5 * h + i + 1)
                for t in range(NT):
                    last = nc.tensor.transpose(bank[6][:, rng(t)], inv[:, t, :], ident[:])
                last.then_inc(xtr_done, 1)
            fill(1)
            pe.wait_ge(xtr_ok, 6 * h + 6)
            pe.wait_ge(kscaled, h + 1)
            for t in range(NT):
                last = nc.tensor.matmul(bank[4][:, rng(t)], kEg[:, t, :], invT[:, t, :], start=True, stop=True)
            last.then_inc(wT_done, 1)
            for t in range(NT):
                last = nc.tensor.matmul(bank[5][:, rng(t)], invT[:, t, :], vTok[:, t, :], start=True, stop=True)
            last.then_inc(u_done, 1)
            fill(1)
            pe.wait_ge(qw_ok, h + 1)
            pe.wait_ge(qq_ok, h + 1)
            pe.wait_ge(att_ok, h + 1)
            for n in range(S // CH):
                t, a = n // 2, n % 2
                rows, orows = slice(a * CH, (a + 1) * CH), slice((1 - a) * CH, (2 - a) * CH)
                pe.wait_ge(s_ok, 9 * h + n + 1)
                if n >= 1:
                    pe.wait_ge(o_ok, 8 * h + n)
                nc.tensor.matmul(bank[6][:, 0:P], qw[:, t, a, :], state[:], start=True, stop=True).then_inc(ws_done, 1)
                if n < 4:
                    fill(1)
                pe.wait_ge(vn_ok, 8 * h + n + 1)
                nc.tensor.matmul(bank[4][:, 0:P], kDec[rows, t, :], vNew[rows, :], start=True, stop=True).then_inc(su_done, 1)
                nc.tensor.matmul(bank[7][orows, 0:P], attT[rows, t, rows], vNew[rows, :],
                                 start=True, stop=True).then_inc(av_done, 1)
            if nxt:
                fill(UNITS - done[0])
            pe.wait_ge(on_ok, h + 1)
            for t in range(NT):
                last = nc.tensor.transpose(bank[5][:, rng(t)], oTok[:, t, :], ident[:])
            last.then_inc(otr_done, 1)

        def delta_act(act, h, nxt):
            a_ = nc.scalar
            act.wait_ge(vtr_done, h + 1)
            a_.activation(vTok[:], tiles(5), ACT.Copy, scale=0.5).then_inc(vtok_ok, 1)
            act.wait_ge(khtr_done, h + 1)
            a_.copy(kHatT[:], bank[4]).then_inc(khT_ok, 1)
            act.wait_ge(dec_done, h + 1)
            a_.activation(decT, tiles(5), ACT.Exp).then_inc(dec_ok, 1)
            prep_hi(act, 2 * h + 3, 1)
            act.wait_ge(xtr_done, 6 * h + 1)
            a_.copy(inv, tiles(6)).then_inc(xtr_ok, 1)
            for i in range(len(LEVELS)):
                if nxt and i == 0:
                    taps_act(act, h + 1, 0)
                if nxt and i == 4:
                    tanh_act(act, h + 1, 0)
                act.wait_ge(xtr_done, 6 * h + i + 2)
                a_.copy(invT, tiles(6)).then_inc(xtr_ok, 1)
            act.wait_ge(wT_done, h + 1)
            a_.copy(qw[:, :, 0, 0:CH], tiles(4)[:, :, 0:CH])
            a_.copy(qw[:, :, 1, CH:P], tiles(4)[:, :, CH:P]).then_inc(qw_ok, 1)
            if nxt:
                taps_act(act, h + 1, 1)
            for n in range(S // CH):
                t, a = n // 2, n % 2
                orows = slice((1 - a) * CH, (2 - a) * CH)
                act.wait_ge(vn_ok, 8 * h + n + 1)
                a_.activation(oTok[orows, t, :], bank[6][orows, 0:P], ACT.Copy, scale=hc[orows, EGS_, t:t + 1]).then_inc(oq_ok, 1)
                if nxt and n == 2:
                    tanh_act(act, h + 1, 1)
                if nxt and n == 3:
                    prep_hi(act, 2 * h + 4, 0)
                if nxt and n == 6:
                    taps_act(act, h + 1, 2)
            act.wait_ge(o_ok, 8 * h + 8)
            a_.activation(oSq, oTok[:], ACT.Square).then_inc(osq_ok, 1)
            if nxt:
                tanh_act(act, h + 1, 2)
            act.wait_ge(y_ok, h + 1)
            a_.copy(bH[:, h, :], yF[:]).then_inc(yh_ok, 1)
            if nxt:
                z_act(act, h + 1)

        def delta_dve(dve, h, nxt):
            v = nc.vector
            v.tensor_copy(hc[:], gate[:, h]).then_inc(hc_ok, 1)
            dve.drain()
            v.tensor_tensor(gA, bm(maskLow[:]), bc(hc[:, G_, :]), ALU.mult).then_inc(gA_ok, 1)
            dve.wait_ge(nrm_done, h + 1)
            v.tensor_scalar(st8[:, 4:8], bank[7][:, 0:4], 4 * EPS, None, ALU.add)
            v.tensor_scalar(st8[:, 0:4], bank[6][:, 0:4], 4 * EPS, None, ALU.add).then_inc(st_ok, 1)
            dve.wait_ge(rs_ok, 2 * h + 1)
            dve.wait_ge(ktr_done, h + 1)
            v.tensor_tensor(kTok[:], tiles(4), bc(rs8[:, 4:8]), ALU.mult).then_inc(khat_ok, 1)
            prep_lo(dve, 2 * h + 3, 1)
            dve.wait_ge(dec_ok, h + 1)
            v.tensor_tensor(decT, decT, bm(maskIncl[:]), ALU.mult)
            dve.drain()
            dve.wait_ge(gram_done, 2 * h + 2)
            dve.wait_ge(bup_ok, h + 1)
            v.tensor_tensor(lowT, tiles(6), decT, ALU.mult)
            dve.drain()
            v.tensor_tensor(lowT, lowT, betaUp, ALU.mult)
            dve.drain()
            v.tensor_tensor(invT, lowT, bm(maskPair[:]), ALU.mult)
            dve.drain()
            v.tensor_tensor(invT, bm(ident[:]), invT, ALU.subtract).then_inc(x1_ok, 1)
            v.tensor_tensor(attT, tiles(7), decT, ALU.mult).then_inc(att_ok, 1)
            for i in range(len(LEVELS)):
                dve.wait_ge(t_done, 5 * h + i + 1)
                v.tensor_tensor(tMask, tiles(4), bm(maskLev[:, i, :]), ALU.mult).then_inc(t_ok, 1)
                dve.wait_ge(p_done, 5 * h + i + 1)
                v.tensor_tensor(inv, inv, tiles(5), ALU.subtract).then_inc(x_ok, 1)
            if nxt:
                silu_dve(dve, h + 1, 0)
            v.memset(state[:], 0.0).then_inc(s_ok, 1)
            dve.wait_ge(u_done, h + 1)
            v.tensor_tensor(uB, tiles(5), bc(hc[:, B_, :]), ALU.mult)
            dve.drain()
            for n in range(S // CH):
                t, a = n // 2, n % 2
                rows, orows = slice(a * CH, (a + 1) * CH), slice((1 - a) * CH, (2 - a) * CH)
                dve.wait_ge(ws_done, 8 * h + n + 1)
                v.scalar_tensor_tensor(out=vNew[rows, :], in0=bank[6][rows, 0:P], scalar=hc[rows, NB_, t:t + 1],
                                       in1=uB[rows, t, :], op0=ALU.mult, op1=ALU.add).then_inc(vn_ok, 1)
                dve.drain()
                dve.wait_ge(su_done, 8 * h + n + 1)
                v.scalar_tensor_tensor(out=state[:], in0=state[:], scalar=hc[:, EL0_ + a, t:t + 1], in1=bank[4][:, 0:P],
                                       op0=ALU.mult, op1=ALU.add).then_inc(s_ok, 1)
                dve.wait_ge(av_done, 8 * h + n + 1)
                dve.wait_ge(oq_ok, 8 * h + n + 1)
                v.tensor_tensor(oTok[orows, t, :], oTok[orows, t, :], bank[7][orows, 0:P], ALU.add).then_inc(o_ok, 1)
                if nxt and n == 4:
                    silu_dve(dve, h + 1, 1)
                if nxt and n == 5:
                    prep_lo(dve, 2 * h + 4, 0)
            v.tensor_tensor(os4[:, 1, :], rs8[:, 0:4], rs8[:, 0:4], ALU.mult)
            dve.wait_ge(osq_ok, h + 1)
            v.tensor_reduce(os4[:, 0, :], oSq, AX, ALU.add)
            dve.drain()
            v.tensor_tensor(os4[:, 0, :], os4[:, 0, :], os4[:, 1, :], ALU.mult)
            dve.drain()
            v.tensor_scalar(os4[:, 0, :], os4[:, 0, :], 1.0 / (P * P), EPS, ALU.mult, ALU.add).then_inc(os_ok, 1)
            if nxt:
                silu_dve(dve, h + 1, 2)
            dve.wait_ge(or_ok, h + 1)
            v.scalar_tensor_tensor(out=os4[:, 3, :], in0=os4[:, 2, :], scalar=0.5 * P ** -0.5, in1=rs8[:, 0:4],
                                   op0=ALU.mult, op1=ALU.mult)
            dve.drain()
            v.tensor_tensor(oTok[:], oTok[:], bc(os4[:, 3, :]), ALU.mult).then_inc(on_ok, 1)
            dve.wait_ge(otr_done, h + 1)
            yt, zt = yF[:].rearrange("p (t c) -> p t c", t=NT), zF.rearrange("p (t c) -> p t c", t=NT)
            for a in range(2):
                last = v.scalar_tensor_tensor(out=yt[:, :, a * CH:(a + 1) * CH], in0=tiles(5)[:, :, (1 - a) * CH:(2 - a) * CH],
                                              scalar=normW, in1=zt[:, :, a * CH:(a + 1) * CH], op0=ALU.mult, op1=ALU.mult)
            last.then_inc(y_ok, 1)
            dve.drain()
            if nxt:
                z_dve(dve, h + 1)
            dve.wait_ge(yh_ok, h + 1)
            v.tensor_tensor(bL[:, h, :], yF[:], bH[:, h, :].bitcast(F32), ALU.subtract).then_inc(yl_ok, 1)
            dve.drain()

        def delta_pool(pool, h, nxt):
            g = nc.gpsimd
            qt = qF.rearrange("p (t c) -> p t c", t=NT)
            pool.wait_ge(st_ok, h + 1)
            g.tensor_tensor(rs8[:, 4:8], st8[:, 4:8], minusHalf[:, 0:4], ALU.pow).then_inc(rs_ok, 1)
            g.tensor_tensor(betaUp, bm(maskUp[:]), bc(hc[:, B_, :]), ALU.mult).then_inc(bup_ok, 1)
            g.tensor_tensor(rs8[:, 0:4], st8[:, 0:4], minusHalf[:, 0:4], ALU.pow).then_inc(rs_ok, 1)
            g.tensor_copy(qw[:, :, 0, CH:P], qt[:, :, 0:CH])
            g.tensor_copy(qw[:, :, 1, 0:CH], qt[:, :, CH:P]).then_inc(qq_ok, 1)
            pool.wait_ge(khat_ok, h + 1)
            g.tensor_tensor(kEg, kTok[:], bc(hc[:, EG_, :]), ALU.mult)
            g.tensor_tensor(kDec, kTok[:], bc(hc[:, ED_, :]), ALU.mult).then_inc(kscaled, 1)
            if nxt:
                for b in range(3):
                    taps_pool(pool, h + 1, b)
                    if b == 1:
                        squares_pool(pool, h + 1)
            pool.wait_ge(os_ok, h + 1)
            g.tensor_tensor(os4[:, 2, :], os4[:, 0, :], minusHalf[:, 0:4], ALU.pow).then_inc(or_ok, 1)

        def dn_pe(pe):
            project_pe(pe, 0, 0, UNITS, first=True)
            with pe.Fori(0, HEADS_A - 1) as h:
                delta_pe(pe, h, True)
            delta_pe(pe, HEADS_A - 1, False)

        def dn_act(act):
            for b in range(3):
                taps_act(act, 0, b, first=True)
                tanh_act(act, 0, b, first=True)
                if b == 1:
                    prep_hi(act, 2, 0)
            z_act(act, 0)
            with act.Fori(0, HEADS_A - 1) as h:
                delta_act(act, h, True)
            delta_act(act, HEADS_A - 1, False)

        def dn_dve(dve):
            for b in range(3):
                silu_dve(dve, 0, b, first=True)
                if b == 1:
                    prep_lo(dve, 2, 0)
            z_dve(dve, 0)
            with dve.Fori(0, HEADS_A - 1) as h:
                delta_dve(dve, h, True)
            delta_dve(dve, HEADS_A - 1, False)

        def dn_pool(pool):
            for b in range(3):
                taps_pool(pool, 0, b)
                if b == 1:
                    squares_pool(pool, 0)
            with pool.Fori(0, HEADS_A - 1) as h:
                delta_pool(pool, h, True)
            delta_pool(pool, HEADS_A - 1, False)

        dn_mem.close()

        acc = sb("acc", [P, KT, S])
        pleT = sb("pleT", [P, KT, S])
        mlp_mem = ExitStack()
        mlp_mem.__enter__()

        def sbm(name, shape, dt=F32):
            return mlp_mem.enter_context(nc.sbuf_tensor(name, shape, dt))
        pTok = sbm("pTok", [P, NT, PLE])
        pH, pL = sbm("pH", [P, 2, S], F32R), sbm("pL", [P, 2, S], F32R)
        hid = sbm("hid", [P, 2, S])
        hid2 = sbm("hid2", [P, 2, S])
        rSq = sbm("rSq", [P, S])
        diag = sbm("diag", [P, NT, P])
        gA2, gB2 = sbm("gA2", [P, 2, S]), sbm("gB2", [P, 2, S])

        res_ok = sem("res_ok")
        next_hi = sem("next_hi")
        next_lo = sem("next_lo")
        sq_done = sem("sq_done")
        sq_used = sem("sq_used")
        n_sum = sem("n_sum"); n_ms = sem("n_ms"); n_r = sem("n_r")
        n_diag = sem("n_diag"); n_bc = sem("n_bc"); n_ok = sem("n_ok")
        p_in = sem("p_in"); ptr_done = sem("ptr_done"); p_hi = sem("p_hi"); p_lo = sem("p_lo")
        hid_f = sem("hid_f"); hid_hi = sem("hid_hi"); hid_lo = sem("hid_lo")
        down_read = sem("down_read")
        ple_ok = sem("ple_ok")
        gate_in = sem("gate_in")
        gate_th = sem("gate_th")

        X_A, X_B = (aH, aL), (bH, bL)
        NEXT = [X_A, X_A, X_B, X_B, X_B, None]

        def next_act(act, u, m):
            act.wait_ge(res_ok, 8 * u + m + 1)
            dst = acc[:, m, :] if NEXT[u] is None else NEXT[u][0][:, m, :]
            nc.scalar.activation(dst, hT[:, m, :], ACT.Copy, scale=gains[:, u + 1, m:m + 1]).then_inc(next_hi, 1)
            if 8 * u + m >= 2:
                act.wait_ge(sq_used, 8 * u + m - 1)
            nc.scalar.activation(sqT[:, m % 2, :], hT[:, m, :], ACT.Square).then_inc(sq_done, 1)

        def next_dve(dve, u, m):
            if NEXT[u] is None:
                return
            dve.wait_ge(next_hi, 8 * u + m + 1)
            nc.vector.scalar_tensor_tensor(out=NEXT[u][1][:, m, :], in0=hT[:, m, :], scalar=gains[:, u + 1, m:m + 1],
                                           in1=NEXT[u][0][:, m, :].bitcast(F32), op0=ALU.mult, op1=ALU.subtract).then_inc(next_lo, 1)

        def norm_pool(pool, u):
            for m in range(KT):
                pool.wait_ge(sq_done, 8 * u + m + 1)
                if m == 0:
                    if u:
                        pool.wait_ge(n_sum, u)
                    nc.gpsimd.tensor_copy(sqSum[:], sqT[:, 0, :]).then_inc(sq_used, 1)
                else:
                    pool.drain()
                    nc.gpsimd.tensor_tensor(sqSum[:], sqSum[:], sqT[:, m % 2, :], ALU.add).then_inc(sq_used, 1)
            if u == 2 and upto <= 4:
                return
            pool.wait_ge(n_ms, u + 1)
            nc.gpsimd.tensor_tensor(rCol[:], msq[:, 0:NT], minusHalf[:, 0:NT], ALU.pow).then_inc(n_r, 1)

        def norm_pe_sum(pe, u):
            pe.wait_ge(sq_used, 8 * u + 8)
            for t in range(NT):
                last = nc.tensor.matmul(bank[7][:, t:t + 1], sqSum[:, rng(t)], ones[:, 0:1], start=True, stop=True)
            last.then_inc(n_sum, 1)

        def norm_dve(dve, u):
            dve.wait_ge(n_sum, u + 1)
            nc.vector.tensor_scalar(msq[:, 0:NT], bank[7][:, 0:NT], 1.0 / D, EPS, ALU.mult, ALU.add).then_inc(n_ms, 1)
            dve.wait_ge(n_r, u + 1)
            if u == 5:
                return
            nc.vector.tensor_tensor(diag[:], ident[:].unsqueeze(1).to_broadcast([P, NT, P]),
                                    rCol[:].unsqueeze(2).to_broadcast([P, NT, P]), ALU.mult).then_inc(n_diag, 1)

        def norm_pe_bc(pe, u):
            pe.wait_ge(n_diag, u + 1)
            nc.tensor.matmul(bank[7], ones[:], diag[:].rearrange("p t c -> p (t c)"), start=True, stop=True).then_inc(n_bc, 1)

        def norm_act(act, u):
            act.wait_ge(n_bc, u + 1)
            nc.scalar.copy(rBC[:], bank[7]).then_inc(n_ok, 1)

        def panel_tile(slot, k, c):
            return slice(k * 256 + c * P, k * 256 + c * P + P)

        def out_pe(pe, n0, u, X, ready):
            for m in range(KT):
                n = n0 + m // 2
                if m % 2 == 0:
                    pe.wait_ge(panel_lo, n + 1)
                if m >= 2:
                    pe.wait_ge(res_ok, 8 * u + m - 1)
                for k in range(KT):
                    if m == 0:
                        ready(pe, k)
                    c = panel_tile(0, k, m % 2)
                    last = product(bank[4 + m % 2], wH[:, n % 2, c], wL[:, n % 2, c], X[0][:, k, :], X[1][:, k, :], k == 0, k == KT - 1)
                last.then_inc(tile_done, 1)

        def out_act(act, n0, u):
            for m in range(KT):
                if m % 2 == 0 and (m or u):
                    prep_hi(act, n0 + m // 2 + 1, (n0 + m // 2 + 1) % 2)
                next_act(act, u, m)

        def out_dve(dve, n0, u, bias=None):
            for m in range(KT):
                if m % 2 == 0 and (m or u):
                    prep_lo(dve, n0 + m // 2 + 1, (n0 + m // 2 + 1) % 2)
                dve.wait_ge(tile_done, tiles_before(n0) + m + 1)
                if bias is None:
                    nc.vector.tensor_tensor(hT[:, m, :], bank[4 + m % 2], hT[:, m, :], ALU.add).then_inc(res_ok, 1)
                else:
                    nc.vector.scalar_tensor_tensor(out=hT[:, m, :], in0=bank[4 + m % 2], scalar=bias[:, m:m + 1], in1=hT[:, m, :],
                                                   op0=ALU.add, op1=ALU.add).then_inc(res_ok, 1)
                if m:
                    next_dve(dve, u, m - 1)
            next_dve(dve, u, KT - 1)

        def up_pe(pe, i, g, n0, u, X, Y, first):
            for m in range(KT):
                n = n0 + 8 * g + m // 2
                s = (n0 + m // 2) % 2
                if m % 2 == 0:
                    pe.wait_ge(panel_lo, n + 1)
                if m >= 2:
                    pe.wait_ge(hid_f, 8 * (GROUPS * i + g) + m - 1)
                for k in range(KT):
                    if m == 0 and first:
                        pe.wait_ge(next_lo, 8 * u - 8 + k + 1)
                    c = panel_tile(s, k, m % 2)
                    last = product(bank[m % 2], wH[:, s, c], wL[:, s, c], X[0][:, k, :], X[1][:, k, :], k == 0, k == KT - 1)
                last.then_inc(tile_done, 1)

        def down_pe(pe, i, g, n0, u, Y):
            for m in range(KT):
                n = n0 + 8 * g + 4 + m // 2
                s = (n0 + 4 + m // 2) % 2
                if m % 2 == 0:
                    pe.wait_ge(panel_lo, n + 1)
                if m >= 2:
                    pe.wait_ge(down_read, 8 * (GROUPS * i + g) + m - 1)
                for k in range(KT):
                    if m == 0:
                        pe.wait_ge(hid_lo, 8 * (GROUPS * i + g) + k + 1)
                    c = panel_tile(s, k, m % 2)
                    last = product(bank[4 + m % 2], wH[:, s, c], wL[:, s, c], Y[0][:, k, :], Y[1][:, k, :], k == 0, k == KT - 1)
                last.then_inc(tile_done, 1)

        def up_act(act, i, g, n0, Y, extra):
            for m in range(KT):
                if m % 2 == 0:
                    prep_hi(act, n0 + 8 * g + m // 2 + 1, (n0 + m // 2 + 1) % 2, extra)
                act.wait_ge(tile_done, 2 * (n0 + 8 * g) + extra + m + 1)
                if m >= 2:
                    act.wait_ge(hid_lo, 8 * (GROUPS * i + g) + m - 1)
                nc.scalar.activation(hid[:, m % 2, :], bank[m % 2], ACT.Relu).then_inc(hid_f, 1)
                act.drain()
                nc.scalar.activation(Y[0][:, m, :], hid[:, m % 2, :], ACT.Square).then_inc(hid_hi, 1)

        def down_act(act, i, g, n0, u, last, extra):
            for m in range(KT):
                if m % 2 == 0:
                    prep_hi(act, n0 + 8 * g + 4 + m // 2 + 1, (n0 + m // 2 + 1) % 2, extra)
                if last:
                    next_act(act, u, m)

        def up_dve(dve, i, g, n0, Y, extra):
            for m in range(KT):
                if m % 2 == 0:
                    prep_lo(dve, n0 + 8 * g + m // 2 + 1, (n0 + m // 2 + 1) % 2)
                dve.wait_ge(hid_f, 8 * (GROUPS * i + g) + m + 1)
                nc.vector.tensor_tensor(hid2[:, m % 2, :], hid[:, m % 2, :], hid[:, m % 2, :], ALU.mult)
                dve.drain()
                dve.wait_ge(hid_hi, 8 * (GROUPS * i + g) + m + 1)
                nc.vector.tensor_tensor(Y[1][:, m, :], hid2[:, m % 2, :], Y[0][:, m, :].bitcast(F32), ALU.subtract).then_inc(hid_lo, 1)

        def down_dve(dve, i, g, n0, u, last, extra):
            for m in range(KT):
                if m % 2 == 0:
                    prep_lo(dve, n0 + 8 * g + 4 + m // 2 + 1, (n0 + m // 2 + 1) % 2)
                dve.wait_ge(tile_done, 2 * (n0 + 8 * g + 4) + extra + m + 1)
                nc.vector.tensor_tensor(acc[:, m, :], bank[4 + m % 2], acc[:, m, :], ALU.add).then_inc(down_read, 1)
                if last:
                    dve.drain()
                    nc.vector.tensor_tensor(acc[:, m, :], acc[:, m, :], rSq[:], ALU.mult)
                    dve.drain()
                    nc.vector.tensor_tensor(hT[:, m, :], acc[:, m, :], hT[:, m, :], ALU.add).then_inc(res_ok, 1)
                    if m:
                        next_dve(dve, u, m - 1)
            if last:
                next_dve(dve, u, KT - 1)

        acc_zero = sem("acc_zero")

        def mlp_pool(pool, i, u):
            nc.gpsimd.memset(acc[:], 0.0).then_inc(acc_zero, 1)

        def mlp_pe(pe, i, n0, u, X, Y):
            up_pe(pe, i, 0, n0, u, X, Y, True)
            norm_pe_sum(pe, u - 1)
            down_pe(pe, i, 0, n0, u, Y)
            norm_pe_bc(pe, u - 1)
            with pe.Fori(1, GROUPS - 1) as g:
                up_pe(pe, i, g, n0, u, X, Y, False)
                down_pe(pe, i, g, n0, u, Y)
            up_pe(pe, i, GROUPS - 1, n0, u, X, Y, False)
            ple_in_pe(pe, i)
            down_pe(pe, i, GROUPS - 1, n0, u, Y)

        def mlp_act(act, i, n0, u, X, Y):
            extra = tiles_before(n0) - 2 * n0
            up_act(act, i, 0, n0, Y, extra)
            down_act(act, i, 0, n0, u, False, extra)
            norm_act(act, u - 1)
            with act.Fori(1, GROUPS - 1) as g:
                up_act(act, i, g, n0, Y, extra)
                down_act(act, i, g, n0, u, False, extra)
            up_act(act, i, GROUPS - 1, n0, Y, extra)
            ple_in_act(act, i)
            down_act(act, i, GROUPS - 1, n0, u, True, extra)

        def mlp_dve(dve, i, n0, u, X, Y):
            extra = tiles_before(n0) - 2 * n0
            up_dve(dve, i, 0, n0, Y, extra)
            norm_dve(dve, u - 1)
            dve.wait_ge(acc_zero, i + 1)
            down_dve(dve, i, 0, n0, u, False, extra)
            with dve.Fori(1, GROUPS - 1) as g:
                up_dve(dve, i, g, n0, Y, extra)
                down_dve(dve, i, g, n0, u, False, extra)
            up_dve(dve, i, GROUPS - 1, n0, Y, extra)
            ple_in_dve(dve, i)
            dve.wait_ge(n_ok, norms_bc(u - 1))
            nc.vector.tensor_tensor(rSq[:], rBC[:], rBC[:], ALU.mult)
            dve.drain()
            down_dve(dve, i, GROUPS - 1, n0, u, True, extra)

        def norms_bc(u):
            return u + 1

        def mlp_sp(sp, i, n0):
            up, down = mlp_w_up[i], mlp_w_down[i]
            with sp.Fori(0, GROUPS) as g:
                for j in range(4):
                    n = n0 + 8 * g + j
                    sp.wait_ge(panel_lo, n - 1)
                    v = up[:, bass.ds(g * D + 256 * j, 256)].rearrange("(k p) n -> p k n", p=P)
                    for q in range(2):
                        sp.dma_start(wRaw[:, (n0 + j) % 2, :].rearrange("p (k n) -> p k n", k=KT)[:, 4 * q:4 * q + 4, :],
                                     v[:, 4 * q:4 * q + 4, :]).then_inc(panel_in[(n0 + j) % 2], PANEL_INC // 2)
                for j in range(4):
                    n = n0 + 8 * g + 4 + j
                    sp.wait_ge(panel_lo, n - 1)
                    for q in range(2):
                        v = down[bass.ds(g * D + q * S, S), 256 * j:256 * j + 256].rearrange("(k p) n -> p k n", p=P)
                        sp.dma_start(wRaw[:, (n0 + j) % 2, :].rearrange("p (k n) -> p k n", k=KT)[:, 4 * q:4 * q + 4, :],
                                     v).then_inc(panel_in[(n0 + j) % 2], PANEL_INC // 2)

        def ple_load(sp, i):
            sp.dma_start(pTok[:], p[i, 0].rearrange("(t p) c -> p t c", p=P)).then_inc(p_in, 16)

        def ple_in_pe(pe, i):
            pe.wait_ge(p_in, 16 * (i + 1))
            for c in range(2):
                for t in range(NT):
                    last = nc.tensor.transpose(bank[2 + c][:, rng(t)], pTok[:, t, rng(c)], ident[:])
                last.then_inc(ptr_done, 1)

        def ple_in_act(act, i):
            for c in range(2):
                act.wait_ge(ptr_done, 2 * i + c + 1)
                nc.scalar.copy(pH[:, c, :], bank[2 + c]).then_inc(p_hi, 1)

        def ple_in_dve(dve, i):
            for c in range(2):
                dve.wait_ge(p_hi, 2 * i + c + 1)
                nc.vector.tensor_tensor(pL[:, c, :], bank[2 + c], pH[:, c, :].bitcast(F32), ALU.subtract).then_inc(p_lo, 1)

        def ple_pe(pe, i, n0, u, X):
            pe.wait_ge(panel_lo, n0 + 1)
            pe.wait_ge(p_lo, 2 * i + 2)
            for m in range(KT):
                if m >= 2:
                    pe.wait_ge(ple_ok, 8 * i + m - 1)
                for k in range(2):
                    c = slice(k * D + m * P, k * D + m * P + P)
                    last = product(bank[m % 2], wH[:, n0 % 2, c], wL[:, n0 % 2, c], pH[:, k, :], pL[:, k, :], k == 0, k == 1)
                last.then_inc(tile_done, 1)
            norm_pe_sum(pe, u - 1)
            for m in range(KT):
                n = n0 + 1 + m // 2
                if m % 2 == 0:
                    pe.wait_ge(panel_lo, n + 1)
                if m >= 2:
                    pe.wait_ge(gate_in, 8 * i + m - 1)
                for k in range(KT):
                    if m == 0:
                        pe.wait_ge(next_lo, 8 * u - 8 + k + 1)
                    c = panel_tile(0, k, m % 2)
                    last = product(bank[2 + m % 2], wH[:, n % 2, c], wL[:, n % 2, c], X[0][:, k, :], X[1][:, k, :], k == 0, k == KT - 1)
                last.then_inc(tile_done, 1)
                if m == 0:
                    norm_pe_bc(pe, u - 1)

        def ple_act(act, i, n0, u):
            prep_hi(act, n0 + 1, (n0 + 1) % 2)
            for m in range(KT):
                act.wait_ge(tile_done, tiles_before(n0) + m + 1)
                nc.scalar.copy(pleT[:, m, :], bank[m % 2]).then_inc(ple_ok, 1)
            norm_act(act, u - 1)
            for m in range(KT):
                if m % 2 == 0:
                    prep_hi(act, n0 + 2 + m // 2, (n0 + 2 + m // 2) % 2)
                act.wait_ge(gate_in, 8 * i + m + 1)
                nc.scalar.activation(gB2[:, m % 2, :], gA2[:, m % 2, :], ACT.Tanh, scale=0.5).then_inc(gate_th, 1)
                if m:
                    next_act(act, u, m - 1)
            next_act(act, u, KT - 1)

        def ple_dve(dve, i, n0, u):
            prep_lo(dve, n0 + 1, (n0 + 1) % 2)
            norm_dve(dve, u - 1)

            def finish(m):
                dve.wait_ge(gate_th, 8 * i + m + 1)
                dve.wait_ge(ple_ok, 8 * i + m + 1)
                nc.vector.scalar_tensor_tensor(out=pleT[:, m, :], in0=gB2[:, m % 2, :], scalar=1.0, in1=pleT[:, m, :],
                                               op0=ALU.add, op1=ALU.mult)
                dve.drain()
                nc.vector.scalar_tensor_tensor(out=hT[:, m, :], in0=pleT[:, m, :], scalar=0.5, in1=hT[:, m, :],
                                               op0=ALU.mult, op1=ALU.add).then_inc(res_ok, 1)
            for m in range(KT):
                if m % 2 == 0:
                    prep_lo(dve, n0 + 2 + m // 2, (n0 + 2 + m // 2) % 2)
                dve.wait_ge(tile_done, tiles_before(n0 + 1) + m + 1)
                if m == 0:
                    dve.wait_ge(n_ok, norms_bc(u - 1))
                nc.vector.tensor_tensor(gA2[:, m % 2, :], bank[2 + m % 2], rBC[:], ALU.mult).then_inc(gate_in, 1)
                if m:
                    finish(m - 1)
                    if m > 1:
                        next_dve(dve, u, m - 2)
            finish(KT - 1)
            next_dve(dve, u, KT - 2)
            next_dve(dve, u, KT - 1)

        def ple_sp(sp, i, n0):
            v = ple_w_proj[i].rearrange("(k p) n -> p k n", p=P)
            dst = wRaw[:, n0 % 2, :].rearrange("p (k n) -> p k n", k=2)
            sp.wait_ge(panel_lo, n0 - 1)
            for q in range(2):
                sp.dma_start(dst[:, q, :], v[:, q, :]).then_inc(panel_in[n0 % 2], PANEL_INC // 2)
            for j in range(4):
                sp.wait_ge(panel_lo, n0 + j)
                load_square(sp, n0 + 1 + j, square_panel(ple_w_gate[i], 0, 256 * j))

        late = [acc, pleT]
        mlp_mem.close()
        qkHi, qkLo = aH[:, 0:2, :], aH[:, 2:4, :]
        qS = sb("qS", [P, GRP, KVH, S], F32R)
        kSH, kSL = sb("kSH", [P, KVH, S], F32R), sb("kSL", [P, KVH, S], F32R)
        vT = pleT[:, 0:2, :].rearrange("p a b -> p (a b)").rearrange("p (t c) -> p t c", t=NT)
        probs = [acc[:, 2 * i:2 * i + 2, :].rearrange("p a b -> p (a b)").rearrange("p (j k) -> p j k", j=GRP) for i in range(2)]
        probsT = acc[:, 4:6, :]
        t1, t2, rot = pleT[:, 2, :], pleT[:, 3, :], [pleT[:, 4 + i, :] for i in range(4)]
        mx = sb("mx", [P, 6, GRP])

        qk_t = sem("qk_t"); qk_m = sem("qk_m"); qk_r = sem("qk_r"); qk_hi = sem("qk_hi"); qk_lo = sem("qk_lo")
        qk_moved = [sem("qk_moved0"), sem("qk_moved1")]
        v_ok = sem("v_ok")
        sc_done = sem("sc_done")
        sc_read = sem("sc_read")
        mx_ok = sem("mx_ok"); ex_ok = sem("ex_ok"); pr_ok = sem("pr_ok")
        ptr2_done = sem("ptr2_done"); pt_ok = sem("pt_ok"); pt_ok2 = sem("pt_ok2")
        pv_done = sem("pv_done"); o_hi = sem("o_hi"); o_lo = sem("o_lo")
        pz_ok = sem("pz_ok")
        ATB = NT * KVH

        def load_rotary(sp, j):
            n = N_SW + j
            v = sw_w_in[0][:, 0:D].rearrange("(k p) (g j c) -> k p j g c", p=P, g=KVH, j=GRP)
            dst = wRaw[:, n % 2, :].rearrange("p (k g c) -> p k g c", k=KT, g=KVH)
            for k in range(KT):
                sp.dma_start(dst[:, k], v[k][:, j]).then_inc(panel_in[n % 2], PANEL_INC // KT)

        def load_mixer_out(sp, j):
            n = N_SWOUT + j
            dst = wRaw[:, n % 2, :].rearrange("p (a j n) -> p a j n", a=2, j=GRP)
            src = sw_w_out[0][:, 256 * j:256 * j + 256].rearrange("(a r j d) n -> a r d j n", a=2, r=2, j=GRP)
            for a in range(2):
                for r in range(2):
                    sp.dma_start(dst[r * HD:(r + 1) * HD, a], src[a, r]).then_inc(panel_in[n % 2], PANEL_INC // 4)

        def stack(sp, j):
            for f in range(2):
                sp.wait_ge(qk_lo, 2 * j + f + 1)
                for i, part in enumerate((qkHi, qkLo)):
                    for g in range(KVH):
                        src = part[g * HALF:(g + 1) * HALF, f, :].bitcast(F32)
                        if j < GRP:
                            r = 2 * i + f
                            sp.dma_start(qS[r * HALF:(r + 1) * HALF, j, g, :].bitcast(F32), src).then_inc(qk_moved[f], 16)
                        else:
                            for r in (f, 2 + f):
                                sp.dma_start((kSH, kSL)[i][r * HALF:(r + 1) * HALF, g, :].bitcast(F32), src).then_inc(qk_moved[f], 16)

        def att_sp(sp):
            for j in range(GRP + 6):
                sp.wait_ge(panel_lo, N_SW + j - 1)
                if j < GRP:
                    load_rotary(sp, j)
                elif j < GRP + 2:
                    load_square(sp, N_SW + j, square_panel(sw_w_in[0], 0, D + 256 * (j - GRP)))
                else:
                    load_mixer_out(sp, j - GRP - 2)
                if 2 <= j < GRP + 3:
                    stack(sp, j - 2)

        def att_pe(pe, u, X):
            n0 = N_SW
            for j in range(GRP + 1):
                n = n0 + j
                pe.wait_ge(panel_lo, n + 1)
                for f in range(2):
                    if j:
                        pe.wait_ge(qk_t, 2 * j - 1 + f)
                    for k in range(KT):
                        if j == 0 and f == 0:
                            pe.wait_ge(next_lo, 8 * u - 8 + k + 1)
                        wv = [w[:, n % 2, panel_tile(0, k, f)] for w in (wH, wL)]
                        last = product(bank[f], wv[0], wv[1], X[0][:, k, :], X[1][:, k, :], k == 0, k == KT - 1)
                    last.then_inc(tile_done, 1)
                    if j == 0 and f == 0:
                        norm_pe_sum(pe, u - 1)
                if j == 0:
                    norm_pe_bc(pe, u - 1)
            n = n0 + GRP + 1
            pe.wait_ge(panel_lo, n + 1)
            for t in range(NT):
                for k in range(KT):
                    w = [w_[:, n % 2, k * 256:(k + 1) * 256] for w_ in (wH, wL)]
                    o = bank[2 + t // 2][:, (t % 2) * 256:(t % 2) * 256 + 256]
                    nc.tensor.matmul(o, X[0][:, k, rng(t)], w[0], start=(k == 0), stop=False)
                    nc.tensor.matmul(o, X[1][:, k, rng(t)], w[0], start=False, stop=False)
                    last = nc.tensor.matmul(o, X[0][:, k, rng(t)], w[1], start=False, stop=(k == KT - 1))
                if t % 2:
                    last.then_inc(tile_done, 1)
            for f in range(2):
                pe.wait_ge(qk_moved[f], 16 * (8 * GRP + 16))
            pe.wait_ge(v_ok, NT)

            def scores(i):
                t, g = i // KVH, i % KVH
                if i >= 2:
                    pe.wait_ge(sc_read, i - 1)
                for j in range(GRP):
                    c0, k0 = (0, (t - 1) * P) if t else (P, 0)
                    o = psum[:, 2 * (i % 2) + j // 2, (j % 2) * 256 + c0:(j % 2) * 256 + 256]
                    nc.tensor.matmul(o, qS[:, j, g, rng(t)], kSH[:, g, k0:(t + 1) * P], start=True, stop=False)
                    last = nc.tensor.matmul(o, qS[:, j, g, rng(t)], kSL[:, g, k0:(t + 1) * P], start=False, stop=True)
                last.then_inc(sc_done, 1)
            scores(0)
            for i in range(ATB):
                t, g = i // KVH, i % KVH
                if i + 1 < ATB:
                    scores(i + 1)
                pe.wait_ge(pr_ok, i + 1)
                for kt in range(2):
                    if t == 0 and kt == 0:
                        continue
                    if i:
                        pe.wait_ge(pt_ok if kt == 0 else pt_ok2, i - KVH if kt == 0 else i) if (kt or i > KVH) else None
                    for j in range(GRP):
                        last = nc.tensor.transpose(bank[4 + kt][:, rng(j)], probs[i % 2][:, j, rng(kt)], ident[:])
                    last.then_inc(ptr2_done, 1)
                pe.wait_ge(pt_ok2, i + 1)
                if t:
                    pe.wait_ge(pt_ok, i - KVH + 1)
                if g % 2 == 0 and i >= 2:
                    pe.wait_ge(o_lo, i // 2) if g % 2 == 0 and i >= 2 else None
                o = bank[6][(g % 2) * HD:(g % 2 + 1) * HD]
                if t:
                    nc.tensor.matmul(o, vT[:, t - 1, g * HD:(g + 1) * HD], probsT[:, 0, :], start=True, stop=False)
                nc.tensor.matmul(o, vT[:, t, g * HD:(g + 1) * HD], probsT[:, 1, :], start=(t == 0), stop=True).then_inc(pv_done, 1)

        def att_act(act, u, O):
            n0 = N_SW
            for j in range(GRP + 1):
                prep_hi(act, n0 + j + 1, (n0 + j + 1) % 2)
                if j == 0:
                    norm_act(act, u - 1)
                for f in range(2):
                    act.wait_ge(qk_r, 2 * j + f + 1)
                    if j:
                        act.wait_ge(qk_moved[f], 16 * 8 * j)
                    nc.scalar.copy(qkHi[:, f, :], rot[2 * f]).then_inc(qk_hi, 1)
            prep_hi(act, N_SWOUT, N_SWOUT % 2)
            a_ = nc.scalar
            for i in range(ATB):
                t, g = i // KVH, i % KVH
                act.wait_ge(mx_ok, i + 1)
                if i >= 2:
                    act.wait_ge(ptr2_done, (i - 1) + max(0, i - 1 - KVH))
                elif i == 0:
                    act.wait_ge(pz_ok, 1)
                for j in range(GRP):
                    src = psum[:, 2 * (i % 2) + j // 2, (j % 2) * 256:(j % 2) * 256 + 256]
                    for a in range(2):
                        rows = slice(a * CH, (a + 1) * CH)
                        ks = slice(P if t == 0 and a == 0 else CH + a * CH, 3 * CH + a * CH)
                        last = a_.activation(probs[i % 2][rows, j, ks], src[rows, ks], ACT.Exp, bias=mx[rows, 3, j:j + 1],
                                             scale=SCALE, accum_out=mx[rows, 4, j:j + 1])
                last.then_inc(sc_read, 1)
                a_.activation(mx[:, 5, :], mx[:, 2, :], ACT.Exp).then_inc(ex_ok, 1)
                if t:
                    act.wait_ge(ptr2_done, i + 1 + i - KVH)
                    a_.copy(probsT[:, 0, :], bank[4]).then_inc(pt_ok, 1)
                if g % 2:
                    act.wait_ge(pv_done, i + 1)
                    a = g // 2
                    a_.copy(O[0][:, GRP * a:GRP * a + GRP, rng(t)], bank[6].rearrange("p (j q) -> p j q", j=GRP)).then_inc(o_hi, 1)

        def att_dve(dve, u, O):
            v = nc.vector
            n0 = N_SW
            tt, st = v.tensor_tensor, v.scalar_tensor_tensor
            for j in range(GRP + 1):
                prep_lo(dve, n0 + j + 1, (n0 + j + 1) % 2)
                if j == 0:
                    norm_dve(dve, u - 1)
                dve.drain()
                if j == 0:
                    dve.wait_ge(n_ok, norms_bc(u - 1))
                    dve.wait_ge(rope_ok, 1)
                r0 = R_BQ + 2 * j if j < GRP else R_BK
                for f, tf in enumerate((t1, t2)):
                    dve.wait_ge(tile_done, tiles_before(n0 + j) + f + 1)
                    tt(tf, bank[f], rBC[:], ALU.mult).then_inc(qk_t, 1)
                dve.drain()
                b1, b2 = colsA[:, r0:r0 + 1], colsA[:, r0 + 1:r0 + 2]
                if j:
                    dve.wait_ge(qk_lo, 2 * j)
                st(out=rot[0], in0=t1, scalar=b1, in1=ropeC[:], op0=ALU.add, op1=ALU.mult)
                st(out=rot[1], in0=t2, scalar=b2, in1=ropeS[:], op0=ALU.add, op1=ALU.mult)
                st(out=rot[2], in0=t2, scalar=b2, in1=ropeC[:], op0=ALU.add, op1=ALU.mult)
                st(out=rot[3], in0=t1, scalar=b1, in1=ropeS[:], op0=ALU.add, op1=ALU.mult).then_inc(qk_m, 1)
                dve.drain()
                tt(rot[0], rot[0], rot[1], ALU.subtract).then_inc(qk_r, 1)
                tt(rot[2], rot[2], rot[3], ALU.add).then_inc(qk_r, 1)
                for f in range(2):
                    dve.wait_ge(qk_hi, 2 * j + f + 1)
                    if j:
                        dve.wait_ge(qk_moved[f], 16 * 8 * j)
                    tt(qkLo[:, f, :], rot[2 * f], qkHi[:, f, :].bitcast(F32), ALU.subtract).then_inc(qk_lo, 1)
            prep_lo(dve, N_SWOUT, N_SWOUT % 2)
            for t in range(NT):
                dve.wait_ge(tile_done, tiles_before(n0 + GRP + 1) + t // 2 + 1)
                st(out=vT[:, t, :], in0=bank[2 + t // 2][:, (t % 2) * 256:(t % 2) * 256 + 256], scalar=rCol[:, t:t + 1],
                   in1=vBias[:], op0=ALU.mult, op1=ALU.add).then_inc(v_ok, 1)

            def maxima(i):
                t, g = i // KVH, i % KVH
                dve.wait_ge(sc_done, i + 1)
                src = psum[:, 2 * (i % 2):2 * (i % 2) + 2, :].rearrange("p b (j k) -> p (b j) k", j=2)
                for a in range(2):
                    rows = slice(a * CH, (a + 1) * CH)
                    ks = slice(P if t == 0 and a == 0 else CH + a * CH, 3 * CH + a * CH)
                    v.tensor_reduce(mx[rows, 0, :], src[rows, :, ks], AX, ALU.max)
                dve.drain()
                st(out=mx[:, 1, :], in0=mx[:, 0, :], scalar=SCALE, in1=sinks[:, g, :], op0=ALU.mult, op1=ALU.max)
                dve.drain()
                tt(mx[:, 2, :], sinks[:, g, :], mx[:, 1, :], ALU.subtract)
                v.tensor_scalar(mx[:, 3, :], mx[:, 1, :], -1.0, None, ALU.mult).then_inc(mx_ok, 1)
            for i in range(ATB):
                t, g = i // KVH, i % KVH
                maxima(i)
                dve.wait_ge(ex_ok, i + 1)
                tt(mx[:, 0, :], mx[:, 4, :], mx[:, 5, :], ALU.add)
                dve.drain()
                v.reciprocal(mx[:, 1, :], mx[:, 0, :])
                dve.drain()
                tt(probs[i % 2], probs[i % 2], mx[:, 1, :].unsqueeze(2).to_broadcast([P, GRP, 256]), ALU.mult).then_inc(pr_ok, 1)
                dve.wait_ge(ptr2_done, i + 1 + max(0, i + 1 - KVH))
                v.tensor_copy(probsT[:, 1, :], bank[5]).then_inc(pt_ok2, 1)
                if g % 2:
                    a = g // 2
                    dve.wait_ge(o_hi, i // 2 + 1)
                    tt(O[1][:, GRP * a:GRP * a + GRP, rng(t)], bank[6].rearrange("p (j q) -> p j q", j=GRP),
                       O[0][:, GRP * a:GRP * a + GRP, rng(t)].bitcast(F32), ALU.subtract).then_inc(o_lo, 1)

        def att_pool(pool):
            pool.wait_ge(next_lo, 24)
            for i in range(2):
                nc.gpsimd.memset(probs[i], 0.0)
            pool.drain()
            pool.sem_inc(pz_ok, 1)

        out_v = out[0]
        ftr_done = sem("ftr_done"); fout_ok = sem("fout_ok")

        def final_pe(pe):
            norm_pe_sum(pe, 5)
            for t in range(NT):
                for hf in range(2):
                    i = 2 * t + hf
                    if i >= 4:
                        pe.wait_ge(fout_ok, i - 3)
                    for k in range(4):
                        last = nc.tensor.transpose(bank[i % 4][:, rng(k)], acc[:, 4 * hf + k, rng(t)], ident[:])
                    last.then_inc(ftr_done, 1)

        def final_act(act):
            act.wait_ge(n_r, 6)
            for i in range(2 * NT):
                act.wait_ge(ftr_done, i + 1)
                nc.scalar.activation(pleT[:, i, :], bank[i % 4], ACT.Copy, scale=rCol[:, i // 2:i // 2 + 1]).then_inc(fout_ok, 1)

        def final_sp(sp):
            for t in range(NT):
                sp.wait_ge(fout_ok, 2 * t + 2)
                sp.dma_start(out_v[t * P:(t + 1) * P, :].rearrange("p (a b) -> p a b", a=2), pleT[:, 2 * t:2 * t + 2, :]).then_inc(out_done, 16)
            sp.wait_ge(out_done, 16 * NT)

        out_done = sem("out_done")
        fin_ok = sem("fin_ok")
        block = ctx.enter_context(nc.Block())

        @block.sync
        def _(sp):
            consts_sp(sp)
            dn_sp(sp)
            for m in range(4):
                sp.wait_ge(panel_lo, N_DNOUT + m - 1)
                load_square(sp, N_DNOUT + m, square_panel(dn_w_out[0], 0, 256 * m))
            sp.wait_ge(res_ok, 1)
            ple_load(sp, 0)
            mlp_sp(sp, 0, N_MLP0)
            ple_sp(sp, 0, N_PLE0)
            if upto > 4:
                att_sp(sp)
                ple_load(sp, 1)
                mlp_sp(sp, 1, N_MLP1)
                ple_sp(sp, 1, N_PLE1)
            if upto > 8:
                final_sp(sp)
            if dbg:
                sp.wait_ge(fin_ok, 1)
                sp.dma_start(dbg[0], hT[:]).then_inc(out_done, 16)
                sp.wait_ge(out_done, 16 + (64 if upto > 8 else 0))

        @block.gpsimd
        def _(pool):
            consts_pool(pool)
            first_norm_pool(pool)
            dn_pool(pool)
            norm_pool(pool, 0)
            mlp_pool(pool, 0, 1)
            norm_pool(pool, 1)
            norm_pool(pool, 2)
            if upto > 4:
                att_pool(pool)
                norm_pool(pool, 3)
                mlp_pool(pool, 1, 4)
                norm_pool(pool, 4)
                norm_pool(pool, 5)

        @block.scalar
        def _(act):
            first_norm_act(act)
            first_tr_act(act)
            rope_act(act)
            gates_act(act)
            gates_act2(act)
            for j in range(2):
                prep_hi(act, j, j)
            dn_act(act)
            out_act(act, N_DNOUT, 0)
            mlp_act(act, 0, N_MLP0, 1, X_A, X_B)
            ple_act(act, 0, N_PLE0, 2)
            if upto > 4:
                att_act(act, 3, X_A)
                out_act(act, N_SWOUT, 3)
                mlp_act(act, 1, N_MLP1, 4, X_B, X_A)
                ple_act(act, 1, N_PLE1, 5)
                final_act(act)

        @block.vector
        def _(dve):
            first_norm_dve(dve)
            first_tr_dve(dve)
            rope_dve(dve)
            gates_dve(dve)
            for j in range(2):
                prep_lo(dve, j, j)
            dve.wait_ge(gate_e, 3)
            dn_dve(dve)
            out_dve(dve, N_DNOUT, 0)
            mlp_dve(dve, 0, N_MLP0, 1, X_A, X_B)
            ple_dve(dve, 0, N_PLE0, 2)
            if upto > 4:
                att_dve(dve, 3, X_A)
                out_dve(dve, N_SWOUT, 3, colsA[:, R_BOUT:R_BOUT + KT])
                mlp_dve(dve, 1, N_MLP1, 4, X_B, X_A)
                ple_dve(dve, 1, N_PLE1, 5)
                norm_dve(dve, 5)
            if dbg:
                nc.vector.memset(mx[:], 0.0).then_inc(fin_ok, 1)

        @block.tensor
        def _(pe):
            first_tr_pe(pe)
            rope_pe(pe)
            gates_pe(pe)
            dn_pe(pe)
            out_pe(pe, N_DNOUT, 0, X_B, lambda e, k: e.wait_ge(yl_ok, k + 1))
            mlp_pe(pe, 0, N_MLP0, 1, X_A, X_B)
            ple_pe(pe, 0, N_PLE0, 2, X_A)
            if upto > 4:
                att_pe(pe, 3, X_B)
                out_pe(pe, N_SWOUT, 3, X_A, lambda e, k: e.wait_ge(o_lo, 2 * NT))
                mlp_pe(pe, 1, N_MLP1, 4, X_B, X_A)
                ple_pe(pe, 1, N_PLE1, 5, X_B)
                final_pe(pe)


_INS = ['x', 'p', 'positions', 'norm_mix', 'norm_mlp', 'norm_ple', 'norm_final', 'dn_w_in', 'dn_conv_w', 'dn_a_log',
        'dn_dt_bias', 'dn_norm_w', 'dn_w_out', 'sw_w_in', 'sw_b_in', 'sw_sinks', 'sw_w_out', 'sw_b_out', 'mlp_w_up',
        'mlp_w_down', 'ple_w_proj', 'ple_w_gate']


def kernel(**inputs):
    import numpy as _np
    import concourse.bacc as _bacc
    from concourse import mybir as _mybir
    from concourse.bass_utils import run_bass_kernel_spmd as _run

    nc = _bacc.Bacc("TRN2", target_bir_lowering=False, num_devices=1, dynamic_dma_scratch_size=1024)
    arrays, args = {}, []
    for name in _INS:
        a = _np.ascontiguousarray(inputs[name])
        arrays[f"in_{name}"] = a
        args.append(nc.dram_tensor(f"in_{name}", a.shape, _mybir.dt.from_np(a.dtype), kind="ExternalInput").ap())
    args.append(nc.dram_tensor("out_0", (1, S, D), F32, kind="ExternalOutput").ap())
    hybrid_trunk(nc, *args)
    r = _run(nc, [arrays], core_ids=[0])
    return r.results[0]["out_0"]
```

```python
import math
from contextlib import ExitStack

import numpy as np
import concourse.bass as bass
from concourse import mybir

F32 = mybir.dt.float32
F32R = mybir.dt.float32r
I32 = mybir.dt.int32
ALU = mybir.AluOpType
ACT = mybir.ActivationFunctionType
AX = mybir.AxisListType.X

P = 128
D = 1024
S = 512
KT = D // P
NT = S // P
CH = 64
EPS = 1e-6
HEADS_A = 8
CONV = 4
GATE_COLS = 2 * HEADS_A
HD = 64
KVH = 4
GRP = 4
HALF = HD // 2
FF = 4 * D
GROUPS = 4
PLE = 256
PW = 2 * D
THETA = 10000.0
PANEL_INC = 128
SCALE = HD ** -0.5
TWO_PI = (6.28125, 0.0019350051879882812, 3.019916050561733e-07)


def hybrid_trunk(nc, x, p, positions, norm_mix, norm_mlp, norm_ple, norm_final,
                 dn_w_in, dn_conv_w, dn_a_log, dn_dt_bias, dn_norm_w, dn_w_out,
                 sw_w_in, sw_b_in, sw_sinks, sw_w_out, sw_b_out,
                 mlp_w_up, mlp_w_down, ple_w_proj, ple_w_gate, out, upto=99, dbg=None):
    ctx = ExitStack()
    with ctx:
        def sb(name, shape, dt=F32):
            return ctx.enter_context(nc.sbuf_tensor(name, shape, dt))

        def sem(name):
            return ctx.enter_context(nc.semaphore(name))

        hT = sb("hT", [P, KT, S])
        aH, aL = sb("aH", [P, KT, S], F32R), sb("aL", [P, KT, S], F32R)
        bH, bL = sb("bH", [P, KT, S], F32R), sb("bL", [P, KT, S], F32R)
        wRaw = sb("wRaw", [P, 2, PW])
        wH, wL = sb("wH", [P, 2, PW], F32R), sb("wL", [P, 2, PW], F32R)
        psum = ctx.enter_context(nc.psum_tensor("psum", [P, 8, S], F32))
        bank = [psum[:, i, :] for i in range(8)]

        ropeC, ropeS = sb("ropeC", [P, S]), sb("ropeS", [P, S])
        ident = sb("ident", [P, P])
        ones = sb("ones", [P, P])
        rBC = sb("rBC", [P, S])
        rCol = sb("rCol", [P, NT])
        sqT = sb("sqT", [P, 2, S])
        sqSum = sb("sqSum", [P, S])
        minusHalf = sb("minusHalf", [P, 8])

        def rng(i):
            return slice(i * P, (i + 1) * P)

        panel_in = [sem("panel_in0"), sem("panel_in1")]
        panel_hi = sem("panel_hi")
        panel_lo = sem("panel_lo")
        tile_done = sem("tile_done")
        const_in = sem("const_in")
        const_ok = sem("const_ok")

        dn_in_v = dn_w_in[0].rearrange("(k p) n -> p k n", p=P)

        def square_panel(w, rows0, cols0):
            v = w[rows0:rows0 + D, cols0:cols0 + 256].rearrange("(k p) n -> p k n", p=P)
            return v

        def load_square(sp, n, view):
            s = n % 2
            dst = wRaw[:, s, :].rearrange("p (k n) -> p k n", k=KT)
            for q in range(2):
                sp.dma_start(dst[:, 4 * q:4 * q + 4, :], view[:, 4 * q:4 * q + 4, :]).then_inc(panel_in[s], PANEL_INC // 2)

        N_DN = 0
        N_DNOUT = N_DN + 2 * HEADS_A
        N_MLP0 = N_DNOUT + 4
        N_PLE0 = N_MLP0 + 8 * GROUPS
        N_SW = N_PLE0 + 5
        N_SWOUT = N_SW + 6
        N_MLP1 = N_SWOUT + 4
        N_PLE1 = N_MLP1 + 8 * GROUPS
        N_END = N_PLE1 + 5
        LAST = N_SW if upto <= 4 else N_END

        def tiles_before(n):
            return 2 * n + 6 * (n > N_PLE0) + 6 * (n > N_PLE1)

        def panel_parts(w, slot, n, split):
            v = w[:, slot, :]
            if not (isinstance(n, int) and N_SW <= n <= N_SW + GRP):
                return [v]
            order = "p (k f g c) -> p k f g c" if split else "p (k g f c) -> p k f g c"
            v = v.rearrange(order, k=KT, f=2, g=KVH)
            return [v[:, :, f] for f in range(2)]

        def prep_hi(act, n, slot, extra=0):
            if isinstance(n, int) and n >= LAST:
                return
            act.wait_ge(panel_in[slot], (n - slot) * (PANEL_INC // 2) + PANEL_INC)
            if not (isinstance(n, int) and n < 2):
                act.wait_ge(tile_done, tiles_before(n - 1) if isinstance(n, int) else 2 * n - 2 + extra)
            last = [nc.scalar.copy(o, r) for o, r in zip(panel_parts(wH, slot, n, True), panel_parts(wRaw, slot, n, False))][-1]
            last.then_inc(panel_hi, 1)

        def prep_lo(dve, n, slot, half=None):
            if isinstance(n, int) and n >= LAST:
                return
            dve.wait_ge(panel_hi, n + 1)
            last = [nc.vector.tensor_tensor(o, r, h_.bitcast(F32), ALU.subtract)
                    for o, r, h_ in zip(*([v if half is None else v[:, half * PW // 2:(half + 1) * PW // 2]
                                           for v in panel_parts(w, slot, n, w is not wRaw)] for w in (wL, wRaw, wH)))][-1]
            if half != 0:
                last.then_inc(panel_lo, 1)

        def product(o, wh, wl, xh, xl, first, last):
            nc.tensor.matmul(o, wh, xh, start=first, stop=False)
            nc.tensor.matmul(o, wl, xh, start=False, stop=False)
            return nc.tensor.matmul(o, wh, xl, start=False, stop=last)

        msq = sb("msq", [P, 8])
        colsA = sb("colsA", [P, P])
        sinks = sb("sinks", [P, KVH, GRP])
        vBias = sb("vBias", [P, KVH * HD])
        dn_mem = ExitStack()
        dn_mem.__enter__()

        def sbd(name, shape, dt=F32):
            return dn_mem.enter_context(nc.sbuf_tensor(name, shape, dt))
        work = sbd("work", [P, 10, S])
        xTok = [work[:, 2 * t:2 * t + 2, :].rearrange("p a b -> p (a b)") for t in range(NT)]
        x_in = sem("x_in")
        x_ss = sem("x_ss")
        x_ms = sem("x_ms")
        x_r = sem("x_r")
        x_scaled = sem("x_scaled")
        x_tr = sem("x_tr")
        x_raw = sem("x_raw")
        x_hi = sem("x_hi")
        x_lo = sem("x_lo")

        maskIncl = sbd("maskIncl", [P, P])
        maskLow = sbd("maskLow", [P, P])
        maskUp = sbd("maskUp", [P, P])
        maskPair = sbd("maskPair", [P, P])
        LEVELS = [2, 4, 8, 16, 32]
        maskLev = sbd("maskLev", [P, len(LEVELS), P])
        chunkSel = sbd("chunkSel", [P, 2, P])
        inclSw = sbd("inclSw", [P, P])

        gw = sbd("gw", [P, KT, GATE_COLS])
        gwH, gwL = sbd("gwH", [P, KT, GATE_COLS], F32R), sbd("gwL", [P, KT, GATE_COLS], F32R)
        convW = sbd("convW", [P, CONV, 3 * HEADS_A])
        aLog = sbd("aLog", [P, HEADS_A])
        dtB = sbd("dtB", [P, HEADS_A])
        rowsA, rowsB = sbd("rowsA", [P, P]), sbd("rowsB", [P, P])
        R_NORMW, R_BOUT, R_BQ, R_BK = 7 * KT, 7 * KT + 1, 8 * KT + 1, 9 * KT + 1
        normW = colsA[:, R_NORMW:R_NORMW + 1]
        gains = colsA[:, 0:7 * KT].rearrange("p (i k) -> p i k", k=KT)
        rows_zero = sem("rows_zero")
        cols_done = sem("cols_done")
        cols_ok = sem("cols_ok")

        def consts_sp(sp):
            for t in range(NT):
                sp.dma_start(xTok[t], x[0, t * P:(t + 1) * P, :]).then_inc(x_in, 16)
            sp.wait_ge(rows_zero, 1)
            for i, g in enumerate((norm_mix[0], norm_mlp[0], norm_ple[0], norm_mix[1], norm_mlp[1], norm_ple[1], norm_final)):
                sp.dma_start(rowsA[i * KT:(i + 1) * KT, :], g.rearrange("(k p) -> k p", p=P)).then_inc(const_in, 16)
            sp.dma_start(rowsA[R_NORMW:R_NORMW + 1, :], dn_norm_w[0:1, :]).then_inc(const_in, 16)
            sp.dma_start(rowsA[R_BOUT:R_BOUT + KT, :], sw_b_out[0].rearrange("(k p) -> k p", p=P)).then_inc(const_in, 16)
            for j in range(GRP):
                for f in range(2):
                    src = sw_b_in[0, 0:D].rearrange("(g j f i) -> j f g i", g=KVH, j=GRP, f=2)[j:j + 1, f]
                    sp.dma_start(rowsA[R_BQ + 2 * j + f:R_BQ + 2 * j + f + 1, :].rearrange("o (g i) -> o g i", g=KVH), src).then_inc(const_in, 16)
            for f in range(2):
                src = sw_b_in[0, D:D + KVH * HD].rearrange("(o g f i) -> o f g i", o=1, g=KVH, f=2)[:, f]
                sp.dma_start(rowsA[R_BK + f:R_BK + f + 1, :].rearrange("o (g i) -> o g i", g=KVH), src).then_inc(const_in, 16)
            sp.dma_start(rowsB[0:CONV * 3 * HEADS_A, :], dn_conv_w[0].rearrange("c (k p) -> (c k) p", p=P)).then_inc(const_in, 16)
            sp.dma_start(gw[:], dn_in_v[:, :, 4 * D:4 * D + GATE_COLS]).then_inc(const_in, 16)
            sp.dma_start(aLog[:], dn_a_log[0:1, :].to_broadcast([P, HEADS_A])).then_inc(const_in, 16)
            sp.dma_start(posI[:], positions[0].rearrange("(t p) -> p t", p=P), allow_slow_non_contiguous=True).then_inc(const_in, 16)
            sp.dma_start(sinks[:].rearrange("p g j -> p (g j)"), sw_sinks[0:1, :].to_broadcast([P, KVH * GRP])).then_inc(const_in, 16)
            sp.dma_start(vBias[:], sw_b_in[0:1, D + KVH * HD:].to_broadcast([P, KVH * HD])).then_inc(const_in, 16)
            sp.dma_start(dtB[:], dn_dt_bias[0:1, :].to_broadcast([P, HEADS_A])).then_inc(const_in, 16)
        N_CONST = 16 * (7 + 2 + 2 * GRP + 2 + 1 + 6)

        posI = sbd("posI", [P, NT], I32)
        posF = sbd("posF", [P, NT])
        freq = sbd("freq", [P, HALF])
        ang = sbd("ang", [P, 2, NT, HALF])
        turn = sbd("turn", [P, 2, NT, HALF])
        trig = sbd("trig", [P, 2, NT, P])
        freq_ok = sem("freq_ok")
        ang_ok = sem("ang_ok")
        trig_ok = sem("trig_ok")
        trig_done = sem("trig_done")
        rope_ok = sem("rope_ok")

        def rope_dve(dve):
            v = nc.vector
            dve.wait_ge(freq_ok, 1)
            dve.wait_ge(const_in, N_CONST)
            v.tensor_copy(posF[:], posI[:])
            dve.drain()
            for s_ in range(2):
                v.tensor_tensor(ang[:, s_], posF[:].unsqueeze(2).to_broadcast([P, NT, HALF]),
                                freq[:].unsqueeze(1).to_broadcast([P, NT, HALF]), ALU.mult)
            dve.drain()
            big = 1.5 * 2 ** 23
            for s_ in range(2):
                v.tensor_scalar(turn[:, s_], ang[:, s_], 1.0 / (2 * math.pi), 0.25 * (1 - s_), ALU.mult, ALU.add)
            dve.drain()
            v.tensor_scalar(turn[:], turn[:], big, None, ALU.add)
            dve.drain()
            v.tensor_scalar(turn[:], turn[:], big, None, ALU.subtract)
            dve.drain()
            for part in TWO_PI:
                v.scalar_tensor_tensor(out=ang[:], in0=turn[:], scalar=-part, in1=ang[:], op0=ALU.mult, op1=ALU.add)
                dve.drain()
            v.tensor_scalar(ang[:, 0], ang[:, 0], math.pi / 2, None, ALU.add)
            dve.drain()
            v.tensor_scalar(ang[:], ang[:], 3.1415925, -3.1415925, ALU.min, ALU.max).then_inc(ang_ok, 1)

        def rope_act(act):
            act.wait_ge(ang_ok, 1)
            for g in range(KVH):
                last = nc.scalar.activation(trig[:, :, :, g * HALF:(g + 1) * HALF], ang[:], ACT.Sin)
            last.then_inc(trig_ok, 1)
            act.wait_ge(trig_done, 1)
            nc.scalar.copy(ropeC[:], bank[6])
            nc.scalar.copy(ropeS[:], bank[7]).then_inc(rope_ok, 1)

        def rope_pe(pe):
            pe.wait_ge(trig_ok, 1)
            for s_ in range(2):
                for t in range(NT):
                    last = nc.tensor.transpose(bank[6 + s_][:, rng(t)], trig[:, s_, t, :], ident[:])
            last.then_inc(trig_done, 1)


        def consts_pool(pool):
            g = nc.gpsimd
            for i in range(HALF):
                g.memset(freq[:, i:i + 1], float(np.float32(THETA) ** (-np.float32(2 * i) / np.float32(HD))))
            g.memset(ones[:], 1.0).then_inc(freq_ok, 1)
            pool.drain()

            def keep(view, base, pattern, cm):
                g.affine_select(out=view, in_=view, compare_op=ALU.is_ge, fill=0.0, base=base,
                                pattern=pattern, channel_multiplier=cm)
                pool.drain()
            g.memset(rowsB[:], 0.0)
            g.memset(rowsA[:], 0.0)
            pool.drain()
            pool.sem_inc(rows_zero, 1)
            for m in (ident, maskIncl, maskLow, maskUp, maskPair, maskLev, chunkSel, inclSw):
                g.memset(m[:], 1.0)
            g.memset(minusHalf[:], -0.5)
            pool.drain()
            keep(ident[:], 0, [[-1, P]], 1)
            keep(ident[:], 0, [[1, P]], -1)
            for m, base, st, cm in ((maskIncl, 0, 1, -1), (maskLow, -1, -1, 1), (maskUp, -1, 1, -1)):
                v = m[:].rearrange("p (a b) -> p a b", a=2)
                keep(v, base, [[CH * st, 2], [st, CH]], cm)
                keep(v, 0, [[-CH, 2], [0, CH]], 1)
                keep(v, CH - 1, [[CH, 2], [0, CH]], -1)
            v = inclSw[:].rearrange("p (a b) -> p a b", a=2)
            keep(v, CH, [[-CH, 2], [1, CH]], -1)
            keep(v, -CH, [[CH, 2], [0, CH]], 1)
            keep(v, 2 * CH - 1, [[-CH, 2], [0, CH]], -1)
            v = maskPair[:].rearrange("p (a b) -> p a b", b=2)
            keep(v, 0, [[-2, CH], [0, 2]], 1)
            keep(v, 0, [[2, CH], [0, 2]], -1)
            keep(v, -1, [[0, CH], [1, 2]], 0)
            for i, b in enumerate(LEVELS):
                n = P // (2 * b)
                v = maskLev[:, i, :].rearrange("p (a b) -> p a b", b=2 * b)
                keep(v, -b, [[-2 * b, n], [0, 2 * b]], 1)
                keep(v, 2 * b - 1, [[2 * b, n], [0, 2 * b]], -1)
                keep(v, b - 1, [[0, n], [-1, 2 * b]], 0)
            keep(chunkSel[:, 0, :], CH - 1, [[0, P]], -1)
            g.affine_select(out=chunkSel[:, 1, :], in_=chunkSel[:, 1, :], compare_op=ALU.is_ge, fill=0.0, base=-CH,
                            pattern=[[0, P]], channel_multiplier=1).then_inc(const_ok, 1)

        ssq = sbd("ssq", [P, NT])
        xScaled = sbd("xScaled", [P, NT, D])

        def first_norm_act(act):
            act.wait_ge(x_in, 16 * NT)
            for t in range(NT):
                nc.scalar.activation(xScaled[:, t, :], xTok[t], ACT.Square, accum_out=ssq[:, t:t + 1]).then_inc(x_ss, 1)

        def first_norm_dve(dve):
            dve.wait_ge(x_ss, NT)
            nc.vector.tensor_scalar(msq[:, 0:NT], ssq[:], 1.0 / D, EPS, ALU.mult, ALU.add).then_inc(x_ms, 1)
            dve.wait_ge(x_r, 1)
            for t in range(NT):
                nc.vector.tensor_scalar(xScaled[:, t, :], xTok[t], rCol[:, t:t + 1], None, ALU.mult).then_inc(x_scaled, 1)

        def first_norm_pool(pool):
            pool.wait_ge(x_ms, 1)
            nc.gpsimd.tensor_tensor(rCol[:], msq[:, 0:NT], minusHalf[:, 0:NT], ALU.pow).then_inc(x_r, 1)

        def first_tr_pe(pe):
            pe.wait_ge(x_in, 16 * NT)
            pe.wait_ge(const_ok, 1)
            for k in range(KT):
                b = k % 2
                if k >= 2:
                    pe.wait_ge(x_raw, k - 1)
                for t in range(NT):
                    last = nc.tensor.transpose(bank[b][:, rng(t)], xTok[t][:, rng(k)], ident[:])
                last.then_inc(x_tr, 1)
            pe.wait_ge(const_in, N_CONST)
            nc.tensor.transpose(bank[4][:, 0:P], rowsA[:], ident[:])
            nc.tensor.transpose(bank[4][:, P:2 * P], rowsB[:], ident[:]).then_inc(cols_done, 1)
            pe.wait_ge(x_scaled, NT)
            for k in range(KT):
                b = 2 + k % 2
                if k >= 2:
                    pe.wait_ge(x_lo, k - 1)
                for t in range(NT):
                    last = nc.tensor.transpose(bank[b][:, rng(t)], xScaled[:, t, rng(k)], ident[:])
                last.then_inc(x_tr, 1)

        def first_tr_act(act):
            for k in range(KT):
                act.wait_ge(x_tr, k + 1)
                nc.scalar.copy(hT[:, k, :], bank[k % 2]).then_inc(x_raw, 1)
            act.wait_ge(cols_done, 1)
            nc.scalar.copy(colsA[:], bank[4][:, 0:P])
            nc.scalar.copy(convW[:].rearrange("p c k -> p (c k)"), bank[4][:, P:P + CONV * 3 * HEADS_A]).then_inc(cols_ok, 1)
            act.drain()
            for k in range(KT):
                act.wait_ge(x_tr, KT + k + 1)
                nc.scalar.activation(aH[:, k, :], bank[2 + k % 2], ACT.Copy, scale=gains[:, 0, k:k + 1]).then_inc(x_hi, 1)

        def first_tr_dve(dve):
            dve.wait_ge(cols_ok, 1)
            for k in range(KT):
                dve.wait_ge(x_hi, k + 1)
                nc.vector.scalar_tensor_tensor(out=aL[:, k, :], in0=bank[2 + k % 2], scalar=gains[:, 0, k:k + 1],
                                               in1=aH[:, k, :].bitcast(F32), op0=ALU.mult, op1=ALU.subtract).then_inc(x_lo, 1)

        G_, B_, NB_, EG_, EGS_, ED_, EL0_, EL1_ = range(8)
        gate = sbd("gate", [P, HEADS_A, 8, NT])
        hc = sbd("hc", [P, 2, 8, NT])
        gt = sbd("gt", [P, 8, HEADS_A, NT])
        gw_hi = sem("gw_hi"); gw_lo = sem("gw_lo")
        gate_raw = sem("gate_raw")
        gate_e = sem("gate_e")
        gate_v = sem("gate_v")
        gate_cum = sem("gate_cum")
        gate_ok = sem("gate_ok")
        logits = bank[4][:, 0:NT * GATE_COLS].rearrange("p (t c) -> p t c", t=NT)
        cums = bank[5][:, 0:5 * HEADS_A * NT].rearrange("p (q h t) -> p q h t", q=5, h=HEADS_A)

        def gates_act(act):
            act.wait_ge(const_in, N_CONST)
            nc.scalar.copy(gwH[:], gw[:]).then_inc(gw_hi, 1)

        def gates_act2(act):
            act.wait_ge(gate_v, 1)
            nc.scalar.activation(gt[:, 1], gt[:, 0], ACT.Abs).then_inc(gate_e, 1)
            nc.scalar.activation(gt[:, 7, :, 0], aLog[:], ACT.Exp)
            act.drain()
            nc.scalar.activation(gt[:, 2], gt[:, 1], ACT.Exp, scale=-1.0)
            act.wait_ge(gate_v, 2)
            nc.scalar.activation(gt[:, 3], gt[:, 3], ACT.Tanh, scale=0.5).then_inc(gate_e, 1)
            act.wait_ge(gate_cum, 1)
            nc.scalar.activation(gate[:, :, EG_:EL1_ + 1, :].rearrange("p h q t -> p q h t"), cums, ACT.Exp).then_inc(gate_e, 1)

        def gates_dve(dve):
            v = nc.vector
            dve.wait_ge(gw_hi, 1)
            v.tensor_tensor(gwL[:], gw[:], gwH[:].bitcast(F32), ALU.subtract).then_inc(gw_lo, 1)
            dve.wait_ge(gate_raw, 1)
            dve.wait_ge(const_in, N_CONST)
            v.tensor_tensor(gt[:, 0], logits[:, :, HEADS_A:].rearrange("p t h -> p h t"),
                            dtB[:].unsqueeze(2).to_broadcast([P, HEADS_A, NT]), ALU.add).then_inc(gate_v, 1)
            v.tensor_copy(gt[:, 3], logits[:, :, 0:HEADS_A].rearrange("p t h -> p h t")).then_inc(gate_v, 1)
            dve.wait_ge(gate_e, 2)
            v.tensor_scalar(gt[:, 4], gt[:, 2], 2.0, None, ALU.add)
            dve.drain()
            v.reciprocal(gt[:, 4], gt[:, 4])
            dve.drain()
            v.tensor_tensor(gt[:, 5], gt[:, 4], gt[:, 2], ALU.mult)
            dve.drain()
            v.tensor_tensor(gt[:, 6], gt[:, 5], gt[:, 5], ALU.mult)
            dve.drain()
            v.tensor_scalar(gt[:, 4], gt[:, 6], 1.0 / 19, None, ALU.mult)
            for n in (17, 15, 13, 11, 9, 7, 5, 3):
                dve.drain()
                v.scalar_tensor_tensor(out=gt[:, 4], in0=gt[:, 4], scalar=1.0 / n, in1=gt[:, 6], op0=ALU.add, op1=ALU.mult)
            dve.drain()
            v.scalar_tensor_tensor(out=gt[:, 4], in0=gt[:, 4], scalar=1.0, in1=gt[:, 5], op0=ALU.add, op1=ALU.mult)
            v.tensor_scalar(gt[:, 0], gt[:, 0], 0.0, None, ALU.max)
            dve.drain()
            v.scalar_tensor_tensor(out=gt[:, 4], in0=gt[:, 4], scalar=2.0, in1=gt[:, 0], op0=ALU.mult, op1=ALU.add)
            dve.drain()
            v.scalar_tensor_tensor(out=gate[:, :, G_, :], in0=gt[:, 4], scalar=-1.0,
                                   in1=gt[:, 7, :, 0:1].to_broadcast([P, HEADS_A, NT]), op0=ALU.mult, op1=ALU.mult)
            v.tensor_scalar(gate[:, :, B_, :], gt[:, 3], 1.0, 0.5, ALU.add, ALU.mult)
            dve.drain()
            v.tensor_scalar(gate[:, :, NB_, :], gate[:, :, B_, :], -1.0, None, ALU.mult)
            v.tensor_copy(gt[:, 5], gate[:, :, G_, :]).then_inc(gate_v, 1)

        def gates_pe(pe):
            pe.wait_ge(gw_lo, 1)
            pe.wait_ge(cols_ok, 1)
            pe.wait_ge(x_lo, KT)
            for t in range(NT):
                for k in range(KT):
                    for i, (a, w) in enumerate(((aH, gwH), (aL, gwH), (aH, gwL))):
                        last = nc.tensor.matmul(logits[:, t, :], a[:, k, rng(t)], w[:, k, :],
                                                start=(k == 0 and i == 0), stop=(k == KT - 1 and i == 2))
            last.then_inc(gate_raw, 1)
            pe.wait_ge(gate_v, 3)
            g = gt[:, 5].rearrange("p h t -> p (h t)")
            for i, m in enumerate((maskIncl[:], inclSw[:], maskLow[:], chunkSel[:, 0, :], chunkSel[:, 1, :])):
                last = nc.tensor.matmul(cums[:, i].rearrange("p h t -> p (h t)"), m, g, start=True, stop=True)
            last.then_inc(gate_cum, 1)

        def t4(buf):
            return buf.rearrange("p (t c) -> p t c", t=NT)
        qF, kF, vF, tanhT = (work[:, i, :] for i in range(4))
        gA, decT, lowT, kEg = (t4(work[:, i, :]) for i in range(4, 8))
        attT = [t4(work[:, 8 + i, :]) for i in range(2)]
        sq2 = xScaled[:, 0, :].rearrange("p (a b) -> p a b", a=2)
        betaUp, inv = t4(xScaled[:, 1, 0:S]), t4(xScaled[:, 1, S:])
        invT, tMask = t4(xScaled[:, 2, 0:S]), t4(xScaled[:, 2, S:])
        qw = [q.rearrange("p (t r c) -> p t r c", t=NT, r=2) for q in (xScaled[:, 3, :], sqT[:].rearrange("p a b -> p (a b)"))]
        taps = sbd("taps", [P, CONV, S])
        kTok, vTok = sbd("kTok", [P, NT, P]), sbd("vTok", [P, NT, P])
        kDec = [trig[:, i] for i in range(2)]
        uB = sbd("uB", [P, 2, NT, P])
        kHatT = sbd("kHatT", [P, S])
        vNew = sbd("vNew", [P, P])
        state = sbd("state", [P, P])
        oTok = sbd("oTok", [P, NT, P])
        yF = sbd("yF", [P, S])
        oSq = t4(yF[:])
        st8 = sbd("st8", [P, 8])
        rs8 = sbd("rs8", [P, 2, 8])
        os4 = sbd("os4", [P, 4, NT])

        zF = [rBC[:], sqSum[:]]
        oq_ok = sem("oq_ok")
        taps_ok = sem("taps_ok")
        conv_ok = sem("conv_ok")
        tanh_ok = sem("tanh_ok")
        feat_ok = sem("feat_ok")
        sq_ok = sem("sq_ok")
        hc_ok = sem("hc_ok")
        nrm_done = sem("nrm_done"); ktr_done = sem("ktr_done"); vtr_done = sem("vtr_done")
        st_ok = sem("st_ok")
        rs_ok = sem("rs_ok")
        khat_ok = sem("khat_ok")
        kscaled = sem("kscaled")
        bup_ok = sem("bup_ok"); decm_ok = sem("decm_ok")
        vtok_ok = sem("vtok_ok")
        khtr_done = sem("khtr_done")
        khT_ok = sem("khT_ok")
        gA_ok = sem("gA_ok")
        dec_done = sem("dec_done")
        dec_ok = sem("dec_ok")
        gram_done = sem("gram_done")
        att_ok = sem("att_ok")
        x1_ok = sem("x1_ok")
        xtr_done = sem("xtr_done")
        xtr_ok = sem("xtr_ok")
        t_done = sem("t_done"); t_ok = sem("t_ok")
        p_done = sem("p_done"); x_ok = sem("x_ok")
        wT_done = sem("wT_done"); u_done = sem("u_done")
        qw_ok = sem("qw_ok")
        qq_ok = sem("qq_ok")
        s_ok = sem("s_ok")
        ws_done = sem("ws_done"); vn_ok = sem("vn_ok")
        su_done = sem("su_done"); av_done = sem("av_done"); o_ok = sem("o_ok")
        osq_ok = sem("osq_ok"); os_ok = sem("os_ok"); or_ok = sem("or_ok"); on_ok = sem("on_ok")
        otr_done = sem("otr_done"); y_ok = sem("y_ok"); yh_ok = sem("yh_ok"); yl_ok = sem("yl_ok")

        def bc(col):
            return col.unsqueeze(2).to_broadcast([P, NT, P])

        def bm(mask):
            return mask.unsqueeze(1).to_broadcast([P, NT, P])

        def tiles(b):
            return bank[b].rearrange("p (t c) -> p t c", t=NT)

        def load_dn(sp, h, j):
            for i in range(2):
                dst = wRaw[:, j, i * D:(i + 1) * D].rearrange("p (k n) -> p k n", k=KT)
                sp.dma_start(dst, dn_in_v[:, :, bass.ds(h * P + (2 * j + i) * D, P)]).then_inc(panel_in[j], PANEL_INC // 2)

        def dn_sp(sp):
            for j in range(2):
                load_dn(sp, 0, j)
            with sp.Fori(1, HEADS_A) as h:
                for j in range(2):
                    sp.wait_ge(panel_lo, 2 * h + j - 1)
                    load_dn(sp, h, j)

        UNITS = 4 * KT
        BX, BY, BZ = 2, 3, 4
        BW, BS, BO = 5, 6, 7

        def project_pe(pe, h, u0, u1, first=False):
            for u in range(u0, u1):
                b, k = u // KT, u % KT
                if u % (2 * KT) == 0:
                    pe.wait_ge(panel_lo, 2 * h + b // 2 + 1)
                if k == 0 and (b >= 2 or not first):
                    if b == 1:
                        pe.wait_ge(feat_ok, 4 * h - 1)
                    else:
                        pe.wait_ge(taps_ok, 3 * h + (0, 0, 1, 2)[b])
                c = (b % 2) * D + k * P
                last = product(bank[b % 2], wH[:, b // 2, c:c + P], wL[:, b // 2, c:c + P],
                               aH[:, k, :], aL[:, k, :], k == 0, k == KT - 1)
                if k == KT - 1:
                    last.then_inc(tile_done, 1)

        def taps_act(act, h, b, first=False):
            act.wait_ge(tile_done, 4 * h + b + 1)
            if b or not first:
                act.wait_ge(feat_ok, 4 * h + b)
            for c in range(CONV):
                last = nc.scalar.activation(taps[:, c, c:S], bank[b % 2][:, 0:S - c], ACT.Copy,
                                            scale=convW[:, CONV - 1 - c, bass.ds(b * HEADS_A + h, 1)])
            last.then_inc(taps_ok, 1)

        def taps_pool(pool, h, b):
            g = nc.gpsimd
            pool.wait_ge(taps_ok, 3 * h + b + 1)
            g.tensor_tensor(taps[:, 0, 1:], taps[:, 0, 1:], taps[:, 1, 1:], ALU.add)
            g.tensor_tensor(taps[:, 2, 3:], taps[:, 2, 3:], taps[:, 3, 3:], ALU.add)
            pool.drain()
            g.tensor_tensor(taps[:, 0, 2:], taps[:, 0, 2:], taps[:, 2, 2:], ALU.add).then_inc(conv_ok, 1)

        def tanh_act(act, h, b, first=False):
            act.wait_ge(conv_ok, 3 * h + b + 1)
            if b == 2:
                act.wait_ge(feat_ok, 4 * h + 3)
            nc.scalar.activation(tanhT, taps[:, 0, :], ACT.Tanh, scale=0.5).then_inc(tanh_ok, 1)

        def silu_dve(dve, h, b, first=False):
            dve.wait_ge(tanh_ok, 4 * h + (1, 2, 4)[b])
            if b == 0 and not first:
                dve.wait_ge(qq_ok, h)
            nc.vector.scalar_tensor_tensor(out=(qF, kF, vF)[b], in0=tanhT, scalar=1.0, in1=taps[:, 0, :],
                                           op0=ALU.add, op1=ALU.mult).then_inc(feat_ok, 1)

        def square_pool(pool, h, b):
            pool.wait_ge(feat_ok, 4 * h + b + 1)
            f = (qF, kF)[b]
            nc.gpsimd.tensor_tensor(sq2[:, b], f, f, ALU.mult).then_inc(sq_ok, 1)

        def z_act(act, h):
            act.wait_ge(tile_done, 4 * h + 4)
            act.wait_ge(feat_ok, 4 * h + 2)
            nc.scalar.activation(tanhT, bank[1], ACT.Tanh, scale=0.5).then_inc(tanh_ok, 1)

        def z_dve(dve, h, slot):
            dve.wait_ge(tanh_ok, 4 * h + 3)
            nc.vector.scalar_tensor_tensor(out=zF[slot], in0=tanhT, scalar=1.0, in1=bank[1], op0=ALU.add, op1=ALU.mult).then_inc(feat_ok, 1)

        def per_tile(fn):
            for t in range(NT):
                last = fn(t)
            return last

        def dn_step_pe(pe, b, a, p, s):
            done = [0]

            def fill(n):
                if p is not None:
                    n = min(n, UNITS - done[0])
                    project_pe(pe, p, done[0], done[0] + n)
                    done[0] += n

            def walk(n):
                if b is None:
                    return
                pe.wait_ge(s_ok, 9 * b + n + 1)
                if n:
                    pe.wait_ge(o_ok, 8 * b + n)
                nc.tensor.matmul(bank[BW][:, 0:P], qw[s][:, n // 2, n % 2, :], state[:], start=True, stop=True).then_inc(ws_done, 1)

            def update(n):
                if b is None:
                    return
                t, c = n // 2, n % 2
                rows, orows = slice(c * CH, (c + 1) * CH), slice((1 - c) * CH, (2 - c) * CH)
                pe.wait_ge(vn_ok, 8 * b + n + 1)
                nc.tensor.matmul(bank[BS][:, 0:P], kDec[s][rows, t, :], vNew[rows, :], start=True, stop=True).then_inc(su_done, 1)
                nc.tensor.matmul(bank[BO][orows, 0:P], attT[s][rows, t, rows], vNew[rows, :],
                                 start=True, stop=True).then_inc(av_done, 1)

            if b is not None:
                pe.wait_ge(qw_ok, b + 1)
                pe.wait_ge(qq_ok, b + 1)
                pe.wait_ge(att_ok, b + 1)
            if a is not None:
                pe.wait_ge(sq_ok, 2 * a + 2)
                for t in range(NT):
                    for c in range(2):
                        src = sq2[:, 0, t * P + (1 - c) * CH:t * P + (1 - c) * CH + CH]
                        nc.tensor.matmul(bank[BZ][c * CH:(c + 1) * CH, t:t + 1], src, ones[:, 0:1], start=True, stop=True)
                per_tile(lambda t: nc.tensor.matmul(bank[BZ][:, NT + t:NT + t + 1], sq2[:, 1, rng(t)], ones[:, 0:1],
                                                    start=True, stop=True)).then_inc(nrm_done, 1)
                per_tile(lambda t: nc.tensor.transpose(bank[BX][:, rng(t)], kF[:, rng(t)], ident[:])).then_inc(ktr_done, 1)
            walk(0)
            fill(F[0])
            update(0)
            if a is not None:
                pe.wait_ge(gA_ok, a + 1)
                per_tile(lambda t: nc.tensor.matmul(bank[BY][:, rng(t)], gA[:, t, :], maskIncl[:], start=True, stop=True)).then_inc(dec_done, 1)
            walk(1)
            fill(F[1])
            if a is not None:
                pe.wait_ge(khat_ok, a + 1)
                per_tile(lambda t: nc.tensor.transpose(bank[BX][:, rng(t)], kTok[:, t, :], ident[:])).then_inc(khtr_done, 1)
            update(1)
            fill(F[2])
            walk(2)
            if a is not None:
                pe.wait_ge(khT_ok, a + 1)
                pe.wait_ge(st_ok, a + 1)
                per_tile(lambda t: nc.tensor.matmul(bank[BZ][:, rng(t)], kHatT[:, rng(t)], kHatT[:, rng(t)],
                                                    start=True, stop=True)).then_inc(gram_done, 1)
                per_tile(lambda t: nc.tensor.matmul(bank[BX][:, rng(t)], kHatT[:, rng(t)], qF[:, rng(t)],
                                                    start=True, stop=True)).then_inc(gram_done, 1)
            update(2)
            fill(F[3])
            walk(3)
            fill(F[4])
            update(3)
            fill(F[5])
            if a is not None:
                pe.wait_ge(x1_ok, a + 1)
                per_tile(lambda t: nc.tensor.transpose(bank[BZ][:, rng(t)], invT[:, t, :], ident[:])).then_inc(xtr_done, 1)
            between = ((lambda: walk(4), lambda: update(4), lambda: walk(5)),
                       (lambda: update(5), lambda: walk(6), lambda: update(6)),
                       (lambda: walk(7), lambda: update(7), lambda: None),
                       (lambda: None,) * 3, (lambda: None,) * 3)
            for i in range(len(LEVELS)):
                between[i][0]()
                fill(F[6][i][0])
                if a is not None:
                    pe.wait_ge(xtr_ok, 6 * a + i + 1)
                    if i == 0:
                        pe.wait_ge(att_ok, a + 1)
                    per_tile(lambda t: nc.tensor.matmul(bank[BX][:, rng(t)], lowT[:, t, :], inv[:, t, :],
                                                        start=True, stop=True)).then_inc(t_done, 1)
                between[i][1]()
                fill(F[6][i][1])
                if a is not None:
                    pe.wait_ge(t_ok, 5 * a + i + 1)
                    if i == 0:
                        pe.wait_ge(dec_ok, a + 1)
                    if i == VTR + 1:
                        pe.wait_ge(vtok_ok, a + 1)
                    per_tile(lambda t: nc.tensor.matmul(bank[BY][:, rng(t)], invT[:, t, :], tMask[:, t, :],
                                                        start=True, stop=True)).then_inc(p_done, 1)
                between[i][2]()
                fill(F[6][i][2])
                if a is not None:
                    pe.wait_ge(x_ok, 5 * a + i + 1)
                    per_tile(lambda t: nc.tensor.transpose(bank[BZ][:, rng(t)], inv[:, t, :], ident[:])).then_inc(xtr_done, 1)
                    if i == VTR:
                        pe.wait_ge(feat_ok, 4 * a + 4)
                        per_tile(lambda t: nc.tensor.transpose(bank[BY][:, rng(t)], vF[:, rng(t)], ident[:])).then_inc(vtr_done, 1)
            if b is not None:
                pe.wait_ge(on_ok, b + 1)
                per_tile(lambda t: nc.tensor.transpose(bank[BS][:, rng(t)], oTok[:, t, :], ident[:])).then_inc(otr_done, 1)
            fill(F[7])
            if a is not None:
                pe.wait_ge(xtr_ok, 6 * a + 6)
                pe.wait_ge(kscaled, a + 1)
                per_tile(lambda t: nc.tensor.matmul(bank[BX][:, rng(t)], kEg[:, t, :], invT[:, t, :],
                                                    start=True, stop=True)).then_inc(wT_done, 1)
                per_tile(lambda t: nc.tensor.matmul(bank[BY][:, rng(t)], invT[:, t, :], vTok[:, t, :],
                                                    start=True, stop=True)).then_inc(u_done, 1)
            fill(UNITS)

        VTR = 0
        F = (1, 1, 2, 1, 1, 3, ((1, 1, 1), (1, 1, 1), (1, 1, 1), (1, 1, 1), (2, 1, 1)), 3)

        def dn_step_act(act, b, a, p, s, n):
            a_ = nc.scalar

            def q_part(n):
                if b is None:
                    return
                t, c = n // 2, n % 2
                orows = slice((1 - c) * CH, (2 - c) * CH)
                act.wait_ge(vn_ok, 8 * b + n + 1)
                a_.activation(oTok[orows, t, :], bank[BW][orows, 0:P], ACT.Copy, scale=hc[orows, s, EGS_, t:t + 1]).then_inc(oq_ok, 1)

            q_part(0)
            if a is not None:
                z_act(act, a)
                act.wait_ge(dec_done, a + 1)
                a_.activation(decT, t4(bank[BY]), ACT.Exp).then_inc(dec_ok, 1)
            q_part(1)
            if a is not None:
                act.wait_ge(khtr_done, a + 1)
                a_.copy(kHatT[:], bank[BX]).then_inc(khT_ok, 1)
            q_part(2)
            q_part(3)
            if n is not None:
                prep_hi(act, n, 1)
            if a is not None:
                act.wait_ge(xtr_done, 6 * a + 1)
                a_.copy(inv, t4(bank[BZ])).then_inc(xtr_ok, 1)
            for i in range(len(LEVELS)):
                if i == 0:
                    if a is not None:
                        tanh_act(act, a, 2)
                    q_part(4)
                    q_part(5)
                if i == 1:
                    q_part(6)
                if i == 2 and p is not None:
                    tanh_act(act, p, 0)
                if i == 4 and p is not None:
                    tanh_act(act, p, 1)
                if a is not None:
                    act.wait_ge(xtr_done, 6 * a + i + 2)
                    a_.copy(invT, t4(bank[BZ])).then_inc(xtr_ok, 1)
                if i == VTR and a is not None:
                    act.wait_ge(vtr_done, a + 1)
                    a_.activation(vTok[:], t4(bank[BY]), ACT.Copy, scale=0.5).then_inc(vtok_ok, 1)
                if i == 1:
                    q_part(7)
                if i == 2 and b is not None:
                    act.wait_ge(o_ok, 8 * b + 8)
                    a_.activation(oSq, oTok[:], ACT.Square).then_inc(osq_ok, 1)
                if p is not None and i % 2 == 0:
                    taps_act(act, p, i // 2)
                if p is not None and i == 3:
                    prep_hi(act, n + 1, 0)
            if b is not None:
                act.wait_ge(y_ok, b + 1)
                a_.copy(bH[:, b, :], yF[:]).then_inc(yh_ok, 1)
            if a is not None:
                act.wait_ge(wT_done, a + 1)
                a_.copy(qw[1 - s][:, :, 0, 0:CH], t4(bank[BX])[:, :, 0:CH])
                a_.copy(qw[1 - s][:, :, 1, CH:P], t4(bank[BX])[:, :, CH:P]).then_inc(qw_ok, 1)

        def dn_step_dve(dve, b, a, p, s, n):
            v = nc.vector

            def correct(n):
                if b is None:
                    return
                t, c = n // 2, n % 2
                rows = slice(c * CH, (c + 1) * CH)
                dve.wait_ge(ws_done, 8 * b + n + 1)
                v.scalar_tensor_tensor(out=vNew[rows, :], in0=bank[BW][rows, 0:P], scalar=hc[rows, s, NB_, t:t + 1],
                                       in1=uB[rows, s, t, :], op0=ALU.mult, op1=ALU.add).then_inc(vn_ok, 1)
                dve.drain()

            def advance(n):
                if b is None:
                    return
                t, c = n // 2, n % 2
                orows = slice((1 - c) * CH, (2 - c) * CH)
                dve.wait_ge(su_done, 8 * b + n + 1)
                v.scalar_tensor_tensor(out=state[:], in0=state[:], scalar=hc[:, s, EL0_ + c, t:t + 1], in1=bank[BS][:, 0:P],
                                       op0=ALU.mult, op1=ALU.add).then_inc(s_ok, 1)
                dve.wait_ge(av_done, 8 * b + n + 1)
                dve.wait_ge(oq_ok, 8 * b + n + 1)
                v.tensor_tensor(oTok[orows, t, :], oTok[orows, t, :], bank[BO][orows, 0:P], ALU.add).then_inc(o_ok, 1)

            def tail(part):
                if b is None:
                    return
                if part == 0:
                    v.tensor_tensor(os4[:, 1, :], rs8[:, s, 0:4], rs8[:, s, 0:4], ALU.mult)
                    dve.wait_ge(osq_ok, b + 1)
                    v.tensor_reduce(os4[:, 0, :], oSq, AX, ALU.add)
                    dve.drain()
                    v.tensor_tensor(os4[:, 0, :], os4[:, 0, :], os4[:, 1, :], ALU.mult)
                    dve.drain()
                    v.tensor_scalar(os4[:, 0, :], os4[:, 0, :], 1.0 / (P * P), EPS, ALU.mult, ALU.add).then_inc(os_ok, 1)
                elif part == 1:
                    dve.wait_ge(or_ok, b + 1)
                    v.scalar_tensor_tensor(out=os4[:, 3, :], in0=os4[:, 2, :], scalar=0.5 * P ** -0.5, in1=rs8[:, s, 0:4],
                                           op0=ALU.mult, op1=ALU.mult)
                    dve.drain()
                    v.tensor_tensor(oTok[:], oTok[:], bc(os4[:, 3, :]), ALU.mult).then_inc(on_ok, 1)
                elif part == 2:
                    dve.wait_ge(otr_done, b + 1)
                    yt, zt = t4(yF[:]), t4(zF[s])
                    for c in range(2):
                        last = v.scalar_tensor_tensor(out=yt[:, :, c * CH:(c + 1) * CH], in0=t4(bank[BS])[:, :, (1 - c) * CH:(2 - c) * CH],
                                                      scalar=normW, in1=zt[:, :, c * CH:(c + 1) * CH], op0=ALU.mult, op1=ALU.mult)
                    last.then_inc(y_ok, 1)
                    dve.drain()
                else:
                    dve.wait_ge(yh_ok, b + 1)
                    v.tensor_tensor(bL[:, b, :], yF[:], bH[:, b, :].bitcast(F32), ALU.subtract).then_inc(yl_ok, 1)

            if a is not None:
                v.tensor_copy(hc[:, 1 - s], gate[:, a]).then_inc(hc_ok, 1)
                dve.drain()
                v.tensor_tensor(gA, bm(maskLow[:]), bc(hc[:, 1 - s, G_, :]), ALU.mult).then_inc(gA_ok, 1)
                dve.wait_ge(nrm_done, a + 1)
                v.tensor_scalar(st8[:], bank[BZ][:, 0:8], 4 * EPS, None, ALU.add).then_inc(st_ok, 1)
            correct(0)
            advance(0)
            if a is not None:
                z_dve(dve, a, 1 - s)
            correct(1)
            if a is not None:
                dve.wait_ge(rs_ok, 2 * a + 1)
                dve.wait_ge(ktr_done, a + 1)
                v.tensor_tensor(kTok[:], t4(bank[BX]), bc(rs8[:, 1 - s, 4:8]), ALU.mult).then_inc(khat_ok, 1)
            advance(1)
            correct(2)
            advance(2)
            correct(3)
            if a is not None:
                dve.wait_ge(gram_done, 2 * a + 2)
                dve.wait_ge(bup_ok, a + 1)
                v.tensor_tensor(lowT, t4(bank[BZ]), betaUp, ALU.mult)
                dve.drain()
                v.tensor_tensor(invT, lowT, bm(maskPair[:]), ALU.mult)
                dve.drain()
                v.tensor_tensor(invT, bm(ident[:]), invT, ALU.subtract).then_inc(x1_ok, 1)
            advance(3)
            if a is not None:
                dve.wait_ge(decm_ok, a + 1)
                v.tensor_tensor(attT[1 - s], t4(bank[BX]), decT, ALU.mult).then_inc(att_ok, 1)
            between = ((lambda: correct(4), lambda: (advance(4), correct(5))),
                       (lambda: (advance(5), correct(6)), lambda: advance(6)),
                       (lambda: correct(7), lambda: advance(7)),
                       (lambda: None, lambda: tail(0)),
                       (lambda: tail(1), lambda: None))
            for i in range(len(LEVELS)):
                between[i][0]()
                if a is not None:
                    dve.wait_ge(t_done, 5 * a + i + 1)
                    v.tensor_tensor(tMask, t4(bank[BX]), bm(maskLev[:, i, :]), ALU.mult).then_inc(t_ok, 1)
                if i == 0 and a is not None:
                    silu_dve(dve, a, 2)
                if i == 2 and p is not None:
                    silu_dve(dve, p, 0)
                between[i][1]()
                if a is not None:
                    dve.wait_ge(p_done, 5 * a + i + 1)
                    v.tensor_tensor(inv, inv, t4(bank[BY]), ALU.subtract).then_inc(x_ok, 1)
                if i in (0, 1) and n is not None:
                    prep_lo(dve, n, 1, i)
                if i == 4 and p is not None:
                    silu_dve(dve, p, 1)
                if i >= 3 and p is not None:
                    prep_lo(dve, n + 1, 0, i - 3)
            tail(2)
            tail(3)
            if a is not None:
                dve.wait_ge(u_done, a + 1)
                v.tensor_tensor(uB[:, 1 - s], t4(bank[BY]), bc(hc[:, 1 - s, B_, :]), ALU.mult)
                dve.drain()
                v.memset(state[:], 0.0).then_inc(s_ok, 1)
            dve.drain()

        def dn_step_pool(pool, b, a, p, s):
            g = nc.gpsimd
            if a is not None:
                qt = t4(qF)
                q_ = 1 - s
                pool.wait_ge(st_ok, a + 1)
                g.tensor_tensor(rs8[:, q_, 4:8], st8[:, 4:8], minusHalf[:, 0:4], ALU.pow).then_inc(rs_ok, 1)
                g.tensor_tensor(betaUp, bm(maskUp[:]), bc(hc[:, q_, B_, :]), ALU.mult)
                g.tensor_tensor(rs8[:, q_, 0:4], st8[:, 0:4], minusHalf[:, 0:4], ALU.pow).then_inc(rs_ok, 1)
                pool.drain()
                pool.wait_ge(dec_ok, a + 1)
                g.tensor_tensor(betaUp, betaUp, decT, ALU.mult).then_inc(bup_ok, 1)
                pool.drain()
                g.tensor_tensor(decT, decT, bm(maskIncl[:]), ALU.mult).then_inc(decm_ok, 1)
                g.tensor_copy(qw[q_][:, :, 0, CH:P], qt[:, :, 0:CH])
                g.tensor_copy(qw[q_][:, :, 1, 0:CH], qt[:, :, CH:P]).then_inc(qq_ok, 1)
                taps_pool(pool, a, 2)
                pool.wait_ge(khat_ok, a + 1)
                g.tensor_tensor(kEg, kTok[:], bc(hc[:, q_, EG_, :]), ALU.mult)
                g.tensor_tensor(kDec[q_], kTok[:], bc(hc[:, q_, ED_, :]), ALU.mult).then_inc(kscaled, 1)
            if p is not None:
                taps_pool(pool, p, 0)
            if b is not None:
                pool.wait_ge(os_ok, b + 1)
                g.tensor_tensor(os4[:, 2, :], os4[:, 0, :], minusHalf[:, 0:4], ALU.pow).then_inc(or_ok, 1)
            if p is not None:
                square_pool(pool, p, 0)
                taps_pool(pool, p, 1)
                square_pool(pool, p, 1)

        PAIRS = (HEADS_A - 2) // 2

        def dn_pe(pe):
            project_pe(pe, 0, 0, UNITS, first=True)
            dn_step_pe(pe, None, 0, 1, 1)
            with pe.Fori(0, PAIRS) as i:
                dn_step_pe(pe, 2 * i, 2 * i + 1, 2 * i + 2, 0)
                dn_step_pe(pe, 2 * i + 1, 2 * i + 2, 2 * i + 3, 1)
            dn_step_pe(pe, HEADS_A - 2, HEADS_A - 1, None, 0)
            dn_step_pe(pe, HEADS_A - 1, None, None, 1)

        def dn_act(act):
            for b in range(2):
                taps_act(act, 0, b, first=True)
                tanh_act(act, 0, b, first=True)
            taps_act(act, 0, 2)
            prep_hi(act, 2, 0)
            dn_step_act(act, None, 0, 1, 1, 3)
            with act.Fori(0, PAIRS) as i:
                dn_step_act(act, 2 * i, 2 * i + 1, 2 * i + 2, 0, 4 * i + 5)
                dn_step_act(act, 2 * i + 1, 2 * i + 2, 2 * i + 3, 1, 4 * i + 7)
            dn_step_act(act, HEADS_A - 2, HEADS_A - 1, None, 0, 2 * HEADS_A + 1)
            dn_step_act(act, HEADS_A - 1, None, None, 1, None)

        def dn_dve(dve):
            for b in range(2):
                silu_dve(dve, 0, b, first=True)
            prep_lo(dve, 2, 0)
            dn_step_dve(dve, None, 0, 1, 1, 3)
            with dve.Fori(0, PAIRS) as i:
                dn_step_dve(dve, 2 * i, 2 * i + 1, 2 * i + 2, 0, 4 * i + 5)
                dn_step_dve(dve, 2 * i + 1, 2 * i + 2, 2 * i + 3, 1, 4 * i + 7)
            dn_step_dve(dve, HEADS_A - 2, HEADS_A - 1, None, 0, 2 * HEADS_A + 1)
            dn_step_dve(dve, HEADS_A - 1, None, None, 1, None)

        def dn_pool(pool):
            for b in range(2):
                taps_pool(pool, 0, b)
                square_pool(pool, 0, b)
            dn_step_pool(pool, None, 0, 1, 1)
            with pool.Fori(0, PAIRS) as i:
                dn_step_pool(pool, 2 * i, 2 * i + 1, 2 * i + 2, 0)
                dn_step_pool(pool, 2 * i + 1, 2 * i + 2, 2 * i + 3, 1)
            dn_step_pool(pool, HEADS_A - 2, HEADS_A - 1, None, 0)
            dn_step_pool(pool, HEADS_A - 1, None, None, 1)

        dn_mem.close()

        acc = sb("acc", [P, KT, S])
        pleT = sb("pleT", [P, KT, S])
        mlp_mem = ExitStack()
        mlp_mem.__enter__()

        def sbm(name, shape, dt=F32):
            return mlp_mem.enter_context(nc.sbuf_tensor(name, shape, dt))
        pTok = sbm("pTok", [P, NT, PLE])
        pH, pL = sbm("pH", [P, 2, S], F32R), sbm("pL", [P, 2, S], F32R)
        hid = sbm("hid", [P, 2, S])
        hid2 = sbm("hid2", [P, 2, S])
        rSq = sbm("rSq", [P, S])
        diag = sbm("diag", [P, NT, P])
        gA2, gB2 = sbm("gA2", [P, 2, S]), sbm("gB2", [P, 2, S])

        res_ok = sem("res_ok")
        next_hi = sem("next_hi")
        next_lo = sem("next_lo")
        sq_done = sem("sq_done")
        sq_used = sem("sq_used")
        n_sum = sem("n_sum"); n_ms = sem("n_ms"); n_r = sem("n_r")
        n_diag = sem("n_diag"); n_bc = sem("n_bc"); n_ok = sem("n_ok")
        p_in = sem("p_in"); ptr_done = sem("ptr_done"); p_hi = sem("p_hi"); p_lo = sem("p_lo")
        hid_f = sem("hid_f"); hid_hi = sem("hid_hi"); hid_lo = sem("hid_lo")
        down_read = sem("down_read")
        ple_ok = sem("ple_ok")
        gate_in = sem("gate_in")
        gate_th = sem("gate_th")

        X_A, X_B = (aH, aL), (bH, bL)
        NEXT = [X_A, X_A, X_B, X_B, X_B, None]

        def next_act(act, u, m):
            act.wait_ge(res_ok, 8 * u + m + 1)
            dst = acc[:, m, :] if NEXT[u] is None else NEXT[u][0][:, m, :]
            nc.scalar.activation(dst, hT[:, m, :], ACT.Copy, scale=gains[:, u + 1, m:m + 1]).then_inc(next_hi, 1)
            if 8 * u + m >= 2:
                act.wait_ge(sq_used, 8 * u + m - 1)
            nc.scalar.activation(sqT[:, m % 2, :], hT[:, m, :], ACT.Square).then_inc(sq_done, 1)

        def next_dve(dve, u, m):
            if NEXT[u] is None:
                return
            dve.wait_ge(next_hi, 8 * u + m + 1)
            nc.vector.scalar_tensor_tensor(out=NEXT[u][1][:, m, :], in0=hT[:, m, :], scalar=gains[:, u + 1, m:m + 1],
                                           in1=NEXT[u][0][:, m, :].bitcast(F32), op0=ALU.mult, op1=ALU.subtract).then_inc(next_lo, 1)

        def norm_pool(pool, u):
            for m in range(KT):
                pool.wait_ge(sq_done, 8 * u + m + 1)
                if m == 0:
                    if u:
                        pool.wait_ge(n_sum, u)
                    nc.gpsimd.tensor_copy(sqSum[:], sqT[:, 0, :]).then_inc(sq_used, 1)
                else:
                    pool.drain()
                    nc.gpsimd.tensor_tensor(sqSum[:], sqSum[:], sqT[:, m % 2, :], ALU.add).then_inc(sq_used, 1)
            if u == 2 and upto <= 4:
                return
            pool.wait_ge(n_ms, u + 1)
            nc.gpsimd.tensor_tensor(rCol[:], msq[:, 0:NT], minusHalf[:, 0:NT], ALU.pow).then_inc(n_r, 1)

        def norm_pe_sum(pe, u):
            pe.wait_ge(sq_used, 8 * u + 8)
            for t in range(NT):
                last = nc.tensor.matmul(bank[7][:, t:t + 1], sqSum[:, rng(t)], ones[:, 0:1], start=True, stop=True)
            last.then_inc(n_sum, 1)

        def norm_dve(dve, u):
            dve.wait_ge(n_sum, u + 1)
            nc.vector.tensor_scalar(msq[:, 0:NT], bank[7][:, 0:NT], 1.0 / D, EPS, ALU.mult, ALU.add).then_inc(n_ms, 1)
            dve.wait_ge(n_r, u + 1)
            if u == 5:
                return
            nc.vector.tensor_tensor(diag[:], ident[:].unsqueeze(1).to_broadcast([P, NT, P]),
                                    rCol[:].unsqueeze(2).to_broadcast([P, NT, P]), ALU.mult).then_inc(n_diag, 1)

        def norm_pe_bc(pe, u):
            pe.wait_ge(n_diag, u + 1)
            nc.tensor.matmul(bank[7], ones[:], diag[:].rearrange("p t c -> p (t c)"), start=True, stop=True).then_inc(n_bc, 1)

        def norm_act(act, u):
            act.wait_ge(n_bc, u + 1)
            nc.scalar.copy(rBC[:], bank[7]).then_inc(n_ok, 1)

        def panel_tile(slot, k, c):
            return slice(k * 256 + c * P, k * 256 + c * P + P)

        def out_pe(pe, n0, u, X, ready):
            for m in range(KT):
                n = n0 + m // 2
                if m % 2 == 0:
                    pe.wait_ge(panel_lo, n + 1)
                if m >= 2:
                    pe.wait_ge(res_ok, 8 * u + m - 1)
                for k in range(KT):
                    if m == 0:
                        ready(pe, k)
                    c = panel_tile(0, k, m % 2)
                    last = product(bank[4 + m % 2], wH[:, n % 2, c], wL[:, n % 2, c], X[0][:, k, :], X[1][:, k, :], k == 0, k == KT - 1)
                last.then_inc(tile_done, 1)

        def out_act(act, n0, u):
            for m in range(KT):
                if m % 2 == 0 and (m or u):
                    prep_hi(act, n0 + m // 2 + 1, (n0 + m // 2 + 1) % 2)
                next_act(act, u, m)

        def out_dve(dve, n0, u, bias=None):
            for m in range(KT):
                if m % 2 == 0 and (m or u):
                    prep_lo(dve, n0 + m // 2 + 1, (n0 + m // 2 + 1) % 2)
                dve.wait_ge(tile_done, tiles_before(n0) + m + 1)
                if bias is None:
                    nc.vector.tensor_tensor(hT[:, m, :], bank[4 + m % 2], hT[:, m, :], ALU.add).then_inc(res_ok, 1)
                else:
                    nc.vector.scalar_tensor_tensor(out=hT[:, m, :], in0=bank[4 + m % 2], scalar=bias[:, m:m + 1], in1=hT[:, m, :],
                                                   op0=ALU.add, op1=ALU.add).then_inc(res_ok, 1)
                if m:
                    next_dve(dve, u, m - 1)
            next_dve(dve, u, KT - 1)

        def up_pe(pe, i, g, n0, u, X, Y, first):
            for m in range(KT):
                n = n0 + 8 * g + m // 2
                s = (n0 + m // 2) % 2
                if m % 2 == 0:
                    pe.wait_ge(panel_lo, n + 1)
                if m >= 2:
                    pe.wait_ge(hid_f, 8 * (GROUPS * i + g) + m - 1)
                for k in range(KT):
                    if m == 0 and first:
                        pe.wait_ge(next_lo, 8 * u - 8 + k + 1)
                    c = panel_tile(s, k, m % 2)
                    last = product(bank[m % 2], wH[:, s, c], wL[:, s, c], X[0][:, k, :], X[1][:, k, :], k == 0, k == KT - 1)
                last.then_inc(tile_done, 1)

        def down_pe(pe, i, g, n0, u, Y):
            for m in range(KT):
                n = n0 + 8 * g + 4 + m // 2
                s = (n0 + 4 + m // 2) % 2
                if m % 2 == 0:
                    pe.wait_ge(panel_lo, n + 1)
                if m >= 2:
                    pe.wait_ge(down_read, 8 * (GROUPS * i + g) + m - 1)
                for k in range(KT):
                    if m == 0:
                        pe.wait_ge(hid_lo, 8 * (GROUPS * i + g) + k + 1)
                    c = panel_tile(s, k, m % 2)
                    last = product(bank[4 + m % 2], wH[:, s, c], wL[:, s, c], Y[0][:, k, :], Y[1][:, k, :], k == 0, k == KT - 1)
                last.then_inc(tile_done, 1)

        def up_act(act, i, g, n0, Y, extra):
            for m in range(KT):
                if m % 2 == 0:
                    prep_hi(act, n0 + 8 * g + m // 2 + 1, (n0 + m // 2 + 1) % 2, extra)
                act.wait_ge(tile_done, 2 * (n0 + 8 * g) + extra + m + 1)
                if m >= 2:
                    act.wait_ge(hid_lo, 8 * (GROUPS * i + g) + m - 1)
                nc.scalar.activation(hid[:, m % 2, :], bank[m % 2], ACT.Relu).then_inc(hid_f, 1)
                act.drain()
                nc.scalar.activation(Y[0][:, m, :], hid[:, m % 2, :], ACT.Square).then_inc(hid_hi, 1)

        def down_act(act, i, g, n0, u, last, extra):
            for m in range(KT):
                if m % 2 == 0:
                    prep_hi(act, n0 + 8 * g + 4 + m // 2 + 1, (n0 + m // 2 + 1) % 2, extra)
                if last:
                    next_act(act, u, m)

        def up_dve(dve, i, g, n0, Y, extra):
            for m in range(KT):
                if m % 2 == 0:
                    prep_lo(dve, n0 + 8 * g + m // 2 + 1, (n0 + m // 2 + 1) % 2)
                dve.wait_ge(hid_f, 8 * (GROUPS * i + g) + m + 1)
                nc.vector.tensor_tensor(hid2[:, m % 2, :], hid[:, m % 2, :], hid[:, m % 2, :], ALU.mult)
                dve.drain()
                dve.wait_ge(hid_hi, 8 * (GROUPS * i + g) + m + 1)
                nc.vector.tensor_tensor(Y[1][:, m, :], hid2[:, m % 2, :], Y[0][:, m, :].bitcast(F32), ALU.subtract).then_inc(hid_lo, 1)

        def down_dve(dve, i, g, n0, u, last, extra):
            for m in range(KT):
                if m % 2 == 0:
                    prep_lo(dve, n0 + 8 * g + 4 + m // 2 + 1, (n0 + m // 2 + 1) % 2)
                dve.wait_ge(tile_done, 2 * (n0 + 8 * g + 4) + extra + m + 1)
                nc.vector.tensor_tensor(acc[:, m, :], bank[4 + m % 2], acc[:, m, :], ALU.add).then_inc(down_read, 1)
                if last:
                    dve.drain()
                    nc.vector.tensor_tensor(acc[:, m, :], acc[:, m, :], rSq[:], ALU.mult)
                    dve.drain()
                    nc.vector.tensor_tensor(hT[:, m, :], acc[:, m, :], hT[:, m, :], ALU.add).then_inc(res_ok, 1)
                    if m:
                        next_dve(dve, u, m - 1)
            if last:
                next_dve(dve, u, KT - 1)

        acc_zero = sem("acc_zero")

        def mlp_pool(pool, i, u):
            nc.gpsimd.memset(acc[:], 0.0).then_inc(acc_zero, 1)

        def mlp_pe(pe, i, n0, u, X, Y):
            up_pe(pe, i, 0, n0, u, X, Y, True)
            norm_pe_sum(pe, u - 1)
            down_pe(pe, i, 0, n0, u, Y)
            norm_pe_bc(pe, u - 1)
            with pe.Fori(1, GROUPS - 1) as g:
                up_pe(pe, i, g, n0, u, X, Y, False)
                down_pe(pe, i, g, n0, u, Y)
            up_pe(pe, i, GROUPS - 1, n0, u, X, Y, False)
            ple_in_pe(pe, i)
            down_pe(pe, i, GROUPS - 1, n0, u, Y)

        def mlp_act(act, i, n0, u, X, Y):
            extra = tiles_before(n0) - 2 * n0
            up_act(act, i, 0, n0, Y, extra)
            down_act(act, i, 0, n0, u, False, extra)
            norm_act(act, u - 1)
            with act.Fori(1, GROUPS - 1) as g:
                up_act(act, i, g, n0, Y, extra)
                down_act(act, i, g, n0, u, False, extra)
            up_act(act, i, GROUPS - 1, n0, Y, extra)
            ple_in_act(act, i)
            down_act(act, i, GROUPS - 1, n0, u, True, extra)

        def mlp_dve(dve, i, n0, u, X, Y):
            extra = tiles_before(n0) - 2 * n0
            up_dve(dve, i, 0, n0, Y, extra)
            norm_dve(dve, u - 1)
            dve.wait_ge(acc_zero, i + 1)
            down_dve(dve, i, 0, n0, u, False, extra)
            with dve.Fori(1, GROUPS - 1) as g:
                up_dve(dve, i, g, n0, Y, extra)
                down_dve(dve, i, g, n0, u, False, extra)
            up_dve(dve, i, GROUPS - 1, n0, Y, extra)
            ple_in_dve(dve, i)
            dve.wait_ge(n_ok, norms_bc(u - 1))
            nc.vector.tensor_tensor(rSq[:], rBC[:], rBC[:], ALU.mult)
            dve.drain()
            down_dve(dve, i, GROUPS - 1, n0, u, True, extra)

        def norms_bc(u):
            return u + 1

        def mlp_sp(sp, i, n0):
            up, down = mlp_w_up[i], mlp_w_down[i]
            with sp.Fori(0, GROUPS) as g:
                for j in range(4):
                    n = n0 + 8 * g + j
                    sp.wait_ge(panel_lo, n - 1)
                    v = up[:, bass.ds(g * D + 256 * j, 256)].rearrange("(k p) n -> p k n", p=P)
                    for q in range(2):
                        sp.dma_start(wRaw[:, (n0 + j) % 2, :].rearrange("p (k n) -> p k n", k=KT)[:, 4 * q:4 * q + 4, :],
                                     v[:, 4 * q:4 * q + 4, :]).then_inc(panel_in[(n0 + j) % 2], PANEL_INC // 2)
                for j in range(4):
                    n = n0 + 8 * g + 4 + j
                    sp.wait_ge(panel_lo, n - 1)
                    for q in range(2):
                        v = down[bass.ds(g * D + q * S, S), 256 * j:256 * j + 256].rearrange("(k p) n -> p k n", p=P)
                        sp.dma_start(wRaw[:, (n0 + j) % 2, :].rearrange("p (k n) -> p k n", k=KT)[:, 4 * q:4 * q + 4, :],
                                     v).then_inc(panel_in[(n0 + j) % 2], PANEL_INC // 2)

        def ple_load(sp, i):
            sp.dma_start(pTok[:], p[i, 0].rearrange("(t p) c -> p t c", p=P)).then_inc(p_in, 16)

        def ple_in_pe(pe, i):
            pe.wait_ge(p_in, 16 * (i + 1))
            for c in range(2):
                for t in range(NT):
                    last = nc.tensor.transpose(bank[2 + c][:, rng(t)], pTok[:, t, rng(c)], ident[:])
                last.then_inc(ptr_done, 1)

        def ple_in_act(act, i):
            for c in range(2):
                act.wait_ge(ptr_done, 2 * i + c + 1)
                nc.scalar.copy(pH[:, c, :], bank[2 + c]).then_inc(p_hi, 1)

        def ple_in_dve(dve, i):
            for c in range(2):
                dve.wait_ge(p_hi, 2 * i + c + 1)
                nc.vector.tensor_tensor(pL[:, c, :], bank[2 + c], pH[:, c, :].bitcast(F32), ALU.subtract).then_inc(p_lo, 1)

        def ple_pe(pe, i, n0, u, X):
            pe.wait_ge(panel_lo, n0 + 1)
            pe.wait_ge(p_lo, 2 * i + 2)
            for m in range(KT):
                if m >= 2:
                    pe.wait_ge(ple_ok, 8 * i + m - 1)
                for k in range(2):
                    c = slice(k * D + m * P, k * D + m * P + P)
                    last = product(bank[m % 2], wH[:, n0 % 2, c], wL[:, n0 % 2, c], pH[:, k, :], pL[:, k, :], k == 0, k == 1)
                last.then_inc(tile_done, 1)
            norm_pe_sum(pe, u - 1)
            for m in range(KT):
                n = n0 + 1 + m // 2
                if m % 2 == 0:
                    pe.wait_ge(panel_lo, n + 1)
                if m >= 2:
                    pe.wait_ge(gate_in, 8 * i + m - 1)
                for k in range(KT):
                    if m == 0:
                        pe.wait_ge(next_lo, 8 * u - 8 + k + 1)
                    c = panel_tile(0, k, m % 2)
                    last = product(bank[2 + m % 2], wH[:, n % 2, c], wL[:, n % 2, c], X[0][:, k, :], X[1][:, k, :], k == 0, k == KT - 1)
                last.then_inc(tile_done, 1)
                if m == 0:
                    norm_pe_bc(pe, u - 1)

        def ple_act(act, i, n0, u):
            prep_hi(act, n0 + 1, (n0 + 1) % 2)
            for m in range(KT):
                act.wait_ge(tile_done, tiles_before(n0) + m + 1)
                nc.scalar.copy(pleT[:, m, :], bank[m % 2]).then_inc(ple_ok, 1)
            norm_act(act, u - 1)
            for m in range(KT):
                if m % 2 == 0:
                    prep_hi(act, n0 + 2 + m // 2, (n0 + 2 + m // 2) % 2)
                act.wait_ge(gate_in, 8 * i + m + 1)
                nc.scalar.activation(gB2[:, m % 2, :], gA2[:, m % 2, :], ACT.Tanh, scale=0.5).then_inc(gate_th, 1)
                if m:
                    next_act(act, u, m - 1)
            next_act(act, u, KT - 1)

        def ple_dve(dve, i, n0, u):
            prep_lo(dve, n0 + 1, (n0 + 1) % 2)
            norm_dve(dve, u - 1)

            def finish(m):
                dve.wait_ge(gate_th, 8 * i + m + 1)
                dve.wait_ge(ple_ok, 8 * i + m + 1)
                nc.vector.scalar_tensor_tensor(out=pleT[:, m, :], in0=gB2[:, m % 2, :], scalar=1.0, in1=pleT[:, m, :],
                                               op0=ALU.add, op1=ALU.mult)
                dve.drain()
                nc.vector.scalar_tensor_tensor(out=hT[:, m, :], in0=pleT[:, m, :], scalar=0.5, in1=hT[:, m, :],
                                               op0=ALU.mult, op1=ALU.add).then_inc(res_ok, 1)
            for m in range(KT):
                if m % 2 == 0:
                    prep_lo(dve, n0 + 2 + m // 2, (n0 + 2 + m // 2) % 2)
                dve.wait_ge(tile_done, tiles_before(n0 + 1) + m + 1)
                if m == 0:
                    dve.wait_ge(n_ok, norms_bc(u - 1))
                nc.vector.tensor_tensor(gA2[:, m % 2, :], bank[2 + m % 2], rBC[:], ALU.mult).then_inc(gate_in, 1)
                if m:
                    finish(m - 1)
                    if m > 1:
                        next_dve(dve, u, m - 2)
            finish(KT - 1)
            next_dve(dve, u, KT - 2)
            next_dve(dve, u, KT - 1)

        def ple_sp(sp, i, n0):
            v = ple_w_proj[i].rearrange("(k p) n -> p k n", p=P)
            dst = wRaw[:, n0 % 2, :].rearrange("p (k n) -> p k n", k=2)
            sp.wait_ge(panel_lo, n0 - 1)
            for q in range(2):
                sp.dma_start(dst[:, q, :], v[:, q, :]).then_inc(panel_in[n0 % 2], PANEL_INC // 2)
            for j in range(4):
                sp.wait_ge(panel_lo, n0 + j)
                load_square(sp, n0 + 1 + j, square_panel(ple_w_gate[i], 0, 256 * j))

        late = [acc, pleT]
        mlp_mem.close()
        qkHi, qkLo = aH[:, 0:2, :], aH[:, 2:4, :]
        qS = sb("qS", [P, GRP, KVH, S], F32R)
        kSH, kSL = sb("kSH", [P, KVH, S], F32R), sb("kSL", [P, KVH, S], F32R)
        vT = pleT[:, 0:2, :].rearrange("p a b -> p (a b)").rearrange("p (t c) -> p t c", t=NT)
        probs = [acc[:, 2 * i:2 * i + 2, :].rearrange("p a b -> p (a b)").rearrange("p (j k) -> p j k", j=GRP) for i in range(2)]
        probsT = acc[:, 4:6, :]
        t1, t2, rot = pleT[:, 2, :], pleT[:, 3, :], [pleT[:, 4 + i, :] for i in range(4)]
        mx = sb("mx", [P, 6, GRP])

        qk_t = sem("qk_t"); qk_m = sem("qk_m"); qk_r = sem("qk_r"); qk_hi = sem("qk_hi"); qk_lo = sem("qk_lo")
        qk_moved = [sem("qk_moved0"), sem("qk_moved1")]
        v_ok = sem("v_ok")
        sc_done = sem("sc_done")
        sc_read = sem("sc_read")
        mx_ok = sem("mx_ok"); ex_ok = sem("ex_ok"); pr_ok = sem("pr_ok")
        ptr2_done = sem("ptr2_done"); pt_ok = sem("pt_ok"); pt_ok2 = sem("pt_ok2")
        pv_done = sem("pv_done"); o_hi = sem("o_hi"); o_lo = sem("o_lo")
        pz_ok = sem("pz_ok")
        ATB = NT * KVH

        def load_rotary(sp, j):
            n = N_SW + j
            v = sw_w_in[0][:, 0:D].rearrange("(k p) (g j c) -> k p j g c", p=P, g=KVH, j=GRP)
            dst = wRaw[:, n % 2, :].rearrange("p (k g c) -> p k g c", k=KT, g=KVH)
            for k in range(KT):
                sp.dma_start(dst[:, k], v[k][:, j]).then_inc(panel_in[n % 2], PANEL_INC // KT)

        def load_mixer_out(sp, j):
            n = N_SWOUT + j
            dst = wRaw[:, n % 2, :].rearrange("p (a j n) -> p a j n", a=2, j=GRP)
            src = sw_w_out[0][:, 256 * j:256 * j + 256].rearrange("(a r j d) n -> a r d j n", a=2, r=2, j=GRP)
            for a in range(2):
                for r in range(2):
                    sp.dma_start(dst[r * HD:(r + 1) * HD, a], src[a, r]).then_inc(panel_in[n % 2], PANEL_INC // 4)

        def stack(sp, j):
            for f in range(2):
                sp.wait_ge(qk_lo, 2 * j + f + 1)
                for i, part in enumerate((qkHi, qkLo)):
                    for g in range(KVH):
                        src = part[g * HALF:(g + 1) * HALF, f, :].bitcast(F32)
                        if j < GRP:
                            r = 2 * i + f
                            sp.dma_start(qS[r * HALF:(r + 1) * HALF, j, g, :].bitcast(F32), src).then_inc(qk_moved[f], 16)
                        else:
                            for r in (f, 2 + f):
                                sp.dma_start((kSH, kSL)[i][r * HALF:(r + 1) * HALF, g, :].bitcast(F32), src).then_inc(qk_moved[f], 16)

        def att_sp(sp):
            for j in range(GRP + 6):
                sp.wait_ge(panel_lo, N_SW + j - 1)
                if j < GRP:
                    load_rotary(sp, j)
                elif j < GRP + 2:
                    load_square(sp, N_SW + j, square_panel(sw_w_in[0], 0, D + 256 * (j - GRP)))
                else:
                    load_mixer_out(sp, j - GRP - 2)
                if 2 <= j < GRP + 3:
                    stack(sp, j - 2)

        def att_pe(pe, u, X):
            n0 = N_SW
            for j in range(GRP + 1):
                n = n0 + j
                pe.wait_ge(panel_lo, n + 1)
                for f in range(2):
                    if j:
                        pe.wait_ge(qk_t, 2 * j - 1 + f)
                    for k in range(KT):
                        if j == 0 and f == 0:
                            pe.wait_ge(next_lo, 8 * u - 8 + k + 1)
                        wv = [w[:, n % 2, panel_tile(0, k, f)] for w in (wH, wL)]
                        last = product(bank[f], wv[0], wv[1], X[0][:, k, :], X[1][:, k, :], k == 0, k == KT - 1)
                    last.then_inc(tile_done, 1)
                    if j == 0 and f == 0:
                        norm_pe_sum(pe, u - 1)
                if j == 0:
                    norm_pe_bc(pe, u - 1)
            n = n0 + GRP + 1
            pe.wait_ge(panel_lo, n + 1)
            for t in range(NT):
                for k in range(KT):
                    w = [w_[:, n % 2, k * 256:(k + 1) * 256] for w_ in (wH, wL)]
                    o = bank[2 + t // 2][:, (t % 2) * 256:(t % 2) * 256 + 256]
                    nc.tensor.matmul(o, X[0][:, k, rng(t)], w[0], start=(k == 0), stop=False)
                    nc.tensor.matmul(o, X[1][:, k, rng(t)], w[0], start=False, stop=False)
                    last = nc.tensor.matmul(o, X[0][:, k, rng(t)], w[1], start=False, stop=(k == KT - 1))
                if t % 2:
                    last.then_inc(tile_done, 1)
            for f in range(2):
                pe.wait_ge(qk_moved[f], 16 * (8 * GRP + 16))
            pe.wait_ge(v_ok, NT)

            def scores(i):
                t, g = i // KVH, i % KVH
                if i >= 2:
                    pe.wait_ge(sc_read, i - 1)
                for j in range(GRP):
                    c0, k0 = (0, (t - 1) * P) if t else (P, 0)
                    o = psum[:, 2 * (i % 2) + j // 2, (j % 2) * 256 + c0:(j % 2) * 256 + 256]
                    nc.tensor.matmul(o, qS[:, j, g, rng(t)], kSH[:, g, k0:(t + 1) * P], start=True, stop=False)
                    last = nc.tensor.matmul(o, qS[:, j, g, rng(t)], kSL[:, g, k0:(t + 1) * P], start=False, stop=True)
                last.then_inc(sc_done, 1)
            scores(0)
            for i in range(ATB):
                t, g = i // KVH, i % KVH
                if i + 1 < ATB:
                    scores(i + 1)
                pe.wait_ge(pr_ok, i + 1)
                for kt in range(2):
                    if t == 0 and kt == 0:
                        continue
                    if i:
                        pe.wait_ge(pt_ok if kt == 0 else pt_ok2, i - KVH if kt == 0 else i) if (kt or i > KVH) else None
                    for j in range(GRP):
                        last = nc.tensor.transpose(bank[4 + kt][:, rng(j)], probs[i % 2][:, j, rng(kt)], ident[:])
                    last.then_inc(ptr2_done, 1)
                pe.wait_ge(pt_ok2, i + 1)
                if t:
                    pe.wait_ge(pt_ok, i - KVH + 1)
                if g % 2 == 0 and i >= 2:
                    pe.wait_ge(o_lo, i // 2) if g % 2 == 0 and i >= 2 else None
                o = bank[6][(g % 2) * HD:(g % 2 + 1) * HD]
                if t:
                    nc.tensor.matmul(o, vT[:, t - 1, g * HD:(g + 1) * HD], probsT[:, 0, :], start=True, stop=False)
                nc.tensor.matmul(o, vT[:, t, g * HD:(g + 1) * HD], probsT[:, 1, :], start=(t == 0), stop=True).then_inc(pv_done, 1)

        def att_act(act, u, O):
            n0 = N_SW
            for j in range(GRP + 1):
                prep_hi(act, n0 + j + 1, (n0 + j + 1) % 2)
                if j == 0:
                    norm_act(act, u - 1)
                for f in range(2):
                    act.wait_ge(qk_r, 2 * j + f + 1)
                    if j:
                        act.wait_ge(qk_moved[f], 16 * 8 * j)
                    nc.scalar.copy(qkHi[:, f, :], rot[2 * f]).then_inc(qk_hi, 1)
            prep_hi(act, N_SWOUT, N_SWOUT % 2)
            a_ = nc.scalar
            for i in range(ATB):
                t, g = i // KVH, i % KVH
                act.wait_ge(mx_ok, i + 1)
                if i >= 2:
                    act.wait_ge(ptr2_done, (i - 1) + max(0, i - 1 - KVH))
                elif i == 0:
                    act.wait_ge(pz_ok, 1)
                for j in range(GRP):
                    src = psum[:, 2 * (i % 2) + j // 2, (j % 2) * 256:(j % 2) * 256 + 256]
                    for a in range(2):
                        rows = slice(a * CH, (a + 1) * CH)
                        ks = slice(P if t == 0 and a == 0 else CH + a * CH, 3 * CH + a * CH)
                        last = a_.activation(probs[i % 2][rows, j, ks], src[rows, ks], ACT.Exp, bias=mx[rows, 3, j:j + 1],
                                             scale=SCALE, accum_out=mx[rows, 4, j:j + 1])
                last.then_inc(sc_read, 1)
                a_.activation(mx[:, 5, :], mx[:, 2, :], ACT.Exp).then_inc(ex_ok, 1)
                if t:
                    act.wait_ge(ptr2_done, i + 1 + i - KVH)
                    a_.copy(probsT[:, 0, :], bank[4]).then_inc(pt_ok, 1)
                if g % 2:
                    act.wait_ge(pv_done, i + 1)
                    a = g // 2
                    a_.copy(O[0][:, GRP * a:GRP * a + GRP, rng(t)], bank[6].rearrange("p (j q) -> p j q", j=GRP)).then_inc(o_hi, 1)

        def att_dve(dve, u, O):
            v = nc.vector
            n0 = N_SW
            tt, st = v.tensor_tensor, v.scalar_tensor_tensor
            for j in range(GRP + 1):
                prep_lo(dve, n0 + j + 1, (n0 + j + 1) % 2)
                if j == 0:
                    norm_dve(dve, u - 1)
                dve.drain()
                if j == 0:
                    dve.wait_ge(n_ok, norms_bc(u - 1))
                    dve.wait_ge(rope_ok, 1)
                r0 = R_BQ + 2 * j if j < GRP else R_BK
                for f, tf in enumerate((t1, t2)):
                    dve.wait_ge(tile_done, tiles_before(n0 + j) + f + 1)
                    tt(tf, bank[f], rBC[:], ALU.mult).then_inc(qk_t, 1)
                dve.drain()
                b1, b2 = colsA[:, r0:r0 + 1], colsA[:, r0 + 1:r0 + 2]
                if j:
                    dve.wait_ge(qk_lo, 2 * j)
                st(out=rot[0], in0=t1, scalar=b1, in1=ropeC[:], op0=ALU.add, op1=ALU.mult)
                st(out=rot[1], in0=t2, scalar=b2, in1=ropeS[:], op0=ALU.add, op1=ALU.mult)
                st(out=rot[2], in0=t2, scalar=b2, in1=ropeC[:], op0=ALU.add, op1=ALU.mult)
                st(out=rot[3], in0=t1, scalar=b1, in1=ropeS[:], op0=ALU.add, op1=ALU.mult).then_inc(qk_m, 1)
                dve.drain()
                tt(rot[0], rot[0], rot[1], ALU.subtract).then_inc(qk_r, 1)
                tt(rot[2], rot[2], rot[3], ALU.add).then_inc(qk_r, 1)
                for f in range(2):
                    dve.wait_ge(qk_hi, 2 * j + f + 1)
                    if j:
                        dve.wait_ge(qk_moved[f], 16 * 8 * j)
                    tt(qkLo[:, f, :], rot[2 * f], qkHi[:, f, :].bitcast(F32), ALU.subtract).then_inc(qk_lo, 1)
            prep_lo(dve, N_SWOUT, N_SWOUT % 2)
            for t in range(NT):
                dve.wait_ge(tile_done, tiles_before(n0 + GRP + 1) + t // 2 + 1)
                st(out=vT[:, t, :], in0=bank[2 + t // 2][:, (t % 2) * 256:(t % 2) * 256 + 256], scalar=rCol[:, t:t + 1],
                   in1=vBias[:], op0=ALU.mult, op1=ALU.add).then_inc(v_ok, 1)

            def maxima(i):
                t, g = i // KVH, i % KVH
                dve.wait_ge(sc_done, i + 1)
                src = psum[:, 2 * (i % 2):2 * (i % 2) + 2, :].rearrange("p b (j k) -> p (b j) k", j=2)
                for a in range(2):
                    rows = slice(a * CH, (a + 1) * CH)
                    ks = slice(P if t == 0 and a == 0 else CH + a * CH, 3 * CH + a * CH)
                    v.tensor_reduce(mx[rows, 0, :], src[rows, :, ks], AX, ALU.max)
                dve.drain()
                st(out=mx[:, 1, :], in0=mx[:, 0, :], scalar=SCALE, in1=sinks[:, g, :], op0=ALU.mult, op1=ALU.max)
                dve.drain()
                tt(mx[:, 2, :], sinks[:, g, :], mx[:, 1, :], ALU.subtract)
                v.tensor_scalar(mx[:, 3, :], mx[:, 1, :], -1.0, None, ALU.mult).then_inc(mx_ok, 1)
            for i in range(ATB):
                t, g = i // KVH, i % KVH
                maxima(i)
                dve.wait_ge(ex_ok, i + 1)
                tt(mx[:, 0, :], mx[:, 4, :], mx[:, 5, :], ALU.add)
                dve.drain()
                v.reciprocal(mx[:, 1, :], mx[:, 0, :])
                dve.drain()
                tt(probs[i % 2], probs[i % 2], mx[:, 1, :].unsqueeze(2).to_broadcast([P, GRP, 256]), ALU.mult).then_inc(pr_ok, 1)
                dve.wait_ge(ptr2_done, i + 1 + max(0, i + 1 - KVH))
                v.tensor_copy(probsT[:, 1, :], bank[5]).then_inc(pt_ok2, 1)
                if g % 2:
                    a = g // 2
                    dve.wait_ge(o_hi, i // 2 + 1)
                    tt(O[1][:, GRP * a:GRP * a + GRP, rng(t)], bank[6].rearrange("p (j q) -> p j q", j=GRP),
                       O[0][:, GRP * a:GRP * a + GRP, rng(t)].bitcast(F32), ALU.subtract).then_inc(o_lo, 1)

        def att_pool(pool):
            pool.wait_ge(next_lo, 24)
            for i in range(2):
                nc.gpsimd.memset(probs[i], 0.0)
            pool.drain()
            pool.sem_inc(pz_ok, 1)

        out_v = out[0]
        ftr_done = sem("ftr_done"); fout_ok = sem("fout_ok")

        def final_pe(pe):
            norm_pe_sum(pe, 5)
            for t in range(NT):
                for hf in range(2):
                    i = 2 * t + hf
                    if i >= 4:
                        pe.wait_ge(fout_ok, i - 3)
                    for k in range(4):
                        last = nc.tensor.transpose(bank[i % 4][:, rng(k)], acc[:, 4 * hf + k, rng(t)], ident[:])
                    last.then_inc(ftr_done, 1)

        def final_act(act):
            act.wait_ge(n_r, 6)
            for i in range(2 * NT):
                act.wait_ge(ftr_done, i + 1)
                nc.scalar.activation(pleT[:, i, :], bank[i % 4], ACT.Copy, scale=rCol[:, i // 2:i // 2 + 1]).then_inc(fout_ok, 1)

        def final_sp(sp):
            for t in range(NT):
                sp.wait_ge(fout_ok, 2 * t + 2)
                sp.dma_start(out_v[t * P:(t + 1) * P, :].rearrange("p (a b) -> p a b", a=2), pleT[:, 2 * t:2 * t + 2, :]).then_inc(out_done, 16)
            sp.wait_ge(out_done, 16 * NT)

        out_done = sem("out_done")
        fin_ok = sem("fin_ok")
        block = ctx.enter_context(nc.Block())

        @block.sync
        def _(sp):
            consts_sp(sp)
            dn_sp(sp)
            for m in range(4):
                sp.wait_ge(panel_lo, N_DNOUT + m - 1)
                load_square(sp, N_DNOUT + m, square_panel(dn_w_out[0], 0, 256 * m))
            sp.wait_ge(res_ok, 1)
            ple_load(sp, 0)
            mlp_sp(sp, 0, N_MLP0)
            ple_sp(sp, 0, N_PLE0)
            if upto > 4:
                att_sp(sp)
                ple_load(sp, 1)
                mlp_sp(sp, 1, N_MLP1)
                ple_sp(sp, 1, N_PLE1)
            if upto > 8:
                final_sp(sp)
            if dbg:
                sp.wait_ge(fin_ok, 1)
                sp.dma_start(dbg[0], hT[:]).then_inc(out_done, 16)
                sp.wait_ge(out_done, 16 + (64 if upto > 8 else 0))

        @block.gpsimd
        def _(pool):
            consts_pool(pool)
            first_norm_pool(pool)
            dn_pool(pool)
            norm_pool(pool, 0)
            mlp_pool(pool, 0, 1)
            norm_pool(pool, 1)
            norm_pool(pool, 2)
            if upto > 4:
                att_pool(pool)
                norm_pool(pool, 3)
                mlp_pool(pool, 1, 4)
                norm_pool(pool, 4)
                norm_pool(pool, 5)

        @block.scalar
        def _(act):
            first_norm_act(act)
            first_tr_act(act)
            rope_act(act)
            gates_act(act)
            gates_act2(act)
            for j in range(2):
                prep_hi(act, j, j)
            dn_act(act)
            out_act(act, N_DNOUT, 0)
            mlp_act(act, 0, N_MLP0, 1, X_A, X_B)
            ple_act(act, 0, N_PLE0, 2)
            if upto > 4:
                att_act(act, 3, X_A)
                out_act(act, N_SWOUT, 3)
                mlp_act(act, 1, N_MLP1, 4, X_B, X_A)
                ple_act(act, 1, N_PLE1, 5)
                final_act(act)

        @block.vector
        def _(dve):
            first_norm_dve(dve)
            first_tr_dve(dve)
            rope_dve(dve)
            gates_dve(dve)
            for j in range(2):
                prep_lo(dve, j, j)
            dve.wait_ge(gate_e, 3)
            dn_dve(dve)
            out_dve(dve, N_DNOUT, 0)
            mlp_dve(dve, 0, N_MLP0, 1, X_A, X_B)
            ple_dve(dve, 0, N_PLE0, 2)
            if upto > 4:
                att_dve(dve, 3, X_A)
                out_dve(dve, N_SWOUT, 3, colsA[:, R_BOUT:R_BOUT + KT])
                mlp_dve(dve, 1, N_MLP1, 4, X_B, X_A)
                ple_dve(dve, 1, N_PLE1, 5)
                norm_dve(dve, 5)
            if dbg:
                nc.vector.memset(mx[:], 0.0).then_inc(fin_ok, 1)

        @block.tensor
        def _(pe):
            first_tr_pe(pe)
            rope_pe(pe)
            gates_pe(pe)
            dn_pe(pe)
            out_pe(pe, N_DNOUT, 0, X_B, lambda e, k: e.wait_ge(yl_ok, k + 1))
            mlp_pe(pe, 0, N_MLP0, 1, X_A, X_B)
            ple_pe(pe, 0, N_PLE0, 2, X_A)
            if upto > 4:
                att_pe(pe, 3, X_B)
                out_pe(pe, N_SWOUT, 3, X_A, lambda e, k: e.wait_ge(o_lo, 2 * NT))
                mlp_pe(pe, 1, N_MLP1, 4, X_B, X_A)
                ple_pe(pe, 1, N_PLE1, 5, X_B)
                final_pe(pe)


_INS = ['x', 'p', 'positions', 'norm_mix', 'norm_mlp', 'norm_ple', 'norm_final', 'dn_w_in', 'dn_conv_w', 'dn_a_log',
        'dn_dt_bias', 'dn_norm_w', 'dn_w_out', 'sw_w_in', 'sw_b_in', 'sw_sinks', 'sw_w_out', 'sw_b_out', 'mlp_w_up',
        'mlp_w_down', 'ple_w_proj', 'ple_w_gate']


def kernel(**inputs):
    import numpy as _np
    import concourse.bacc as _bacc
    from concourse import mybir as _mybir
    from concourse.bass_utils import run_bass_kernel_spmd as _run

    nc = _bacc.Bacc("TRN2", target_bir_lowering=False, num_devices=1, dynamic_dma_scratch_size=1024)
    arrays, args = {}, []
    for name in _INS:
        a = _np.ascontiguousarray(inputs[name])
        arrays[f"in_{name}"] = a
        args.append(nc.dram_tensor(f"in_{name}", a.shape, _mybir.dt.from_np(a.dtype), kind="ExternalInput").ap())
    args.append(nc.dram_tensor("out_0", (1, S, D), F32, kind="ExternalOutput").ap())
    hybrid_trunk(nc, *args)
    r = _run(nc, [arrays], core_ids=[0])
    return r.results[0]["out_0"]
```

```python
import math
from contextlib import ExitStack

import numpy as np
import concourse.bass as bass
from concourse import mybir

F32 = mybir.dt.float32
F32R = mybir.dt.float32r
I32 = mybir.dt.int32
ALU = mybir.AluOpType
ACT = mybir.ActivationFunctionType
AX = mybir.AxisListType.X

P = 128
D = 1024
S = 512
KT = D // P
NT = S // P
CH = 64
EPS = 1e-6
HEADS_A = 8
CONV = 4
GATE_COLS = 2 * HEADS_A
HD = 64
KVH = 4
GRP = 4
HALF = HD // 2
FF = 4 * D
GROUPS = 4
PLE = 256
PW = 2 * D
THETA = 10000.0
PANEL_INC = 128
SCALE = HD ** -0.5
TWO_PI = (6.28125, 0.0019350051879882812, 3.019916050561733e-07)


def hybrid_trunk(nc, x, p, positions, norm_mix, norm_mlp, norm_ple, norm_final,
                 dn_w_in, dn_conv_w, dn_a_log, dn_dt_bias, dn_norm_w, dn_w_out,
                 sw_w_in, sw_b_in, sw_sinks, sw_w_out, sw_b_out,
                 mlp_w_up, mlp_w_down, ple_w_proj, ple_w_gate, out):
    ctx = ExitStack()
    with ctx:
        def sb(name, shape, dt=F32):
            return ctx.enter_context(nc.sbuf_tensor(name, shape, dt))

        def sem(name):
            return ctx.enter_context(nc.semaphore(name))

        hT = sb("hT", [P, KT, S])
        aH, aL = sb("aH", [P, KT, S], F32R), sb("aL", [P, KT, S], F32R)
        bH, bL = sb("bH", [P, KT, S], F32R), sb("bL", [P, KT, S], F32R)
        wRaw = sb("wRaw", [P, 2, PW])
        wH, wL = sb("wH", [P, 2, PW], F32R), sb("wL", [P, 2, PW], F32R)
        psum = ctx.enter_context(nc.psum_tensor("psum", [P, 8, S], F32))
        bank = [psum[:, i, :] for i in range(8)]

        ropeC, ropeS = sb("ropeC", [P, S]), sb("ropeS", [P, S])
        ident = sb("ident", [P, P])
        ones = sb("ones", [P, P])
        rBC = sb("rBC", [P, S])
        small = sb("small", [P, 3, NT])
        rCol, msq, minusHalf = small[:, 0, :], small[:, 1, :], small[:, 2, :]
        sqT = sb("sqT", [P, 2, S])
        sqSum = sb("sqSum", [P, S])

        def rng(i):
            return slice(i * P, (i + 1) * P)

        panel_in = [sem("panel_in0"), sem("panel_in1")]
        panel_hi = sem("panel_hi")
        panel_lo = sem("panel_lo")
        tile_done = sem("tile_done")
        const_in = sem("const_in")
        const_ok = sem("const_ok")

        dn_in_v = dn_w_in[0].rearrange("(k p) n -> p k n", p=P)

        def square_panel(w, rows0, cols0):
            v = w[rows0:rows0 + D, cols0:cols0 + 256].rearrange("(k p) n -> p k n", p=P)
            return v

        def load_square(sp, n, view):
            s = n % 2
            dst = wRaw[:, s, :].rearrange("p (k n) -> p k n", k=KT)
            for q in range(2):
                sp.dma_start(dst[:, 4 * q:4 * q + 4, :], view[:, 4 * q:4 * q + 4, :]).then_inc(panel_in[s], PANEL_INC // 2)

        N_DN = 0
        N_DNOUT = N_DN + 2 * HEADS_A
        N_MLP0 = N_DNOUT + 4
        N_PLE0 = N_MLP0 + 8 * GROUPS
        N_SW = N_PLE0 + 5
        N_SWOUT = N_SW + 6
        N_MLP1 = N_SWOUT + 4
        N_PLE1 = N_MLP1 + 8 * GROUPS
        N_END = N_PLE1 + 5

        def tiles_before(n):
            return 2 * n + 6 * (n > N_PLE0) + 6 * (n > N_PLE1)

        def panel_parts(w, slot, n, split):
            v = w[:, slot, :]
            if not (isinstance(n, int) and N_SW <= n <= N_SW + GRP):
                return [v]
            order = "p (k f g c) -> p k f g c" if split else "p (k g f c) -> p k f g c"
            v = v.rearrange(order, k=KT, f=2, g=KVH)
            return [v[:, :, f] for f in range(2)]

        def prep_hi(act, n, slot, extra=0):
            if isinstance(n, int) and n >= N_END:
                return
            act.wait_ge(panel_in[slot], (n - slot) * (PANEL_INC // 2) + PANEL_INC)
            if not (isinstance(n, int) and n < 2):
                act.wait_ge(tile_done, tiles_before(n - 1) if isinstance(n, int) else 2 * n - 2 + extra)
            last = [nc.scalar.copy(o, r) for o, r in zip(panel_parts(wH, slot, n, True), panel_parts(wRaw, slot, n, False))][-1]
            last.then_inc(panel_hi, 1)

        def prep_lo(dve, n, slot, half=None):
            if isinstance(n, int) and n >= N_END:
                return
            dve.wait_ge(panel_hi, n + 1)
            last = [nc.vector.tensor_tensor(o, r, h_.bitcast(F32), ALU.subtract)
                    for o, r, h_ in zip(*([v if half is None else v[:, half * PW // 2:(half + 1) * PW // 2]
                                           for v in panel_parts(w, slot, n, w is not wRaw)] for w in (wL, wRaw, wH)))][-1]
            if half != 0:
                last.then_inc(panel_lo, 1)

        def product(o, wh, wl, xh, xl, first, last):
            nc.tensor.matmul(o, wh, xh, start=first, stop=False)
            nc.tensor.matmul(o, wl, xh, start=False, stop=False)
            return nc.tensor.matmul(o, wh, xl, start=False, stop=last)

        R_NORMW = 7 * KT
        R_BOUT = CONV * 3 * HEADS_A
        R_BQ = R_BOUT + KT
        R_BK = R_BQ + 2 * GRP
        colsA, colsB = sb("colsA", [P, R_NORMW + 1]), sb("colsB", [P, R_BK + 2])
        sinks = sb("sinks", [P, KVH, GRP])
        vBias = sb("vBias", [P, KVH * HD])
        dn_mem = ExitStack()
        dn_mem.__enter__()

        def sbd(name, shape, dt=F32):
            return dn_mem.enter_context(nc.sbuf_tensor(name, shape, dt))
        work = sbd("work", [P, 10, S])
        xTok = [work[:, 2 * t:2 * t + 2, :].rearrange("p a b -> p (a b)") for t in range(NT)]
        x_in = sem("x_in")
        x_ss = sem("x_ss")
        x_ms = sem("x_ms")
        x_r = sem("x_r")
        x_scaled = sem("x_scaled")
        x_tr = sem("x_tr")
        x_raw = sem("x_raw")
        x_hi = sem("x_hi")
        x_lo = sem("x_lo")

        maskIncl = sbd("maskIncl", [P, P])
        maskLow = sbd("maskLow", [P, P])
        maskUp = sbd("maskUp", [P, P])
        maskPair = sbd("maskPair", [P, P])
        LEVELS = [2, 4, 8, 16, 32]
        maskLev = sbd("maskLev", [P, len(LEVELS), P])
        chunkSel = sbd("chunkSel", [P, 2, P])
        inclSw = sbd("inclSw", [P, P])

        gw = sbd("gw", [P, KT, GATE_COLS])
        gwH, gwL = sbd("gwH", [P, KT, GATE_COLS], F32R), sbd("gwL", [P, KT, GATE_COLS], F32R)
        convW = colsB[:, 0:CONV * 3 * HEADS_A].rearrange("p (c k) -> p c k", c=CONV)
        aLog = sbd("aLog", [P, HEADS_A])
        dtB = sbd("dtB", [P, HEADS_A])
        rowsA, rowsB = sbd("rowsA", [P, P]), sbd("rowsB", [P, P])
        normW = colsA[:, R_NORMW:R_NORMW + 1]
        gains = colsA[:, 0:7 * KT].rearrange("p (i k) -> p i k", k=KT)
        rows_zero = sem("rows_zero")
        cols_done = sem("cols_done")
        cols_ok = sem("cols_ok")
        pos_in = sem("pos_in")
        late_in = sem("late_in")
        ident_ok = sem("ident_ok")

        def consts_sp(sp):
            sp.dma_start(posI[:], positions[0].rearrange("(t p) -> p t", p=P), allow_slow_non_contiguous=True).then_inc(pos_in, 16)
            for t in range(NT):
                sp.dma_start(xTok[t], x[0, t * P:(t + 1) * P, :]).then_inc(x_in, 16)
            sp.wait_ge(rows_zero, 1)
            for i, g in enumerate((norm_mix[0], norm_mlp[0], norm_ple[0], norm_mix[1], norm_mlp[1], norm_ple[1], norm_final)):
                sp.dma_start(rowsA[i * KT:(i + 1) * KT, :], g.rearrange("(k p) -> k p", p=P)).then_inc(const_in, 16)
            sp.dma_start(rowsA[R_NORMW:R_NORMW + 1, :], dn_norm_w[0:1, :]).then_inc(const_in, 16)
            sp.dma_start(gw[:], dn_in_v[:, :, 4 * D:4 * D + GATE_COLS]).then_inc(const_in, 16)
            sp.dma_start(aLog[:], dn_a_log[0:1, :].to_broadcast([P, HEADS_A])).then_inc(const_in, 16)
            sp.dma_start(dtB[:], dn_dt_bias[0:1, :].to_broadcast([P, HEADS_A])).then_inc(const_in, 16)
            for j in range(2):
                load_dn(sp, 0, j)
            sp.dma_start(rowsB[0:R_BOUT, :], dn_conv_w[0].rearrange("c (k p) -> (c k) p", p=P)).then_inc(late_in, 16)
            sp.dma_start(rowsB[R_BOUT:R_BOUT + KT, :], sw_b_out[0].rearrange("(k p) -> k p", p=P)).then_inc(late_in, 16)
            for j in range(GRP):
                for f in range(2):
                    src = sw_b_in[0, 0:D].rearrange("(g j f i) -> j f g i", g=KVH, j=GRP, f=2)[j:j + 1, f]
                    sp.dma_start(rowsB[R_BQ + 2 * j + f:R_BQ + 2 * j + f + 1, :].rearrange("o (g i) -> o g i", g=KVH), src).then_inc(late_in, 16)
            for f in range(2):
                src = sw_b_in[0, D:D + KVH * HD].rearrange("(o g f i) -> o f g i", o=1, g=KVH, f=2)[:, f]
                sp.dma_start(rowsB[R_BK + f:R_BK + f + 1, :].rearrange("o (g i) -> o g i", g=KVH), src).then_inc(late_in, 16)
            sp.dma_start(sinks[:].rearrange("p g j -> p (g j)"), sw_sinks[0:1, :].to_broadcast([P, KVH * GRP])).then_inc(late_in, 16)
            sp.dma_start(vBias[:], sw_b_in[0:1, D + KVH * HD:].to_broadcast([P, KVH * HD])).then_inc(late_in, 16)
        N_CONST = 16 * (7 + 1 + 3)
        N_LATE = 16 * (2 + 2 * GRP + 2 + 2)

        posI = sbd("posI", [P, NT], I32)
        posF = sbd("posF", [P, NT])
        freq = sbd("freq", [P, HALF])
        ang = sbd("ang", [P, 2, NT, HALF])
        turn = sbd("turn", [P, 2, NT, HALF])
        trig = sbd("trig", [P, 2, NT, P])
        freq_ok = sem("freq_ok")
        ang_ok = sem("ang_ok")
        trig_ok = sem("trig_ok")
        trig_done = sem("trig_done")
        rope_ok = sem("rope_ok")

        def rope_dve(dve):
            v = nc.vector
            dve.wait_ge(freq_ok, 1)
            dve.wait_ge(pos_in, 16)
            v.tensor_copy(posF[:], posI[:])
            dve.drain()
            for s_ in range(2):
                v.tensor_tensor(ang[:, s_], posF[:].unsqueeze(2).to_broadcast([P, NT, HALF]),
                                freq[:].unsqueeze(1).to_broadcast([P, NT, HALF]), ALU.mult)
            dve.drain()
            big = 1.5 * 2 ** 23
            for s_ in range(2):
                v.tensor_scalar(turn[:, s_], ang[:, s_], 1.0 / (2 * math.pi), 0.25 * (1 - s_), ALU.mult, ALU.add)
            dve.drain()
            v.tensor_scalar(turn[:], turn[:], big, None, ALU.add)
            dve.drain()
            v.tensor_scalar(turn[:], turn[:], big, None, ALU.subtract)
            dve.drain()
            for part in TWO_PI:
                v.scalar_tensor_tensor(out=ang[:], in0=turn[:], scalar=-part, in1=ang[:], op0=ALU.mult, op1=ALU.add)
                dve.drain()
            v.tensor_scalar(ang[:, 0], ang[:, 0], math.pi / 2, None, ALU.add)
            dve.drain()
            v.tensor_scalar(ang[:], ang[:], 3.1415925, -3.1415925, ALU.min, ALU.max).then_inc(ang_ok, 1)

        def rope_act(act):
            act.wait_ge(ang_ok, 1)
            for g in range(KVH):
                last = nc.scalar.activation(trig[:, :, :, g * HALF:(g + 1) * HALF], ang[:], ACT.Sin)
            last.then_inc(trig_ok, 1)

        def rope_act2(act):
            act.wait_ge(trig_done, 1)
            nc.scalar.copy(ropeC[:], bank[6])
            nc.scalar.copy(ropeS[:], bank[7]).then_inc(rope_ok, 1)

        def rope_pe(pe):
            pe.wait_ge(ident_ok, 1)
            pe.wait_ge(trig_ok, 1)
            for s_ in range(2):
                for t in range(NT):
                    last = nc.tensor.transpose(bank[6 + s_][:, rng(t)], trig[:, s_, t, :], ident[:])
            last.then_inc(trig_done, 1)


        def consts_pool(pool):
            g = nc.gpsimd

            def keep(view, base, pattern, cm):
                g.affine_select(out=view, in_=view, compare_op=ALU.is_ge, fill=0.0, base=base,
                                pattern=pattern, channel_multiplier=cm)
                pool.drain()
            g.memset(ident[:], 1.0)
            g.memset(rowsB[:], 0.0)
            g.memset(rowsA[:], 0.0)
            pool.drain()
            pool.sem_inc(rows_zero, 1)
            keep(ident[:], 0, [[-1, P]], 1)
            keep(ident[:], 0, [[1, P]], -1)
            pool.sem_inc(ident_ok, 1)
            for i in range(HALF):
                g.memset(freq[:, i:i + 1], float(np.float32(THETA) ** (-np.float32(2 * i) / np.float32(HD))))
            g.memset(ones[:], 1.0).then_inc(freq_ok, 1)
            for m in (maskIncl, maskLow, maskUp, maskPair, maskLev, chunkSel, inclSw):
                g.memset(m[:], 1.0)
            g.memset(minusHalf, -0.5)
            pool.drain()
            for m, base, st, cm in ((maskIncl, 0, 1, -1), (maskLow, -1, -1, 1), (maskUp, -1, 1, -1)):
                v = m[:].rearrange("p (a b) -> p a b", a=2)
                keep(v, base, [[CH * st, 2], [st, CH]], cm)
                keep(v, 0, [[-CH, 2], [0, CH]], 1)
                keep(v, CH - 1, [[CH, 2], [0, CH]], -1)
            first_norm_pool(pool)
            v = inclSw[:].rearrange("p (a b) -> p a b", a=2)
            keep(v, CH, [[-CH, 2], [1, CH]], -1)
            keep(v, -CH, [[CH, 2], [0, CH]], 1)
            keep(v, 2 * CH - 1, [[-CH, 2], [0, CH]], -1)
            keep(chunkSel[:, 0, :], CH - 1, [[0, P]], -1)
            keep(chunkSel[:, 1, :], -CH, [[0, P]], 1)
            pool.sem_inc(const_ok, 1)
            v = maskPair[:].rearrange("p (a b) -> p a b", b=2)
            keep(v, 0, [[-2, CH], [0, 2]], 1)
            keep(v, 0, [[2, CH], [0, 2]], -1)
            keep(v, -1, [[0, CH], [1, 2]], 0)
            for i, b in enumerate(LEVELS):
                n = P // (2 * b)
                v = maskLev[:, i, :].rearrange("p (a b) -> p a b", b=2 * b)
                keep(v, -b, [[-2 * b, n], [0, 2 * b]], 1)
                keep(v, 2 * b - 1, [[2 * b, n], [0, 2 * b]], -1)
                keep(v, b - 1, [[0, n], [-1, 2 * b]], 0)

        ssq = sbd("ssq", [P, NT])
        xScaled = sbd("xScaled", [P, NT, D])

        def first_norm_act(act):
            act.wait_ge(x_in, 16 * NT)
            for t in range(NT):
                nc.scalar.activation(xScaled[:, t, :], xTok[t], ACT.Square, accum_out=ssq[:, t:t + 1]).then_inc(x_ss, 1)

        def scale_act(act):
            act.wait_ge(x_r, 1)
            for t in range(NT):
                nc.scalar.activation(xScaled[:, t, :], xTok[t], ACT.Copy, scale=rCol[:, t:t + 1]).then_inc(x_scaled, 1)

        def first_norm_dve(dve):
            dve.wait_ge(x_ss, NT)
            nc.vector.tensor_scalar(msq[:, 0:NT], ssq[:], 1.0 / D, EPS, ALU.mult, ALU.add).then_inc(x_ms, 1)

        def first_norm_pool(pool):
            pool.wait_ge(x_ms, 1)
            nc.gpsimd.tensor_tensor(rCol, msq[:, 0:NT], minusHalf[:, 0:NT], ALU.pow).then_inc(x_r, 1)

        XB = (2, 3, 0, 1)

        def first_tr_pe(pe):
            pe.wait_ge(ident_ok, 1)
            pe.wait_ge(x_in, 16 * NT)
            for k in range(KT):
                b = k % 2
                if k >= 2:
                    pe.wait_ge(x_raw, k - 1)
                for t in range(NT):
                    last = nc.tensor.transpose(bank[b][:, rng(t)], xTok[t][:, rng(k)], ident[:])
                last.then_inc(x_tr, 1)
            pe.wait_ge(const_in, N_CONST)
            nc.tensor.transpose(bank[4][:, 0:P], rowsA[:], ident[:]).then_inc(cols_done, 1)
            pe.wait_ge(x_scaled, NT)
            for k in range(KT):
                b = XB[k % 4]
                if k == 2:
                    pe.wait_ge(x_raw, KT)
                if k >= 4:
                    pe.wait_ge(x_lo, k - 3)
                for t in range(NT):
                    last = nc.tensor.transpose(bank[b][:, rng(t)], xScaled[:, t, rng(k)], ident[:])
                last.then_inc(x_tr, 1)

        def first_tr_act(act):
            act.wait_ge(cols_done, 1)
            nc.scalar.copy(colsA[:], bank[4][:, 0:R_NORMW + 1]).then_inc(cols_ok, 1)
            act.drain()
            for k in range(KT):
                act.wait_ge(x_tr, KT + k + 1)
                nc.scalar.activation(aH[:, k, :], bank[XB[k % 4]], ACT.Copy, scale=gains[:, 0, k:k + 1]).then_inc(x_hi, 1)

        def raw_dve(dve, k0, k1):
            for k in range(k0, k1):
                dve.wait_ge(x_tr, k + 1)
                nc.vector.tensor_copy(hT[:, k, :], bank[k % 2]).then_inc(x_raw, 1)

        def first_tr_dve(dve):
            dve.wait_ge(cols_ok, 1)
            for k in range(KT):
                dve.wait_ge(x_hi, k + 1)
                nc.vector.scalar_tensor_tensor(out=aL[:, k, :], in0=bank[XB[k % 4]], scalar=gains[:, 0, k:k + 1],
                                               in1=aH[:, k, :].bitcast(F32), op0=ALU.mult, op1=ALU.subtract).then_inc(x_lo, 1)

        G_, B_, NB_, EG_, EGS_, ED_, EL0_, EL1_ = range(8)
        gate = sbd("gate", [P, HEADS_A, 8, NT])
        hc = sbd("hc", [P, 2, 8, NT])
        gt = sbd("gt", [P, 8, HEADS_A, NT])
        gw_hi = sem("gw_hi")
        gw_lo = sem("gw_lo")
        gate_raw = sem("gate_raw")
        gate_e = sem("gate_e")
        gate_v = sem("gate_v")
        gate_cum = sem("gate_cum")
        gateT_done = sem("gateT_done")
        gateT_ok = sem("gateT_ok")
        logits = bank[6][:, 0:NT * GATE_COLS].rearrange("p (t c) -> p t c", t=NT)
        cums = bank[5][:, 0:5 * HEADS_A * NT].rearrange("p (q h t) -> p q h t", q=5, h=HEADS_A)

        def gates_act(act):
            act.wait_ge(const_in, N_CONST)
            nc.scalar.copy(gwH[:], gw[:]).then_inc(gw_hi, 1)

        def gates_act2(act):
            act.wait_ge(gateT_done, 1)
            nc.scalar.copy(kHatT[0:GATE_COLS, :], bank[4][0:GATE_COLS, :]).then_inc(gateT_ok, 1)
            prep_hi(act, 1, 1)
            act.wait_ge(cols_done, 2)
            nc.scalar.copy(colsB[:], bank[7][:, 0:R_BK + 2]).then_inc(cols_ok, 1)
            act.drain()
            act.wait_ge(gate_v, 1)
            nc.scalar.activation(gt[:, 1], gt[:, 0], ACT.Abs).then_inc(gate_e, 1)
            nc.scalar.activation(gt[:, 7, :, 0], aLog[:], ACT.Exp)
            act.drain()
            nc.scalar.activation(gt[:, 2], gt[:, 1], ACT.Exp, scale=-1.0)
            act.wait_ge(gate_v, 2)
            nc.scalar.activation(gt[:, 3], gt[:, 3], ACT.Tanh, scale=0.5).then_inc(gate_e, 1)

        def gates_act3(act):
            act.wait_ge(gate_cum, 1)
            nc.scalar.activation(gate[:, :, EG_:EL1_ + 1, :].rearrange("p h q t -> p q h t"), cums, ACT.Exp).then_inc(gate_e, 1)

        def gates_dve(dve):
            v = nc.vector
            dve.wait_ge(gw_hi, 1)
            v.tensor_tensor(gwL[:], gw[:], gwH[:].bitcast(F32), ALU.subtract).then_inc(gw_lo, 1)

        def gates_dve2(dve):
            v = nc.vector
            dve.wait_ge(gate_raw, 1)
            dve.wait_ge(const_in, N_CONST)
            v.tensor_tensor(gt[:, 0], logits[:, :, HEADS_A:].rearrange("p t h -> p h t"),
                            dtB[:].unsqueeze(2).to_broadcast([P, HEADS_A, NT]), ALU.add).then_inc(gate_v, 1)
            v.tensor_copy(gt[:, 3], logits[:, :, 0:HEADS_A].rearrange("p t h -> p h t")).then_inc(gate_v, 1)
            dve.wait_ge(gate_e, 2)
            v.tensor_scalar(gt[:, 4], gt[:, 2], 2.0, None, ALU.add)
            dve.drain()
            v.reciprocal(gt[:, 4], gt[:, 4])
            dve.drain()
            v.tensor_tensor(gt[:, 5], gt[:, 4], gt[:, 2], ALU.mult)
            dve.drain()
            v.tensor_tensor(gt[:, 6], gt[:, 5], gt[:, 5], ALU.mult)
            dve.drain()
            v.tensor_scalar(gt[:, 4], gt[:, 6], 1.0 / 19, None, ALU.mult)
            for n in (17, 15, 13, 11, 9, 7, 5, 3):
                dve.drain()
                v.scalar_tensor_tensor(out=gt[:, 4], in0=gt[:, 4], scalar=1.0 / n, in1=gt[:, 6], op0=ALU.add, op1=ALU.mult)
            dve.drain()
            v.scalar_tensor_tensor(out=gt[:, 4], in0=gt[:, 4], scalar=1.0, in1=gt[:, 5], op0=ALU.add, op1=ALU.mult)
            v.tensor_scalar(gt[:, 0], gt[:, 0], 0.0, None, ALU.max)
            dve.drain()
            v.scalar_tensor_tensor(out=gt[:, 4], in0=gt[:, 4], scalar=2.0, in1=gt[:, 0], op0=ALU.mult, op1=ALU.add)
            dve.drain()
            v.scalar_tensor_tensor(out=gate[:, :, G_, :], in0=gt[:, 4], scalar=-1.0,
                                   in1=gt[:, 7, :, 0:1].to_broadcast([P, HEADS_A, NT]), op0=ALU.mult, op1=ALU.mult)
            v.tensor_scalar(gate[:, :, B_, :], gt[:, 3], 1.0, 0.5, ALU.add, ALU.mult)
            dve.drain()
            v.tensor_scalar(gate[:, :, NB_, :], gate[:, :, B_, :], -1.0, None, ALU.mult)
            v.tensor_copy(gt[:, 5], gate[:, :, G_, :]).then_inc(gate_v, 1)

        def gates_pe(pe):
            pe.wait_ge(gw_lo, 1)
            pe.wait_ge(x_lo, KT)
            for k in range(KT):
                last = product(bank[4][0:GATE_COLS, :], gwH[:, k, :], gwL[:, k, :], aH[:, k, :], aL[:, k, :], k == 0, k == KT - 1)
            last.then_inc(gateT_done, 1)

        def gates_pe2(pe):
            pe.wait_ge(rope_ok, 1)
            pe.wait_ge(late_in, N_LATE)
            nc.tensor.transpose(bank[7][:, 0:P], rowsB[:], ident[:]).then_inc(cols_done, 1)
            pe.wait_ge(gateT_ok, 1)
            for t in range(NT):
                last = nc.tensor.transpose(logits[:, t, :], kHatT[0:GATE_COLS, rng(t)], ident[0:GATE_COLS, 0:GATE_COLS])
            last.then_inc(gate_raw, 1)

        def gates_pe3(pe):
            pe.wait_ge(const_ok, 1)
            pe.wait_ge(gate_v, 3)
            g = gt[:, 5].rearrange("p h t -> p (h t)")
            for i, m in enumerate((maskIncl[:], inclSw[:], maskLow[:], chunkSel[:, 0, :], chunkSel[:, 1, :])):
                last = nc.tensor.matmul(cums[:, i].rearrange("p h t -> p (h t)"), m, g, start=True, stop=True)
            last.then_inc(gate_cum, 1)

        def t4(buf):
            return buf.rearrange("p (t c) -> p t c", t=NT)
        qF, kF, vF, tanhT = (work[:, i, :] for i in range(4))
        gA, decT, lowT, kEg = (t4(work[:, i, :]) for i in range(4, 8))
        attT = [t4(work[:, 8 + i, :]) for i in range(2)]
        sq2 = xScaled[:, 0, :].rearrange("p (a b) -> p a b", a=2)
        betaUp, inv = t4(xScaled[:, 1, 0:S]), t4(xScaled[:, 1, S:])
        invT, tMask = t4(xScaled[:, 2, 0:S]), t4(xScaled[:, 2, S:])
        qw = [q.rearrange("p (t r c) -> p t r c", t=NT, r=2) for q in (xScaled[:, 3, :], sqT[:].rearrange("p a b -> p (a b)"))]
        taps = sbd("taps", [P, CONV, S])
        kTok, vTok = sbd("kTok", [P, NT, P]), sbd("vTok", [P, NT, P])
        kDec = [trig[:, i] for i in range(2)]
        uB = sbd("uB", [P, 2, NT, P])
        kHatT = sbd("kHatT", [P, S])
        vNew = sbd("vNew", [P, P])
        state = sbd("state", [P, P])
        oTok = sbd("oTok", [P, NT, P])
        yF = sbd("yF", [P, S])
        oSq = t4(yF[:])
        st8 = sbd("st8", [P, 8])
        rs8 = sbd("rs8", [P, 2, 8])
        os4 = sbd("os4", [P, 4, NT])

        zF = [rBC[:], sqSum[:]]
        oq_ok = sem("oq_ok")
        taps_ok = sem("taps_ok")
        conv_ok = sem("conv_ok")
        tanh_ok = sem("tanh_ok")
        feat_ok = sem("feat_ok")
        sq_ok = sem("sq_ok")
        nrm_done = sem("nrm_done")
        ktr_done = sem("ktr_done")
        vtr_done = sem("vtr_done")
        st_ok = sem("st_ok")
        rs_ok = sem("rs_ok")
        khat_ok = sem("khat_ok")
        kscaled = sem("kscaled")
        bup_ok = sem("bup_ok"); decm_ok = sem("decm_ok")
        vtok_ok = sem("vtok_ok")
        khtr_done = sem("khtr_done")
        khT_ok = sem("khT_ok")
        gA_ok = sem("gA_ok")
        dec_done = sem("dec_done")
        dec_ok = sem("dec_ok")
        gram_done = sem("gram_done")
        att_ok = sem("att_ok")
        x1_ok = sem("x1_ok")
        xtr_done = sem("xtr_done")
        xtr_ok = sem("xtr_ok")
        t_done = sem("t_done")
        t_ok = sem("t_ok")
        p_done = sem("p_done")
        x_ok = sem("x_ok")
        wT_done = sem("wT_done")
        u_done = sem("u_done")
        qw_ok = sem("qw_ok")
        qq_ok = sem("qq_ok")
        s_ok = sem("s_ok")
        ws_done = sem("ws_done")
        vn_ok = sem("vn_ok")
        su_done = sem("su_done")
        av_done = sem("av_done")
        o_ok = sem("o_ok")
        osq_ok = sem("osq_ok")
        os_ok = sem("os_ok")
        or_ok = sem("or_ok")
        on_ok = sem("on_ok")
        otr_done = sem("otr_done")
        y_ok = sem("y_ok")
        yh_ok = sem("yh_ok")
        yl_ok = sem("yl_ok")

        def bc(col):
            return col.unsqueeze(2).to_broadcast([P, NT, P])

        def bm(mask):
            return mask.unsqueeze(1).to_broadcast([P, NT, P])

        def tiles(b):
            return bank[b].rearrange("p (t c) -> p t c", t=NT)

        def load_dn(sp, h, j):
            for i in range(2):
                dst = wRaw[:, j, i * D:(i + 1) * D].rearrange("p (k n) -> p k n", k=KT)
                sp.dma_start(dst, dn_in_v[:, :, bass.ds(h * P + (2 * j + i) * D, P)]).then_inc(panel_in[j], PANEL_INC // 2)

        def dn_sp(sp):
            with sp.Fori(1, HEADS_A) as h:
                for j in range(2):
                    sp.wait_ge(panel_lo, 2 * h + j - 1)
                    load_dn(sp, h, j)

        UNITS = 4 * KT
        BX, BY, BZ = 2, 3, 4
        BW, BS, BO = 5, 6, 7

        def project_pe(pe, h, u0, u1, first=False):
            for u in range(u0, u1):
                b, k = u // KT, u % KT
                if u % (2 * KT) == 0:
                    pe.wait_ge(panel_lo, 2 * h + b // 2 + 1)
                if k == 0 and (b >= 2 or not first):
                    if b == 1:
                        pe.wait_ge(feat_ok, 4 * h - 1)
                    else:
                        pe.wait_ge(taps_ok, 3 * h + (0, 0, 1, 2)[b])
                c = (b % 2) * D + k * P
                last = product(bank[b % 2], wH[:, b // 2, c:c + P], wL[:, b // 2, c:c + P],
                               aH[:, k, :], aL[:, k, :], k == 0, k == KT - 1)
                if k == KT - 1:
                    last.then_inc(tile_done, 1)

        def taps_act(act, h, b, first=False):
            act.wait_ge(tile_done, 4 * h + b + 1)
            if b or not first:
                act.wait_ge(feat_ok, 4 * h + b)
            for c in range(CONV):
                last = nc.scalar.activation(taps[:, c, c:S], bank[b % 2][:, 0:S - c], ACT.Copy,
                                            scale=convW[:, CONV - 1 - c, bass.ds(b * HEADS_A + h, 1)])
            last.then_inc(taps_ok, 1)

        def taps_pool(pool, h, b):
            g = nc.gpsimd
            pool.wait_ge(taps_ok, 3 * h + b + 1)
            g.tensor_tensor(taps[:, 0, 1:], taps[:, 0, 1:], taps[:, 1, 1:], ALU.add)
            g.tensor_tensor(taps[:, 2, 3:], taps[:, 2, 3:], taps[:, 3, 3:], ALU.add)
            pool.drain()
            g.tensor_tensor(taps[:, 0, 2:], taps[:, 0, 2:], taps[:, 2, 2:], ALU.add).then_inc(conv_ok, 1)

        def tanh_act(act, h, b, first=False):
            act.wait_ge(conv_ok, 3 * h + b + 1)
            if b == 2:
                act.wait_ge(feat_ok, 4 * h + 3)
            nc.scalar.activation(tanhT, taps[:, 0, :], ACT.Tanh, scale=0.5).then_inc(tanh_ok, 1)

        def silu_dve(dve, h, b, first=False):
            dve.wait_ge(tanh_ok, 4 * h + (1, 2, 4)[b])
            if b == 0 and not first:
                dve.wait_ge(qq_ok, h)
            nc.vector.scalar_tensor_tensor(out=(qF, kF, vF)[b], in0=tanhT, scalar=1.0, in1=taps[:, 0, :],
                                           op0=ALU.add, op1=ALU.mult).then_inc(feat_ok, 1)

        def square_pool(pool, h, b):
            pool.wait_ge(feat_ok, 4 * h + b + 1)
            f = (qF, kF)[b]
            nc.gpsimd.tensor_tensor(sq2[:, b], f, f, ALU.mult).then_inc(sq_ok, 1)

        def z_act(act, h):
            act.wait_ge(tile_done, 4 * h + 4)
            act.wait_ge(feat_ok, 4 * h + 2)
            nc.scalar.activation(tanhT, bank[1], ACT.Tanh, scale=0.5).then_inc(tanh_ok, 1)

        def z_dve(dve, h, slot):
            dve.wait_ge(tanh_ok, 4 * h + 3)
            nc.vector.scalar_tensor_tensor(out=zF[slot], in0=tanhT, scalar=1.0, in1=bank[1], op0=ALU.add, op1=ALU.mult).then_inc(feat_ok, 1)

        def per_tile(fn):
            for t in range(NT):
                last = fn(t)
            return last

        def dn_step_pe(pe, b, a, p, s):
            done = [0]

            def fill(n):
                if p is not None:
                    n = min(n, UNITS - done[0])
                    project_pe(pe, p, done[0], done[0] + n)
                    done[0] += n

            def walk(n):
                if b is None:
                    return
                pe.wait_ge(s_ok, 9 * b + n + 1)
                if n:
                    pe.wait_ge(o_ok, 8 * b + n)
                nc.tensor.matmul(bank[BW][:, 0:P], qw[s][:, n // 2, n % 2, :], state[:], start=True, stop=True).then_inc(ws_done, 1)

            def update(n):
                if b is None:
                    return
                t, c = n // 2, n % 2
                rows, orows = slice(c * CH, (c + 1) * CH), slice((1 - c) * CH, (2 - c) * CH)
                pe.wait_ge(vn_ok, 8 * b + n + 1)
                nc.tensor.matmul(bank[BS][:, 0:P], kDec[s][rows, t, :], vNew[rows, :], start=True, stop=True).then_inc(su_done, 1)
                nc.tensor.matmul(bank[BO][orows, 0:P], attT[s][rows, t, rows], vNew[rows, :],
                                 start=True, stop=True).then_inc(av_done, 1)

            if b is not None:
                pe.wait_ge(qw_ok, b + 1)
                pe.wait_ge(qq_ok, b + 1)
                pe.wait_ge(att_ok, b + 1)
            if a is not None:
                pe.wait_ge(sq_ok, 2 * a + 2)
                for t in range(NT):
                    for c in range(2):
                        src = sq2[:, 0, t * P + (1 - c) * CH:t * P + (1 - c) * CH + CH]
                        nc.tensor.matmul(bank[BZ][c * CH:(c + 1) * CH, t:t + 1], src, ones[:, 0:1], start=True, stop=True)
                per_tile(lambda t: nc.tensor.matmul(bank[BZ][:, NT + t:NT + t + 1], sq2[:, 1, rng(t)], ones[:, 0:1],
                                                    start=True, stop=True)).then_inc(nrm_done, 1)
                per_tile(lambda t: nc.tensor.transpose(bank[BX][:, rng(t)], kF[:, rng(t)], ident[:])).then_inc(ktr_done, 1)
            walk(0)
            fill(F[0])
            update(0)
            if a is not None:
                pe.wait_ge(gA_ok, a + 1)
                per_tile(lambda t: nc.tensor.matmul(bank[BY][:, rng(t)], gA[:, t, :], maskIncl[:], start=True, stop=True)).then_inc(dec_done, 1)
            walk(1)
            fill(F[1])
            if a is not None:
                pe.wait_ge(khat_ok, a + 1)
                per_tile(lambda t: nc.tensor.transpose(bank[BX][:, rng(t)], kTok[:, t, :], ident[:])).then_inc(khtr_done, 1)
            update(1)
            fill(F[2])
            walk(2)
            if a is not None:
                pe.wait_ge(khT_ok, a + 1)
                pe.wait_ge(st_ok, a + 1)
                per_tile(lambda t: nc.tensor.matmul(bank[BZ][:, rng(t)], kHatT[:, rng(t)], kHatT[:, rng(t)],
                                                    start=True, stop=True)).then_inc(gram_done, 1)
                per_tile(lambda t: nc.tensor.matmul(bank[BX][:, rng(t)], kHatT[:, rng(t)], qF[:, rng(t)],
                                                    start=True, stop=True)).then_inc(gram_done, 1)
            update(2)
            fill(F[3])
            walk(3)
            fill(F[4])
            update(3)
            fill(F[5])
            if a is not None:
                pe.wait_ge(x1_ok, a + 1)
                per_tile(lambda t: nc.tensor.transpose(bank[BZ][:, rng(t)], invT[:, t, :], ident[:])).then_inc(xtr_done, 1)
            between = ((lambda: walk(4), lambda: update(4), lambda: walk(5)),
                       (lambda: update(5), lambda: walk(6), lambda: update(6)),
                       (lambda: walk(7), lambda: update(7), lambda: None),
                       (lambda: None,) * 3, (lambda: None,) * 3)
            for i in range(len(LEVELS)):
                between[i][0]()
                fill(F[6][i][0])
                if a is not None:
                    pe.wait_ge(xtr_ok, 6 * a + i + 1)
                    if i == 0:
                        pe.wait_ge(att_ok, a + 1)
                    per_tile(lambda t: nc.tensor.matmul(bank[BX][:, rng(t)], lowT[:, t, :], inv[:, t, :],
                                                        start=True, stop=True)).then_inc(t_done, 1)
                between[i][1]()
                fill(F[6][i][1])
                if a is not None:
                    pe.wait_ge(t_ok, 5 * a + i + 1)
                    if i == 0:
                        pe.wait_ge(dec_ok, a + 1)
                    if i == VTR + 1:
                        pe.wait_ge(vtok_ok, a + 1)
                    per_tile(lambda t: nc.tensor.matmul(bank[BY][:, rng(t)], invT[:, t, :], tMask[:, t, :],
                                                        start=True, stop=True)).then_inc(p_done, 1)
                between[i][2]()
                fill(F[6][i][2])
                if a is not None:
                    pe.wait_ge(x_ok, 5 * a + i + 1)
                    per_tile(lambda t: nc.tensor.transpose(bank[BZ][:, rng(t)], inv[:, t, :], ident[:])).then_inc(xtr_done, 1)
                    if i == VTR:
                        pe.wait_ge(feat_ok, 4 * a + 4)
                        per_tile(lambda t: nc.tensor.transpose(bank[BY][:, rng(t)], vF[:, rng(t)], ident[:])).then_inc(vtr_done, 1)
            if b is not None:
                pe.wait_ge(on_ok, b + 1)
                per_tile(lambda t: nc.tensor.transpose(bank[BS][:, rng(t)], oTok[:, t, :], ident[:])).then_inc(otr_done, 1)
            fill(F[7])
            if a is not None:
                pe.wait_ge(xtr_ok, 6 * a + 6)
                pe.wait_ge(kscaled, a + 1)
                per_tile(lambda t: nc.tensor.matmul(bank[BX][:, rng(t)], kEg[:, t, :], invT[:, t, :],
                                                    start=True, stop=True)).then_inc(wT_done, 1)
                per_tile(lambda t: nc.tensor.matmul(bank[BY][:, rng(t)], invT[:, t, :], vTok[:, t, :],
                                                    start=True, stop=True)).then_inc(u_done, 1)
            fill(UNITS)

        VTR = 0
        F = (1, 1, 2, 1, 1, 3, ((1, 1, 1), (1, 1, 1), (1, 1, 1), (1, 1, 1), (2, 1, 1)), 3)

        def dn_step_act(act, b, a, p, s, n):
            a_ = nc.scalar

            def q_part(n):
                if b is None:
                    return
                t, c = n // 2, n % 2
                orows = slice((1 - c) * CH, (2 - c) * CH)
                act.wait_ge(vn_ok, 8 * b + n + 1)
                a_.activation(oTok[orows, t, :], bank[BW][orows, 0:P], ACT.Copy, scale=hc[orows, s, EGS_, t:t + 1]).then_inc(oq_ok, 1)

            q_part(0)
            if a is not None:
                z_act(act, a)
                act.wait_ge(dec_done, a + 1)
                a_.activation(decT, t4(bank[BY]), ACT.Exp).then_inc(dec_ok, 1)
            q_part(1)
            if a is not None:
                act.wait_ge(khtr_done, a + 1)
                a_.copy(kHatT[:], bank[BX]).then_inc(khT_ok, 1)
            q_part(2)
            q_part(3)
            if n is not None:
                prep_hi(act, n, 1)
            if a is not None:
                act.wait_ge(xtr_done, 6 * a + 1)
                a_.copy(inv, t4(bank[BZ])).then_inc(xtr_ok, 1)
            for i in range(len(LEVELS)):
                if i == 0:
                    if a is not None:
                        tanh_act(act, a, 2)
                    q_part(4)
                    q_part(5)
                if i == 1:
                    q_part(6)
                if i == 2 and p is not None:
                    tanh_act(act, p, 0)
                if i == 4 and p is not None:
                    tanh_act(act, p, 1)
                if a is not None:
                    act.wait_ge(xtr_done, 6 * a + i + 2)
                    a_.copy(invT, t4(bank[BZ])).then_inc(xtr_ok, 1)
                if i == VTR and a is not None:
                    act.wait_ge(vtr_done, a + 1)
                    a_.activation(vTok[:], t4(bank[BY]), ACT.Copy, scale=0.5).then_inc(vtok_ok, 1)
                if i == 1:
                    q_part(7)
                if i == 2 and b is not None:
                    act.wait_ge(o_ok, 8 * b + 8)
                    a_.activation(oSq, oTok[:], ACT.Square).then_inc(osq_ok, 1)
                if p is not None and i % 2 == 0:
                    taps_act(act, p, i // 2)
                if p is not None and i == 3:
                    prep_hi(act, n + 1, 0)
            if b is not None:
                act.wait_ge(y_ok, b + 1)
                a_.copy(bH[:, b, :], yF[:]).then_inc(yh_ok, 1)
            if a is not None:
                act.wait_ge(wT_done, a + 1)
                a_.copy(qw[1 - s][:, :, 0, 0:CH], t4(bank[BX])[:, :, 0:CH])
                a_.copy(qw[1 - s][:, :, 1, CH:P], t4(bank[BX])[:, :, CH:P]).then_inc(qw_ok, 1)

        def dn_step_dve(dve, b, a, p, s, n):
            v = nc.vector

            def correct(n):
                if b is None:
                    return
                t, c = n // 2, n % 2
                rows = slice(c * CH, (c + 1) * CH)
                dve.wait_ge(ws_done, 8 * b + n + 1)
                v.scalar_tensor_tensor(out=vNew[rows, :], in0=bank[BW][rows, 0:P], scalar=hc[rows, s, NB_, t:t + 1],
                                       in1=uB[rows, s, t, :], op0=ALU.mult, op1=ALU.add).then_inc(vn_ok, 1)
                dve.drain()

            def advance(n):
                if b is None:
                    return
                t, c = n // 2, n % 2
                orows = slice((1 - c) * CH, (2 - c) * CH)
                dve.wait_ge(su_done, 8 * b + n + 1)
                v.scalar_tensor_tensor(out=state[:], in0=state[:], scalar=hc[:, s, EL0_ + c, t:t + 1], in1=bank[BS][:, 0:P],
                                       op0=ALU.mult, op1=ALU.add).then_inc(s_ok, 1)
                dve.wait_ge(av_done, 8 * b + n + 1)
                dve.wait_ge(oq_ok, 8 * b + n + 1)
                v.tensor_tensor(oTok[orows, t, :], oTok[orows, t, :], bank[BO][orows, 0:P], ALU.add).then_inc(o_ok, 1)

            def tail(part):
                if b is None:
                    return
                if part == 0:
                    v.tensor_tensor(os4[:, 1, :], rs8[:, s, 0:4], rs8[:, s, 0:4], ALU.mult)
                    dve.wait_ge(osq_ok, b + 1)
                    v.tensor_reduce(os4[:, 0, :], oSq, AX, ALU.add)
                    dve.drain()
                    v.tensor_tensor(os4[:, 0, :], os4[:, 0, :], os4[:, 1, :], ALU.mult)
                    dve.drain()
                    v.tensor_scalar(os4[:, 0, :], os4[:, 0, :], 1.0 / (P * P), EPS, ALU.mult, ALU.add).then_inc(os_ok, 1)
                elif part == 1:
                    dve.wait_ge(or_ok, b + 1)
                    v.scalar_tensor_tensor(out=os4[:, 3, :], in0=os4[:, 2, :], scalar=0.5 * P ** -0.5, in1=rs8[:, s, 0:4],
                                           op0=ALU.mult, op1=ALU.mult)
                    dve.drain()
                    v.tensor_tensor(oTok[:], oTok[:], bc(os4[:, 3, :]), ALU.mult).then_inc(on_ok, 1)
                elif part == 2:
                    dve.wait_ge(otr_done, b + 1)
                    yt, zt = t4(yF[:]), t4(zF[s])
                    for c in range(2):
                        last = v.scalar_tensor_tensor(out=yt[:, :, c * CH:(c + 1) * CH], in0=t4(bank[BS])[:, :, (1 - c) * CH:(2 - c) * CH],
                                                      scalar=normW, in1=zt[:, :, c * CH:(c + 1) * CH], op0=ALU.mult, op1=ALU.mult)
                    last.then_inc(y_ok, 1)
                    dve.drain()
                else:
                    dve.wait_ge(yh_ok, b + 1)
                    v.tensor_tensor(bL[:, b, :], yF[:], bH[:, b, :].bitcast(F32), ALU.subtract).then_inc(yl_ok, 1)

            if a is not None:
                v.tensor_copy(hc[:, 1 - s], gate[:, a])
                dve.drain()
                v.tensor_tensor(gA, bm(maskLow[:]), bc(hc[:, 1 - s, G_, :]), ALU.mult).then_inc(gA_ok, 1)
                dve.wait_ge(nrm_done, a + 1)
                v.tensor_scalar(st8[:], bank[BZ][:, 0:8], 4 * EPS, None, ALU.add).then_inc(st_ok, 1)
            correct(0)
            advance(0)
            if a is not None:
                z_dve(dve, a, 1 - s)
            correct(1)
            if a is not None:
                dve.wait_ge(rs_ok, 2 * a + 1)
                dve.wait_ge(ktr_done, a + 1)
                v.tensor_tensor(kTok[:], t4(bank[BX]), bc(rs8[:, 1 - s, 4:8]), ALU.mult).then_inc(khat_ok, 1)
            advance(1)
            correct(2)
            advance(2)
            correct(3)
            if a is not None:
                dve.wait_ge(gram_done, 2 * a + 2)
                dve.wait_ge(bup_ok, a + 1)
                v.tensor_tensor(lowT, t4(bank[BZ]), betaUp, ALU.mult)
                dve.drain()
                v.tensor_tensor(invT, lowT, bm(maskPair[:]), ALU.mult)
                dve.drain()
                v.tensor_tensor(invT, bm(ident[:]), invT, ALU.subtract).then_inc(x1_ok, 1)
            advance(3)
            if a is not None:
                dve.wait_ge(decm_ok, a + 1)
                v.tensor_tensor(attT[1 - s], t4(bank[BX]), decT, ALU.mult).then_inc(att_ok, 1)
            between = ((lambda: correct(4), lambda: (advance(4), correct(5))),
                       (lambda: (advance(5), correct(6)), lambda: advance(6)),
                       (lambda: correct(7), lambda: advance(7)),
                       (lambda: None, lambda: tail(0)),
                       (lambda: tail(1), lambda: None))
            for i in range(len(LEVELS)):
                between[i][0]()
                if a is not None:
                    dve.wait_ge(t_done, 5 * a + i + 1)
                    v.tensor_tensor(tMask, t4(bank[BX]), bm(maskLev[:, i, :]), ALU.mult).then_inc(t_ok, 1)
                if i == 0 and a is not None:
                    silu_dve(dve, a, 2)
                if i == 2 and p is not None:
                    silu_dve(dve, p, 0)
                between[i][1]()
                if a is not None:
                    dve.wait_ge(p_done, 5 * a + i + 1)
                    v.tensor_tensor(inv, inv, t4(bank[BY]), ALU.subtract).then_inc(x_ok, 1)
                if i in (0, 1) and n is not None:
                    prep_lo(dve, n, 1, i)
                if i == 4 and p is not None:
                    silu_dve(dve, p, 1)
                if i == 4 and p is not None:
                    prep_lo(dve, n + 1, 0, 0)
            tail(2)
            if p is not None:
                prep_lo(dve, n + 1, 0, 1)
            tail(3)
            if a is not None:
                dve.wait_ge(u_done, a + 1)
                v.tensor_tensor(uB[:, 1 - s], t4(bank[BY]), bc(hc[:, 1 - s, B_, :]), ALU.mult)
                dve.drain()
                v.memset(state[:], 0.0).then_inc(s_ok, 1)
            dve.drain()

        def dn_step_pool(pool, b, a, p, s):
            g = nc.gpsimd
            if a is not None:
                qt = t4(qF)
                q_ = 1 - s
                pool.wait_ge(st_ok, a + 1)
                g.tensor_tensor(rs8[:, q_, 4:8], st8[:, 4:8], minusHalf[:, 0:4], ALU.pow).then_inc(rs_ok, 1)
                g.tensor_tensor(betaUp, bm(maskUp[:]), bc(hc[:, q_, B_, :]), ALU.mult)
                g.tensor_tensor(rs8[:, q_, 0:4], st8[:, 0:4], minusHalf[:, 0:4], ALU.pow).then_inc(rs_ok, 1)
                pool.drain()
                pool.wait_ge(dec_ok, a + 1)
                g.tensor_tensor(betaUp, betaUp, decT, ALU.mult).then_inc(bup_ok, 1)
                pool.drain()
                g.tensor_tensor(decT, decT, bm(maskIncl[:]), ALU.mult).then_inc(decm_ok, 1)
                g.tensor_copy(qw[q_][:, :, 0, CH:P], qt[:, :, 0:CH])
                g.tensor_copy(qw[q_][:, :, 1, 0:CH], qt[:, :, CH:P]).then_inc(qq_ok, 1)
                taps_pool(pool, a, 2)
                pool.wait_ge(khat_ok, a + 1)
                g.tensor_tensor(kEg, kTok[:], bc(hc[:, q_, EG_, :]), ALU.mult)
                g.tensor_tensor(kDec[q_], kTok[:], bc(hc[:, q_, ED_, :]), ALU.mult).then_inc(kscaled, 1)
            if p is not None:
                taps_pool(pool, p, 0)
            if b is not None:
                pool.wait_ge(os_ok, b + 1)
                g.tensor_tensor(os4[:, 2, :], os4[:, 0, :], minusHalf[:, 0:4], ALU.pow).then_inc(or_ok, 1)
            if p is not None:
                square_pool(pool, p, 0)
                taps_pool(pool, p, 1)
                square_pool(pool, p, 1)

        PAIRS = (HEADS_A - 2) // 2

        def dn_pe(pe):
            project_pe(pe, 0, 0, 4, first=True)
            gates_pe2(pe)
            project_pe(pe, 0, 4, 24, first=True)
            gates_pe3(pe)
            project_pe(pe, 0, 24, UNITS, first=True)
            dn_step_pe(pe, None, 0, 1, 1)
            with pe.Fori(0, PAIRS) as i:
                dn_step_pe(pe, 2 * i, 2 * i + 1, 2 * i + 2, 0)
                dn_step_pe(pe, 2 * i + 1, 2 * i + 2, 2 * i + 3, 1)
            dn_step_pe(pe, HEADS_A - 2, HEADS_A - 1, None, 0)
            dn_step_pe(pe, HEADS_A - 1, None, None, 1)

        def dn_act(act):
            for b in range(2):
                taps_act(act, 0, b, first=True)
                tanh_act(act, 0, b, first=True)
            gates_act3(act)
            taps_act(act, 0, 2)
            prep_hi(act, 2, 0)
            dn_step_act(act, None, 0, 1, 1, 3)
            with act.Fori(0, PAIRS) as i:
                dn_step_act(act, 2 * i, 2 * i + 1, 2 * i + 2, 0, 4 * i + 5)
                dn_step_act(act, 2 * i + 1, 2 * i + 2, 2 * i + 3, 1, 4 * i + 7)
            dn_step_act(act, HEADS_A - 2, HEADS_A - 1, None, 0, 2 * HEADS_A + 1)
            dn_step_act(act, HEADS_A - 1, None, None, 1, None)

        def dn_dve(dve):
            for b in range(2):
                silu_dve(dve, 0, b, first=True)
            prep_lo(dve, 2, 0)
            dve.wait_ge(gate_e, 3)
            dn_step_dve(dve, None, 0, 1, 1, 3)
            with dve.Fori(0, PAIRS) as i:
                dn_step_dve(dve, 2 * i, 2 * i + 1, 2 * i + 2, 0, 4 * i + 5)
                dn_step_dve(dve, 2 * i + 1, 2 * i + 2, 2 * i + 3, 1, 4 * i + 7)
            dn_step_dve(dve, HEADS_A - 2, HEADS_A - 1, None, 0, 2 * HEADS_A + 1)
            dn_step_dve(dve, HEADS_A - 1, None, None, 1, None)

        def dn_pool(pool):
            for b in range(2):
                taps_pool(pool, 0, b)
                square_pool(pool, 0, b)
            dn_step_pool(pool, None, 0, 1, 1)
            with pool.Fori(0, PAIRS) as i:
                dn_step_pool(pool, 2 * i, 2 * i + 1, 2 * i + 2, 0)
                dn_step_pool(pool, 2 * i + 1, 2 * i + 2, 2 * i + 3, 1)
            dn_step_pool(pool, HEADS_A - 2, HEADS_A - 1, None, 0)
            dn_step_pool(pool, HEADS_A - 1, None, None, 1)

        dn_mem.close()

        acc = sb("acc", [P, KT, S])
        pleT = sb("pleT", [P, KT, S])
        mlp_mem = ExitStack()
        mlp_mem.__enter__()

        def sbm(name, shape, dt=F32):
            return mlp_mem.enter_context(nc.sbuf_tensor(name, shape, dt))
        pTok = sbm("pTok", [P, NT, PLE])
        pH, pL = sbm("pH", [P, 2, S], F32R), sbm("pL", [P, 2, S], F32R)
        hid = sbm("hid", [P, 2, S])
        hid2 = sbm("hid2", [P, 2, S])
        rSq = sbm("rSq", [P, S])
        diag = sbm("diag", [P, NT, P])
        gA2, gB2 = sbm("gA2", [P, 2, S]), sbm("gB2", [P, 2, S])

        res_ok = sem("res_ok")
        next_hi = sem("next_hi")
        next_lo = sem("next_lo")
        sq_done = sem("sq_done")
        sq_used = sem("sq_used")
        n_sum = sem("n_sum")
        n_ms = sem("n_ms")
        n_r = sem("n_r")
        n_diag = sem("n_diag")
        n_bc = sem("n_bc")
        n_ok = sem("n_ok")
        p_in = sem("p_in")
        ptr_done = sem("ptr_done")
        p_hi = sem("p_hi")
        p_lo = sem("p_lo")
        hid_f = sem("hid_f")
        hid_hi = sem("hid_hi")
        hid_lo = sem("hid_lo")
        down_read = sem("down_read")
        ple_ok = sem("ple_ok")
        gate_in = sem("gate_in")
        gate_th = sem("gate_th")

        X_A, X_B = (aH, aL), (bH, bL)
        NEXT = [X_A, X_A, X_B, X_B, X_B, None]

        def next_act(act, u, m):
            act.wait_ge(res_ok, 8 * u + m + 1)
            dst = acc[:, m, :] if NEXT[u] is None else NEXT[u][0][:, m, :]
            nc.scalar.activation(dst, hT[:, m, :], ACT.Copy, scale=gains[:, u + 1, m:m + 1]).then_inc(next_hi, 1)
            if 8 * u + m >= 2:
                act.wait_ge(sq_used, 8 * u + m - 1)
            nc.scalar.activation(sqT[:, m % 2, :], hT[:, m, :], ACT.Square).then_inc(sq_done, 1)

        def next_dve(dve, u, m):
            if NEXT[u] is None:
                return
            dve.wait_ge(next_hi, 8 * u + m + 1)
            nc.vector.scalar_tensor_tensor(out=NEXT[u][1][:, m, :], in0=hT[:, m, :], scalar=gains[:, u + 1, m:m + 1],
                                           in1=NEXT[u][0][:, m, :].bitcast(F32), op0=ALU.mult, op1=ALU.subtract).then_inc(next_lo, 1)

        def norm_pool(pool, u):
            for m in range(KT):
                pool.wait_ge(sq_done, 8 * u + m + 1)
                if m == 0:
                    if u:
                        pool.wait_ge(n_sum, u)
                    nc.gpsimd.tensor_copy(sqSum[:], sqT[:, 0, :]).then_inc(sq_used, 1)
                else:
                    pool.drain()
                    nc.gpsimd.tensor_tensor(sqSum[:], sqSum[:], sqT[:, m % 2, :], ALU.add).then_inc(sq_used, 1)
            pool.wait_ge(n_ms, u + 1)
            nc.gpsimd.tensor_tensor(rCol, msq[:, 0:NT], minusHalf[:, 0:NT], ALU.pow).then_inc(n_r, 1)

        def norm_pe_sum(pe, u):
            pe.wait_ge(sq_used, 8 * u + 8)
            for t in range(NT):
                last = nc.tensor.matmul(bank[7][:, t:t + 1], sqSum[:, rng(t)], ones[:, 0:1], start=True, stop=True)
            last.then_inc(n_sum, 1)

        def norm_dve(dve, u):
            dve.wait_ge(n_sum, u + 1)
            nc.vector.tensor_scalar(msq[:, 0:NT], bank[7][:, 0:NT], 1.0 / D, EPS, ALU.mult, ALU.add).then_inc(n_ms, 1)
            dve.wait_ge(n_r, u + 1)
            if u == 5:
                return
            nc.vector.tensor_tensor(diag[:], ident[:].unsqueeze(1).to_broadcast([P, NT, P]),
                                    rCol.unsqueeze(2).to_broadcast([P, NT, P]), ALU.mult).then_inc(n_diag, 1)

        def norm_pe_bc(pe, u):
            pe.wait_ge(n_diag, u + 1)
            nc.tensor.matmul(bank[7], ones[:], diag[:].rearrange("p t c -> p (t c)"), start=True, stop=True).then_inc(n_bc, 1)

        def norm_act(act, u):
            act.wait_ge(n_bc, u + 1)
            nc.scalar.copy(rBC[:], bank[7]).then_inc(n_ok, 1)

        def panel_tile(slot, k, c):
            return slice(k * 256 + c * P, k * 256 + c * P + P)

        def out_pe(pe, n0, u, X, ready):
            for m in range(KT):
                n = n0 + m // 2
                if m % 2 == 0:
                    pe.wait_ge(panel_lo, n + 1)
                if m >= 2:
                    pe.wait_ge(res_ok, 8 * u + m - 1)
                for k in range(KT):
                    if m == 0:
                        ready(pe, k)
                    c = panel_tile(0, k, m % 2)
                    last = product(bank[4 + m % 2], wH[:, n % 2, c], wL[:, n % 2, c], X[0][:, k, :], X[1][:, k, :], k == 0, k == KT - 1)
                last.then_inc(tile_done, 1)

        def out_act(act, n0, u):
            for m in range(KT):
                if m % 2 == 0 and (m or u):
                    prep_hi(act, n0 + m // 2 + 1, (n0 + m // 2 + 1) % 2)
                next_act(act, u, m)

        def out_dve(dve, n0, u, bias=None):
            for m in range(KT):
                if m % 2 == 0 and (m or u):
                    prep_lo(dve, n0 + m // 2 + 1, (n0 + m // 2 + 1) % 2)
                dve.wait_ge(tile_done, tiles_before(n0) + m + 1)
                if bias is None:
                    nc.vector.tensor_tensor(hT[:, m, :], bank[4 + m % 2], hT[:, m, :], ALU.add).then_inc(res_ok, 1)
                else:
                    nc.vector.scalar_tensor_tensor(out=hT[:, m, :], in0=bank[4 + m % 2], scalar=bias[:, m:m + 1], in1=hT[:, m, :],
                                                   op0=ALU.add, op1=ALU.add).then_inc(res_ok, 1)
                if m:
                    next_dve(dve, u, m - 1)
            next_dve(dve, u, KT - 1)

        def up_pe(pe, i, g, n0, u, X, Y, first):
            for m in range(KT):
                n = n0 + 8 * g + m // 2
                s = (n0 + m // 2) % 2
                if m % 2 == 0:
                    pe.wait_ge(panel_lo, n + 1)
                if m >= 2:
                    pe.wait_ge(hid_f, 8 * (GROUPS * i + g) + m - 1)
                for k in range(KT):
                    if m == 0 and first:
                        pe.wait_ge(next_lo, 8 * u - 8 + k + 1)
                    c = panel_tile(s, k, m % 2)
                    last = product(bank[m % 2], wH[:, s, c], wL[:, s, c], X[0][:, k, :], X[1][:, k, :], k == 0, k == KT - 1)
                last.then_inc(tile_done, 1)

        def down_pe(pe, i, g, n0, u, Y):
            for m in range(KT):
                n = n0 + 8 * g + 4 + m // 2
                s = (n0 + 4 + m // 2) % 2
                if m % 2 == 0:
                    pe.wait_ge(panel_lo, n + 1)
                if m >= 2:
                    pe.wait_ge(down_read, 8 * (GROUPS * i + g) + m - 1)
                for k in range(KT):
                    if m == 0:
                        pe.wait_ge(hid_lo, 8 * (GROUPS * i + g) + k + 1)
                    c = panel_tile(s, k, m % 2)
                    last = product(bank[4 + m % 2], wH[:, s, c], wL[:, s, c], Y[0][:, k, :], Y[1][:, k, :], k == 0, k == KT - 1)
                last.then_inc(tile_done, 1)

        def up_act(act, i, g, n0, Y, extra):
            for m in range(KT):
                if m % 2 == 0:
                    prep_hi(act, n0 + 8 * g + m // 2 + 1, (n0 + m // 2 + 1) % 2, extra)
                act.wait_ge(tile_done, 2 * (n0 + 8 * g) + extra + m + 1)
                if m >= 2:
                    act.wait_ge(hid_lo, 8 * (GROUPS * i + g) + m - 1)
                nc.scalar.activation(hid[:, m % 2, :], bank[m % 2], ACT.Relu).then_inc(hid_f, 1)
                act.drain()
                nc.scalar.activation(Y[0][:, m, :], hid[:, m % 2, :], ACT.Square).then_inc(hid_hi, 1)

        def down_act(act, i, g, n0, u, last, extra):
            for m in range(KT):
                if m % 2 == 0:
                    prep_hi(act, n0 + 8 * g + 4 + m // 2 + 1, (n0 + m // 2 + 1) % 2, extra)
                if last:
                    next_act(act, u, m)

        def up_dve(dve, i, g, n0, Y, extra):
            for m in range(KT):
                if m % 2 == 0:
                    prep_lo(dve, n0 + 8 * g + m // 2 + 1, (n0 + m // 2 + 1) % 2)
                dve.wait_ge(hid_f, 8 * (GROUPS * i + g) + m + 1)
                nc.vector.tensor_tensor(hid2[:, m % 2, :], hid[:, m % 2, :], hid[:, m % 2, :], ALU.mult)
                dve.drain()
                dve.wait_ge(hid_hi, 8 * (GROUPS * i + g) + m + 1)
                nc.vector.tensor_tensor(Y[1][:, m, :], hid2[:, m % 2, :], Y[0][:, m, :].bitcast(F32), ALU.subtract).then_inc(hid_lo, 1)

        def down_dve(dve, i, g, n0, u, last, extra):
            for m in range(KT):
                if m % 2 == 0:
                    prep_lo(dve, n0 + 8 * g + 4 + m // 2 + 1, (n0 + m // 2 + 1) % 2)
                dve.wait_ge(tile_done, 2 * (n0 + 8 * g + 4) + extra + m + 1)
                nc.vector.tensor_tensor(acc[:, m, :], bank[4 + m % 2], acc[:, m, :], ALU.add).then_inc(down_read, 1)
                if last:
                    dve.drain()
                    nc.vector.tensor_tensor(acc[:, m, :], acc[:, m, :], rSq[:], ALU.mult)
                    dve.drain()
                    nc.vector.tensor_tensor(hT[:, m, :], acc[:, m, :], hT[:, m, :], ALU.add).then_inc(res_ok, 1)
                    if m:
                        next_dve(dve, u, m - 1)
            if last:
                next_dve(dve, u, KT - 1)

        acc_zero = sem("acc_zero")

        def mlp_pool(pool, i, u):
            nc.gpsimd.memset(acc[:], 0.0).then_inc(acc_zero, 1)

        def mlp_pe(pe, i, n0, u, X, Y):
            up_pe(pe, i, 0, n0, u, X, Y, True)
            norm_pe_sum(pe, u - 1)
            down_pe(pe, i, 0, n0, u, Y)
            norm_pe_bc(pe, u - 1)
            with pe.Fori(1, GROUPS - 1) as g:
                up_pe(pe, i, g, n0, u, X, Y, False)
                down_pe(pe, i, g, n0, u, Y)
            up_pe(pe, i, GROUPS - 1, n0, u, X, Y, False)
            ple_in_pe(pe, i)
            down_pe(pe, i, GROUPS - 1, n0, u, Y)

        def mlp_act(act, i, n0, u, X, Y):
            extra = tiles_before(n0) - 2 * n0
            up_act(act, i, 0, n0, Y, extra)
            down_act(act, i, 0, n0, u, False, extra)
            norm_act(act, u - 1)
            with act.Fori(1, GROUPS - 1) as g:
                up_act(act, i, g, n0, Y, extra)
                down_act(act, i, g, n0, u, False, extra)
            up_act(act, i, GROUPS - 1, n0, Y, extra)
            ple_in_act(act, i)
            down_act(act, i, GROUPS - 1, n0, u, True, extra)

        def mlp_dve(dve, i, n0, u, X, Y):
            extra = tiles_before(n0) - 2 * n0
            up_dve(dve, i, 0, n0, Y, extra)
            norm_dve(dve, u - 1)
            dve.wait_ge(acc_zero, i + 1)
            down_dve(dve, i, 0, n0, u, False, extra)
            with dve.Fori(1, GROUPS - 1) as g:
                up_dve(dve, i, g, n0, Y, extra)
                down_dve(dve, i, g, n0, u, False, extra)
            up_dve(dve, i, GROUPS - 1, n0, Y, extra)
            ple_in_dve(dve, i)
            dve.wait_ge(n_ok, norms_bc(u - 1))
            nc.vector.tensor_tensor(rSq[:], rBC[:], rBC[:], ALU.mult)
            dve.drain()
            down_dve(dve, i, GROUPS - 1, n0, u, True, extra)

        def norms_bc(u):
            return u + 1

        def mlp_sp(sp, i, n0):
            up, down = mlp_w_up[i], mlp_w_down[i]
            with sp.Fori(0, GROUPS) as g:
                for j in range(4):
                    n = n0 + 8 * g + j
                    sp.wait_ge(panel_lo, n - 1)
                    v = up[:, bass.ds(g * D + 256 * j, 256)].rearrange("(k p) n -> p k n", p=P)
                    for q in range(2):
                        sp.dma_start(wRaw[:, (n0 + j) % 2, :].rearrange("p (k n) -> p k n", k=KT)[:, 4 * q:4 * q + 4, :],
                                     v[:, 4 * q:4 * q + 4, :]).then_inc(panel_in[(n0 + j) % 2], PANEL_INC // 2)
                for j in range(4):
                    n = n0 + 8 * g + 4 + j
                    sp.wait_ge(panel_lo, n - 1)
                    for q in range(2):
                        v = down[bass.ds(g * D + q * S, S), 256 * j:256 * j + 256].rearrange("(k p) n -> p k n", p=P)
                        sp.dma_start(wRaw[:, (n0 + j) % 2, :].rearrange("p (k n) -> p k n", k=KT)[:, 4 * q:4 * q + 4, :],
                                     v).then_inc(panel_in[(n0 + j) % 2], PANEL_INC // 2)

        def ple_load(sp, i):
            sp.dma_start(pTok[:], p[i, 0].rearrange("(t p) c -> p t c", p=P)).then_inc(p_in, 16)

        def ple_in_pe(pe, i):
            pe.wait_ge(p_in, 16 * (i + 1))
            for c in range(2):
                for t in range(NT):
                    last = nc.tensor.transpose(bank[2 + c][:, rng(t)], pTok[:, t, rng(c)], ident[:])
                last.then_inc(ptr_done, 1)

        def ple_in_act(act, i):
            for c in range(2):
                act.wait_ge(ptr_done, 2 * i + c + 1)
                nc.scalar.copy(pH[:, c, :], bank[2 + c]).then_inc(p_hi, 1)

        def ple_in_dve(dve, i):
            for c in range(2):
                dve.wait_ge(p_hi, 2 * i + c + 1)
                nc.vector.tensor_tensor(pL[:, c, :], bank[2 + c], pH[:, c, :].bitcast(F32), ALU.subtract).then_inc(p_lo, 1)

        def ple_pe(pe, i, n0, u, X):
            pe.wait_ge(panel_lo, n0 + 1)
            pe.wait_ge(p_lo, 2 * i + 2)
            for m in range(KT):
                if m >= 2:
                    pe.wait_ge(ple_ok, 8 * i + m - 1)
                for k in range(2):
                    c = slice(k * D + m * P, k * D + m * P + P)
                    last = product(bank[m % 2], wH[:, n0 % 2, c], wL[:, n0 % 2, c], pH[:, k, :], pL[:, k, :], k == 0, k == 1)
                last.then_inc(tile_done, 1)
            norm_pe_sum(pe, u - 1)
            for m in range(KT):
                n = n0 + 1 + m // 2
                if m % 2 == 0:
                    pe.wait_ge(panel_lo, n + 1)
                if m >= 2:
                    pe.wait_ge(gate_in, 8 * i + m - 1)
                for k in range(KT):
                    if m == 0:
                        pe.wait_ge(next_lo, 8 * u - 8 + k + 1)
                    c = panel_tile(0, k, m % 2)
                    last = product(bank[2 + m % 2], wH[:, n % 2, c], wL[:, n % 2, c], X[0][:, k, :], X[1][:, k, :], k == 0, k == KT - 1)
                last.then_inc(tile_done, 1)
                if m == 0:
                    norm_pe_bc(pe, u - 1)

        def ple_act(act, i, n0, u):
            prep_hi(act, n0 + 1, (n0 + 1) % 2)
            for m in range(KT):
                act.wait_ge(tile_done, tiles_before(n0) + m + 1)
                nc.scalar.copy(pleT[:, m, :], bank[m % 2]).then_inc(ple_ok, 1)
            norm_act(act, u - 1)
            for m in range(KT):
                if m % 2 == 0:
                    prep_hi(act, n0 + 2 + m // 2, (n0 + 2 + m // 2) % 2)
                act.wait_ge(gate_in, 8 * i + m + 1)
                nc.scalar.activation(gB2[:, m % 2, :], gA2[:, m % 2, :], ACT.Tanh, scale=0.5).then_inc(gate_th, 1)
                if m:
                    next_act(act, u, m - 1)
            next_act(act, u, KT - 1)

        def ple_dve(dve, i, n0, u):
            prep_lo(dve, n0 + 1, (n0 + 1) % 2)
            norm_dve(dve, u - 1)

            def finish(m):
                dve.wait_ge(gate_th, 8 * i + m + 1)
                dve.wait_ge(ple_ok, 8 * i + m + 1)
                nc.vector.scalar_tensor_tensor(out=pleT[:, m, :], in0=gB2[:, m % 2, :], scalar=1.0, in1=pleT[:, m, :],
                                               op0=ALU.add, op1=ALU.mult)
                dve.drain()
                nc.vector.scalar_tensor_tensor(out=hT[:, m, :], in0=pleT[:, m, :], scalar=0.5, in1=hT[:, m, :],
                                               op0=ALU.mult, op1=ALU.add).then_inc(res_ok, 1)
            for m in range(KT):
                if m % 2 == 0:
                    prep_lo(dve, n0 + 2 + m // 2, (n0 + 2 + m // 2) % 2)
                dve.wait_ge(tile_done, tiles_before(n0 + 1) + m + 1)
                if m == 0:
                    dve.wait_ge(n_ok, norms_bc(u - 1))
                nc.vector.tensor_tensor(gA2[:, m % 2, :], bank[2 + m % 2], rBC[:], ALU.mult).then_inc(gate_in, 1)
                if m:
                    finish(m - 1)
                    if m > 1:
                        next_dve(dve, u, m - 2)
            finish(KT - 1)
            next_dve(dve, u, KT - 2)
            next_dve(dve, u, KT - 1)

        def ple_sp(sp, i, n0):
            v = ple_w_proj[i].rearrange("(k p) n -> p k n", p=P)
            dst = wRaw[:, n0 % 2, :].rearrange("p (k n) -> p k n", k=2)
            sp.wait_ge(panel_lo, n0 - 1)
            for q in range(2):
                sp.dma_start(dst[:, q, :], v[:, q, :]).then_inc(panel_in[n0 % 2], PANEL_INC // 2)
            for j in range(4):
                sp.wait_ge(panel_lo, n0 + j)
                load_square(sp, n0 + 1 + j, square_panel(ple_w_gate[i], 0, 256 * j))

        mlp_mem.close()
        qkHi, qkLo = [[a[:, 2 * i:2 * i + 2, :] for i in range(4)] for a in (aH, aL)]
        qS = sb("qS", [P, GRP, 2, 2, S], F32R)
        kS = sb("kS", [P, 2, 2, S], F32R)
        vT = pleT[:, 0:2, :].rearrange("p a b -> p (a b)").rearrange("p (t c) -> p t c", t=NT)
        probs = [acc[:, 2 * i:2 * i + 2, :].rearrange("p a b -> p (a b)").rearrange("p (j k) -> p j k", j=GRP) for i in range(2)]
        probsT = [acc[:, 4 + 2 * i:6 + 2 * i, :] for i in range(2)]
        t1, t2, rot = pleT[:, 2, :], pleT[:, 3, :], [pleT[:, 4 + i, :] for i in range(4)]
        mxs = sqSum[:, 0:12 * GRP].rearrange("p (s a j) -> p s a j", s=2, a=6)

        qk_t = sem("qk_t")
        qk_r = sem("qk_r")
        qk_hi = sem("qk_hi")
        qk_lo = sem("qk_lo")
        qk_moved = [sem("qk_moved0"), sem("qk_moved1")]
        v_ok = sem("v_ok")
        sc_done = sem("sc_done")
        sc_read = sem("sc_read")
        mx_ok = sem("mx_ok")
        ex_ok = sem("ex_ok")
        pr_ok = sem("pr_ok")
        ptr2_done = sem("ptr2_done")
        pt_ok = sem("pt_ok")
        pt_ok2 = sem("pt_ok2")
        pv_done = sem("pv_done")
        o_hi = sem("o_hi")
        o_lo = sem("o_lo")
        pz_ok = sem("pz_ok")
        ATB = NT * KVH

        def load_rotary(sp, j):
            n = N_SW + 1 + j
            v = sw_w_in[0][:, 0:D].rearrange("(k p) (g j c) -> p j g k c", p=P, g=KVH, j=GRP)
            dst = wRaw[:, n % 2, :].rearrange("p (k g c) -> p k g c", k=KT, g=KVH)
            for g in range(KVH):
                sp.dma_start(dst[:, :, g], v[:, j, g]).then_inc(panel_in[n % 2], PANEL_INC // KVH)

        def load_mixer_out(sp, j):
            n = N_SWOUT + j
            dst = wRaw[:, n % 2, :].rearrange("p (a j n) -> p a j n", a=2, j=GRP)
            src = sw_w_out[0][:, 256 * j:256 * j + 256].rearrange("(a r j d) n -> a r d j n", a=2, r=2, j=GRP)
            for a in range(2):
                for r in range(2):
                    sp.dma_start(dst[r * HD:(r + 1) * HD, a], src[a, r]).then_inc(panel_in[n % 2], PANEL_INC // 4)

        def stack(sp, j, f):
            sp.wait_ge(qk_lo, 2 * j + f + 1)
            for i, part in enumerate((qkHi, qkLo)):
                for g in range(KVH):
                    src = part[j % 4][g * HALF:(g + 1) * HALF, f, :].bitcast(F32)
                    r = (g // 2) * HD + f * HALF
                    dst = qS[r:r + HALF, j - 1, g % 2, i, :] if j else kS[r:r + HALF, g % 2, i, :]
                    sp.dma_start(dst.bitcast(F32), src).then_inc(qk_moved[f], 16)

        def att_sp(sp):
            for j in range(GRP + 2):
                sp.wait_ge(panel_lo, N_SW + j - 1)
                if 1 <= j <= GRP:
                    load_rotary(sp, j - 1)
                else:
                    load_square(sp, N_SW + j, square_panel(sw_w_in[0], 0, D + (256 if j else 0)))
                if j in (2, 3):
                    stack(sp, 0, j - 2)
                elif j >= 4:
                    for f in range(2):
                        stack(sp, j - 3, f)
            for j in range(3, GRP + 1):
                for f in range(2):
                    stack(sp, j, f)
            for j in range(4):
                sp.wait_ge(panel_lo, N_SWOUT + j - 1)
                load_mixer_out(sp, j)

        def att_pe(pe, u, X):
            n0 = N_SW
            for j in range(GRP + 1):
                n = n0 + j
                pe.wait_ge(panel_lo, n + 1)
                for f in range(2):
                    if j:
                        pe.wait_ge(qk_t, 2 * j - 1 + f)
                    for k in range(KT):
                        if j == 0 and f == 0:
                            pe.wait_ge(next_lo, 8 * u - 8 + k + 1)
                        wv = [w[:, n % 2, panel_tile(0, k, f)] for w in (wH, wL)]
                        last = product(bank[f], wv[0], wv[1], X[0][:, k, :], X[1][:, k, :], k == 0, k == KT - 1)
                    last.then_inc(tile_done, 1)
                    if j == 0 and f == 0:
                        norm_pe_sum(pe, u - 1)
                if j == 0:
                    norm_pe_bc(pe, u - 1)
            n = n0 + GRP + 1
            pe.wait_ge(panel_lo, n + 1)
            for t in range(NT):
                for k in range(KT):
                    w = [w_[:, n % 2, k * 256:(k + 1) * 256] for w_ in (wH, wL)]
                    o = bank[2 + t // 2][:, (t % 2) * 256:(t % 2) * 256 + 256]
                    nc.tensor.matmul(o, X[0][:, k, rng(t)], w[0], start=(k == 0), stop=False)
                    nc.tensor.matmul(o, X[1][:, k, rng(t)], w[0], start=False, stop=False)
                    last = nc.tensor.matmul(o, X[0][:, k, rng(t)], w[1], start=False, stop=(k == KT - 1))
                if t % 2:
                    last.then_inc(tile_done, 1)
            for f in range(2):
                pe.wait_ge(qk_moved[f], 16 * 8 * (GRP + 1))
            pe.wait_ge(v_ok, NT)

            def scores(i):
                t, g = i // KVH, i % KVH
                if i >= 2:
                    pe.wait_ge(sc_read, i - 1)
                for j in range(GRP):
                    c0, k0 = (0, (t - 1) * P) if t else (P, 0)
                    o = psum[:, 2 * (i % 2) + j // 2, (j % 2) * 256 + c0:(j % 2) * 256 + 256]
                    rows = slice((g // 2) * HD, (g // 2 + 1) * HD)
                    q = [qS[rows, j, g % 2, part, rng(t)] for part in range(2)]
                    k = [kS[rows, g % 2, part, k0:(t + 1) * P] for part in range(2)]
                    last = product(o, q[0], q[1], k[0], k[1], True, True)
                last.then_inc(sc_done, 1)
            scores(0)
            def values(i):
                t, g = i // KVH, i % KVH
                pe.wait_ge(pt_ok2, i + 1)
                if t:
                    pe.wait_ge(pt_ok, i - KVH + 1)
                if g % 2 == 0 and i >= 4:
                    pe.wait_ge(o_lo, i // 2 - 1)
                o = bank[6 + i // 2 % 2][(g % 2) * HD:(g % 2 + 1) * HD]
                if t:
                    nc.tensor.matmul(o, vT[:, t - 1, g * HD:(g + 1) * HD], probsT[i % 2][:, 0, :], start=True, stop=False)
                nc.tensor.matmul(o, vT[:, t, g * HD:(g + 1) * HD], probsT[i % 2][:, 1, :], start=(t == 0), stop=True).then_inc(pv_done, 1)

            scores(1)
            for i in range(ATB):
                t, g = i // KVH, i % KVH
                if i + 2 < ATB:
                    scores(i + 2)
                pe.wait_ge(pr_ok, i + 1)
                if t:
                    if i > KVH:
                        pe.wait_ge(pt_ok, i - KVH)
                    for j in range(GRP):
                        last = nc.tensor.transpose(bank[4][:, rng(j)], probs[i % 2][:, j, rng(0)], ident[:])
                    last.then_inc(ptr2_done, 1)
                if i:
                    pe.wait_ge(pt_ok2, i)
                for j in range(GRP):
                    last = nc.tensor.transpose(bank[5][:, rng(j)], probs[i % 2][:, j, rng(1)], ident[:])
                last.then_inc(ptr2_done, 1)
                if i:
                    values(i - 1)
            values(ATB - 1)

        def att_act(act, u, O):
            n0 = N_SW
            for j in range(GRP + 1):
                prep_hi(act, n0 + j + 1, (n0 + j + 1) % 2)
                if j == 0:
                    norm_act(act, u - 1)
                for f in range(2):
                    act.wait_ge(qk_r, 2 * j + f + 1)
                    if j >= 4:
                        act.wait_ge(qk_moved[f], 16 * 8 * (j - 3))
                    nc.scalar.copy(qkHi[j % 4][:, f, :], rot[2 * f]).then_inc(qk_hi, 1)
            a_ = nc.scalar

            def exps(i):
                t, mx = i // KVH, mxs[:, i % 2]
                act.wait_ge(mx_ok, i + 1)
                if i >= 2:
                    act.wait_ge(ptr2_done, (i - 1) + max(0, i - 1 - KVH))
                elif i == 0:
                    act.wait_ge(pz_ok, 1)
                for j in range(GRP):
                    src = psum[:, 2 * (i % 2) + j // 2, (j % 2) * 256:(j % 2) * 256 + 256]
                    for a in range(2):
                        rows = slice(a * CH, (a + 1) * CH)
                        ks = slice(P if t == 0 and a == 0 else CH + a * CH, 3 * CH + a * CH)
                        last = a_.activation(probs[i % 2][rows, j, ks], src[rows, ks], ACT.Exp, bias=mx[rows, 3, j:j + 1],
                                             scale=SCALE, accum_out=mx[rows, 4, j:j + 1])
                last.then_inc(sc_read, 1)
                a_.activation(mx[:, 5, :], mx[:, 2, :], ACT.Exp).then_inc(ex_ok, 1)

            def out_hi(i):
                t, g = i // KVH, i % KVH
                if g % 2:
                    act.wait_ge(pv_done, i + 1)
                    a = g // 2
                    a_.copy(O[0][:, GRP * a:GRP * a + GRP, rng(t)], bank[6 + i // 2 % 2].rearrange("p (j q) -> p j q", j=GRP)).then_inc(o_hi, 1)
            exps(0)
            for i in range(ATB):
                t = i // KVH
                if i + 1 < ATB:
                    exps(i + 1)
                if t:
                    act.wait_ge(ptr2_done, i + 1 + i - KVH)
                    a_.copy(probsT[i % 2][:, 0, :], bank[4]).then_inc(pt_ok, 1)
                if i >= 2:
                    out_hi(i - 2)
                if i == KVH:
                    prep_hi(act, N_SWOUT, N_SWOUT % 2)
            for i in range(ATB - 2, ATB):
                out_hi(i)

        def att_dve(dve, u, O):
            v = nc.vector
            n0 = N_SW
            tt, st = v.tensor_tensor, v.scalar_tensor_tensor
            for j in range(GRP + 1):
                prep_lo(dve, n0 + j + 1, (n0 + j + 1) % 2)
                if j == 0:
                    norm_dve(dve, u - 1)
                dve.drain()
                if j == 0:
                    dve.wait_ge(n_ok, norms_bc(u - 1))
                    dve.wait_ge(rope_ok, 1)
                r0 = R_BQ + 2 * (j - 1) if j else R_BK
                for f, tf in enumerate((t1, t2)):
                    dve.wait_ge(tile_done, tiles_before(n0 + j) + f + 1)
                    tt(tf, bank[f], rBC[:], ALU.mult).then_inc(qk_t, 1)
                dve.drain()
                b1, b2 = colsB[:, r0:r0 + 1], colsB[:, r0 + 1:r0 + 2]
                if j:
                    dve.wait_ge(qk_lo, 2 * j)
                st(out=rot[0], in0=t1, scalar=b1, in1=ropeC[:], op0=ALU.add, op1=ALU.mult)
                st(out=rot[1], in0=t2, scalar=b2, in1=ropeS[:], op0=ALU.add, op1=ALU.mult)
                st(out=rot[2], in0=t2, scalar=b2, in1=ropeC[:], op0=ALU.add, op1=ALU.mult)
                st(out=rot[3], in0=t1, scalar=b1, in1=ropeS[:], op0=ALU.add, op1=ALU.mult)
                dve.drain()
                tt(rot[0], rot[0], rot[1], ALU.subtract).then_inc(qk_r, 1)
                tt(rot[2], rot[2], rot[3], ALU.add).then_inc(qk_r, 1)
                for f in range(2):
                    dve.wait_ge(qk_hi, 2 * j + f + 1)
                    if j >= 4:
                        dve.wait_ge(qk_moved[f], 16 * 8 * (j - 3))
                    tt(qkLo[j % 4][:, f, :], rot[2 * f], qkHi[j % 4][:, f, :].bitcast(F32), ALU.subtract).then_inc(qk_lo, 1)
            for t in range(NT):
                dve.wait_ge(tile_done, tiles_before(n0 + GRP + 1) + t // 2 + 1)
                st(out=vT[:, t, :], in0=bank[2 + t // 2][:, (t % 2) * 256:(t % 2) * 256 + 256], scalar=rCol[:, t:t + 1],
                   in1=vBias[:], op0=ALU.mult, op1=ALU.add).then_inc(v_ok, 1)

            def maxima(i):
                t, g, mx = i // KVH, i % KVH, mxs[:, i % 2]
                dve.wait_ge(sc_done, i + 1)
                src = psum[:, 2 * (i % 2):2 * (i % 2) + 2, :].rearrange("p b (j k) -> p (b j) k", j=2)
                for a in range(2):
                    rows = slice(a * CH, (a + 1) * CH)
                    ks = slice(P if t == 0 and a == 0 else CH + a * CH, 3 * CH + a * CH)
                    v.tensor_reduce(mx[rows, 0, :], src[rows, :, ks], AX, ALU.max)
                dve.drain()
                st(out=mx[:, 1, :], in0=mx[:, 0, :], scalar=SCALE, in1=sinks[:, g, :], op0=ALU.mult, op1=ALU.max)
                dve.drain()
                tt(mx[:, 2, :], sinks[:, g, :], mx[:, 1, :], ALU.subtract)
                v.tensor_scalar(mx[:, 3, :], mx[:, 1, :], -1.0, None, ALU.mult).then_inc(mx_ok, 1)

            def out_lo(i):
                t, g = i // KVH, i % KVH
                if g % 2:
                    a = g // 2
                    dve.wait_ge(o_hi, i // 2 + 1)
                    tt(O[1][:, GRP * a:GRP * a + GRP, rng(t)], bank[6 + i // 2 % 2].rearrange("p (j q) -> p j q", j=GRP),
                       O[0][:, GRP * a:GRP * a + GRP, rng(t)].bitcast(F32), ALU.subtract).then_inc(o_lo, 1)
            maxima(0)
            maxima(1)
            for i in range(ATB):
                mx = mxs[:, i % 2]
                dve.wait_ge(ex_ok, i + 1)
                tt(mx[:, 0, :], mx[:, 4, :], mx[:, 5, :], ALU.add)
                dve.drain()
                v.reciprocal(mx[:, 1, :], mx[:, 0, :])
                dve.drain()
                tt(probs[i % 2], probs[i % 2], mx[:, 1, :].unsqueeze(2).to_broadcast([P, GRP, 256]), ALU.mult).then_inc(pr_ok, 1)
                if i + 2 < ATB:
                    dve.drain()
                    maxima(i + 2)
                dve.wait_ge(ptr2_done, i + 1 + max(0, i + 1 - KVH))
                v.tensor_copy(probsT[i % 2][:, 1, :], bank[5]).then_inc(pt_ok2, 1)
                if i >= 2:
                    out_lo(i - 2)
                if i == KVH:
                    prep_lo(dve, N_SWOUT, N_SWOUT % 2)
            for i in range(ATB - 2, ATB):
                out_lo(i)

        def att_pool(pool):
            pool.wait_ge(next_lo, 24)
            for i in range(2):
                nc.gpsimd.memset(probs[i], 0.0)
            pool.drain()
            pool.sem_inc(pz_ok, 1)

        out_v = out[0]
        ftr_done = sem("ftr_done")
        fout_ok = sem("fout_ok")

        def final_pe(pe):
            norm_pe_sum(pe, 5)
            for t in range(NT):
                for hf in range(2):
                    i = 2 * t + hf
                    if i >= 4:
                        pe.wait_ge(fout_ok, i - 3)
                    for k in range(4):
                        last = nc.tensor.transpose(bank[i % 4][:, rng(k)], acc[:, 4 * hf + k, rng(t)], ident[:])
                    last.then_inc(ftr_done, 1)

        def final_act(act):
            act.wait_ge(n_r, 6)
            for i in range(2 * NT):
                act.wait_ge(ftr_done, i + 1)
                nc.scalar.activation(pleT[:, i, :], bank[i % 4], ACT.Copy, scale=rCol[:, i // 2:i // 2 + 1]).then_inc(fout_ok, 1)

        def final_sp(sp):
            for t in range(NT):
                sp.wait_ge(fout_ok, 2 * t + 2)
                sp.dma_start(out_v[t * P:(t + 1) * P, :].rearrange("p (a b) -> p a b", a=2), pleT[:, 2 * t:2 * t + 2, :]).then_inc(out_done, 16)
            sp.wait_ge(out_done, 16 * NT)

        out_done = sem("out_done")
        block = ctx.enter_context(nc.Block())

        @block.sync
        def _(sp):
            consts_sp(sp)
            dn_sp(sp)
            for m in range(4):
                sp.wait_ge(panel_lo, N_DNOUT + m - 1)
                load_square(sp, N_DNOUT + m, square_panel(dn_w_out[0], 0, 256 * m))
            sp.wait_ge(res_ok, 1)
            ple_load(sp, 0)
            mlp_sp(sp, 0, N_MLP0)
            ple_sp(sp, 0, N_PLE0)
            att_sp(sp)
            ple_load(sp, 1)
            mlp_sp(sp, 1, N_MLP1)
            ple_sp(sp, 1, N_PLE1)
            final_sp(sp)

        @block.gpsimd
        def _(pool):
            consts_pool(pool)
            dn_pool(pool)
            norm_pool(pool, 0)
            mlp_pool(pool, 0, 1)
            norm_pool(pool, 1)
            norm_pool(pool, 2)
            att_pool(pool)
            norm_pool(pool, 3)
            mlp_pool(pool, 1, 4)
            norm_pool(pool, 4)
            norm_pool(pool, 5)

        @block.scalar
        def _(act):
            rope_act(act)
            first_norm_act(act)
            rope_act2(act)
            gates_act(act)
            scale_act(act)
            first_tr_act(act)
            prep_hi(act, 0, 0)
            gates_act2(act)
            dn_act(act)
            out_act(act, N_DNOUT, 0)
            mlp_act(act, 0, N_MLP0, 1, X_A, X_B)
            ple_act(act, 0, N_PLE0, 2)
            att_act(act, 3, X_A)
            out_act(act, N_SWOUT, 3)
            mlp_act(act, 1, N_MLP1, 4, X_B, X_A)
            ple_act(act, 1, N_PLE1, 5)
            final_act(act)

        @block.vector
        def _(dve):
            rope_dve(dve)
            raw_dve(dve, 0, 2)
            first_norm_dve(dve)
            raw_dve(dve, 2, KT)
            gates_dve(dve)
            first_tr_dve(dve)
            prep_lo(dve, 0, 0)
            gates_dve2(dve)
            prep_lo(dve, 1, 1)
            dn_dve(dve)
            out_dve(dve, N_DNOUT, 0)
            mlp_dve(dve, 0, N_MLP0, 1, X_A, X_B)
            ple_dve(dve, 0, N_PLE0, 2)
            att_dve(dve, 3, X_A)
            out_dve(dve, N_SWOUT, 3, colsB[:, R_BOUT:R_BOUT + KT])
            mlp_dve(dve, 1, N_MLP1, 4, X_B, X_A)
            ple_dve(dve, 1, N_PLE1, 5)
            norm_dve(dve, 5)

        @block.tensor
        def _(pe):
            rope_pe(pe)
            first_tr_pe(pe)
            gates_pe(pe)
            dn_pe(pe)
            out_pe(pe, N_DNOUT, 0, X_B, lambda e, k: e.wait_ge(yl_ok, k + 1))
            mlp_pe(pe, 0, N_MLP0, 1, X_A, X_B)
            ple_pe(pe, 0, N_PLE0, 2, X_A)
            att_pe(pe, 3, X_B)
            out_pe(pe, N_SWOUT, 3, X_A, lambda e, k: e.wait_ge(o_lo, 2 * NT))
            mlp_pe(pe, 1, N_MLP1, 4, X_B, X_A)
            ple_pe(pe, 1, N_PLE1, 5, X_B)
            final_pe(pe)


_INS = ['x', 'p', 'positions', 'norm_mix', 'norm_mlp', 'norm_ple', 'norm_final', 'dn_w_in', 'dn_conv_w', 'dn_a_log',
        'dn_dt_bias', 'dn_norm_w', 'dn_w_out', 'sw_w_in', 'sw_b_in', 'sw_sinks', 'sw_w_out', 'sw_b_out', 'mlp_w_up',
        'mlp_w_down', 'ple_w_proj', 'ple_w_gate']


def kernel(**inputs):
    import numpy as _np
    import concourse.bacc as _bacc
    from concourse import mybir as _mybir
    from concourse.bass_utils import run_bass_kernel_spmd as _run

    nc = _bacc.Bacc("TRN2", target_bir_lowering=False, num_devices=1, dynamic_dma_scratch_size=1024)
    arrays, args = {}, []
    for name in _INS:
        a = _np.ascontiguousarray(inputs[name])
        arrays[f"in_{name}"] = a
        args.append(nc.dram_tensor(f"in_{name}", a.shape, _mybir.dt.from_np(a.dtype), kind="ExternalInput").ap())
    args.append(nc.dram_tensor("out_0", (1, S, D), F32, kind="ExternalOutput").ap())
    hybrid_trunk(nc, *args)
    r = _run(nc, [arrays], core_ids=[0])
    return r.results[0]["out_0"]
```
